# Optimizing a Trainium2 kernel written in Bass

```python
import math
import jax, jax.numpy as jnp
from jax import lax
import numpy as np

D_MODEL = 1024
BATCH = 1
SEQ = 512
DEPTH = 1

CHUNK = 64
PLE_DIM = 256
SG_BLOCK = 128
SG_GROUPS = 4
SG_WIDTH = 512
SG_GROUP_CH = SG_WIDTH // SG_GROUPS
SB_HEADS = 8
SB_HEAD_DIM = 64
SB_WIDTH = SB_HEADS * SB_HEAD_DIM
SB_QBLOCK = 128
IN_SIZES = (SG_WIDTH, SG_WIDTH, SB_WIDTH, SB_WIDTH, SB_WIDTH, D_MODEL, D_MODEL)
IN_PROJ_WIDTH = 2 * SG_WIDTH + 3 * SB_WIDTH + 2 * D_MODEL
IN_SPLITS = (SG_WIDTH, 2 * SG_WIDTH, 2 * SG_WIDTH + SB_WIDTH, 2 * SG_WIDTH + 2 * SB_WIDTH,
             2 * SG_WIDTH + 3 * SB_WIDTH, 2 * SG_WIDTH + 3 * SB_WIDTH + D_MODEL)
N_EXPERTS = 64
N_GROUPS = 8
TOPK_GROUPS = 4
TOP_K = 8
EXPERT_FF = 256
SHARED_FF = 256
ROUTED_SCALE = 2.5
MOE_BLOCK = 128
LN_EPS = 1e-5
DEEPNORM_ALPHA = (2.0 * DEPTH) ** 0.25
DEEPNORM_BETA = (8.0 * DEPTH) ** -0.25

kernel_name = "hybrid_sgmlp_stickbreak_moe_deepnorm"

def layer_norm(x, g, b):
    xf = x.astype(jnp.float32)
    mu = jnp.mean(xf, axis=-1, keepdims=True)
    xc = xf - mu
    var = jnp.mean(jnp.square(xc), axis=-1, keepdims=True)
    y = xc * lax.rsqrt(var + LN_EPS)
    return (y * g.astype(jnp.float32) + b.astype(jnp.float32)).astype(x.dtype)

def spatial_gating(u, v, ln_g, ln_b, w_s, b_s):
    bsz, seq, _ = u.shape
    nb = seq // SG_BLOCK
    v = layer_norm(v, ln_g, ln_b).reshape(bsz, nb, SG_BLOCK, SG_GROUPS, SG_GROUP_CH)
    pos = jnp.arange(SG_BLOCK)
    mask = (pos[None, :] // CHUNK) <= (pos[:, None] // CHUNK)
    w = jnp.where(mask[None], w_s, jnp.zeros_like(w_s))
    s = jnp.einsum('gij,bnjgc->bnigc', w, v) + b_s.T[None, None, :, :, None]
    return u * s.reshape(bsz, seq, SG_WIDTH)

def stick_breaking_attention(q, k, v):
    bsz, seq, _, _ = q.shape
    q = q.transpose(0, 2, 1, 3)
    k = k.transpose(0, 2, 1, 3)
    v = v.transpose(0, 2, 1, 3)
    scale = 1.0 / math.sqrt(SB_HEAD_DIM)
    outs = []
    for blk in range(seq // SB_QBLOCK):
        lo = blk * SB_QBLOCK
        hi = lo + SB_QBLOCK
        z = jnp.einsum('bhqd,bhkd->bhqk', q[:, :, lo:hi], k[:, :, :hi]).astype(jnp.float32) * scale
        t_idx = lo + jnp.arange(SB_QBLOCK)[:, None]
        s_idx = jnp.arange(hi)[None, :]
        causal = s_idx < t_idx
        log_1m = jnp.where(causal, jax.nn.log_sigmoid(-z), 0.0)
        tail = lax.cumsum(log_1m, axis=3, reverse=True) - log_1m
        a = jnp.where(causal, jnp.exp(jax.nn.log_sigmoid(z) + tail), 0.0)
        outs.append(jnp.einsum('bhqk,bhkd->bhqd', a.astype(v.dtype), v[:, :, :hi]))
    o = jnp.concatenate(outs, axis=2)
    return o.transpose(0, 2, 1, 3).reshape(bsz, seq, SB_WIDTH)

def moe_ffn(x, router_w, router_bias, w_gate, w_up, w_down, sh_gate, sh_up, sh_down):
    bsz, seq, dm = x.shape
    n_tok = bsz * seq
    xf = x.reshape(n_tok, dm)
    scores = jax.nn.sigmoid((xf @ router_w).astype(jnp.float32))
    sel = scores + router_bias.astype(jnp.float32)
    grp = jnp.sum(lax.top_k(sel.reshape(n_tok, N_GROUPS, N_EXPERTS // N_GROUPS), 2)[0], axis=-1)
    _, gidx = lax.top_k(grp, TOPK_GROUPS)
    gmask = jnp.any(gidx[:, :, None] == jnp.arange(N_GROUPS)[None, None, :], axis=1)
    emask = jnp.repeat(gmask, N_EXPERTS // N_GROUPS, axis=1)
    _, eidx = lax.top_k(jnp.where(emask, sel, -jnp.inf), TOP_K)
    wsel = jnp.take_along_axis(scores, eidx, axis=1)
    wsel = wsel / jnp.sum(wsel, axis=-1, keepdims=True) * ROUTED_SCALE
    n_assign = n_tok * TOP_K
    flat_e = eidx.reshape(n_assign).astype(jnp.int32)
    flat_tok = jnp.repeat(jnp.arange(n_tok, dtype=jnp.int32), TOP_K)
    flat_w = wsel.reshape(n_assign)
    order = jnp.argsort(flat_e)
    sorted_e = flat_e[order]
    counts = jnp.bincount(flat_e, length=N_EXPERTS).astype(jnp.int32)
    starts = jnp.cumsum(counts) - counts
    padded = (counts + MOE_BLOCK - 1) // MOE_BLOCK * MOE_BLOCK
    pad_ends = jnp.cumsum(padded)
    pad_starts = pad_ends - padded
    dest = pad_starts[sorted_e] + jnp.arange(n_assign, dtype=jnp.int32) - starts[sorted_e]
    n_blocks = n_assign // MOE_BLOCK + N_EXPERTS
    n_rows = n_blocks * MOE_BLOCK
    row_tok = jnp.full((n_rows,), n_tok, jnp.int32).at[dest].set(flat_tok[order])
    row_w = jnp.zeros((n_rows,), jnp.float32).at[dest].set(flat_w[order])
    block_e = jnp.minimum(jnp.searchsorted(pad_ends, jnp.arange(n_blocks, dtype=jnp.int32) * MOE_BLOCK,
                                           side='right'), N_EXPERTS - 1)
    x_pad = jnp.concatenate([xf, jnp.zeros((1, dm), xf.dtype)], axis=0)

    def expert_block(args):
        tok, e = args
        xb = x_pad[tok]
        hb = jax.nn.silu(xb @ w_gate[e]) * (xb @ w_up[e])
        return hb @ w_down[e]

    yb = lax.map(expert_block, (row_tok.reshape(n_blocks, MOE_BLOCK), block_e))
    yb = yb.reshape(n_rows, dm) * row_w[:, None].astype(yb.dtype)
    routed = jax.ops.segment_sum(yb, row_tok, num_segments=n_tok + 1)[:n_tok]
    shared = (jax.nn.silu(xf @ sh_gate) * (xf @ sh_up)) @ sh_down
    return (routed + shared).reshape(bsz, seq, dm)

def setup_inputs(seed: int = 0) -> dict:
    key = jax.random.key(seed)
    ks = jax.random.split(key, 26)
    L = DEPTH
    D = D_MODEL

    def nrm(k, shape, scale):
        return jax.random.normal(k, shape, jnp.float32) * scale

    return {
        "x": nrm(ks[0], (BATCH, SEQ, D), 1.0),
        "p": nrm(ks[1], (DEPTH, BATCH, SEQ, PLE_DIM), 1.0),
        "ln_in_g": 1.0 + nrm(ks[2], (D,), 0.02),
        "ln_in_b": nrm(ks[3], (D,), 0.02),
        "w_in": nrm(ks[4], (L, D, IN_PROJ_WIDTH), D ** -0.5),
        "sg_ln_g": 1.0 + nrm(ks[5], (L, SG_WIDTH), 0.02),
        "sg_ln_b": nrm(ks[6], (L, SG_WIDTH), 0.02),
        "sg_w_s": nrm(ks[7], (L, SG_GROUPS, SG_BLOCK, SG_BLOCK), SG_BLOCK ** -0.5),
        "sg_b_s": 1.0 + nrm(ks[8], (L, SG_GROUPS, SG_BLOCK), 0.1),
        "w_branch_a": nrm(ks[9], (L, SG_WIDTH, D), SG_WIDTH ** -0.5),
        "w_branch_b": nrm(ks[10], (L, SB_WIDTH, D), SB_WIDTH ** -0.5),
        "w_out": nrm(ks[11], (L, D, D), D ** -0.5 * DEEPNORM_BETA),
        "ln1_g": 1.0 + nrm(ks[12], (L, D), 0.02),
        "ln1_b": nrm(ks[13], (L, D), 0.02),
        "router_w": nrm(ks[14], (L, D, N_EXPERTS), D ** -0.5),
        "router_bias": nrm(ks[15], (L, N_EXPERTS), 0.01),
        "moe_w_gate": nrm(ks[16], (L, N_EXPERTS, D, EXPERT_FF), D ** -0.5),
        "moe_w_up": nrm(ks[17], (L, N_EXPERTS, D, EXPERT_FF), D ** -0.5),
        "moe_w_down": nrm(ks[18], (L, N_EXPERTS, EXPERT_FF, D), EXPERT_FF ** -0.5 * DEEPNORM_BETA),
        "sh_w_gate": nrm(ks[19], (L, D, SHARED_FF), D ** -0.5),
        "sh_w_up": nrm(ks[20], (L, D, SHARED_FF), D ** -0.5),
        "sh_w_down": nrm(ks[21], (L, SHARED_FF, D), SHARED_FF ** -0.5 * DEEPNORM_BETA),
        "ple_w_proj": nrm(ks[22], (L, PLE_DIM, D), PLE_DIM ** -0.5 * DEEPNORM_BETA),
        "ple_w_gate": nrm(ks[23], (L, D, D), D ** -0.5),
        "ln2_g": 1.0 + nrm(ks[24], (L, D), 0.02),
        "ln2_b": nrm(ks[25], (L, D), 0.02),
    }

def reference(x, p, ln_in_g, ln_in_b, w_in, sg_ln_g, sg_ln_b, sg_w_s, sg_b_s, w_branch_a, w_branch_b,
              w_out, ln1_g, ln1_b, router_w, router_bias, moe_w_gate, moe_w_up, moe_w_down,
              sh_w_gate, sh_w_up, sh_w_down, ple_w_proj, ple_w_gate, ln2_g, ln2_b):
    bsz, seq, _ = x.shape
    h = layer_norm(x, ln_in_g, ln_in_b)
    for i in range(DEPTH):
        proj = h @ w_in[i]
        u, v_sg, q, k, v_sb, g_a, g_b = jnp.split(proj, IN_SPLITS, axis=-1)
        y_a = spatial_gating(jax.nn.gelu(u), jax.nn.gelu(v_sg), sg_ln_g[i], sg_ln_b[i], sg_w_s[i], sg_b_s[i])
        y_b = stick_breaking_attention(q.reshape(bsz, seq, SB_HEADS, SB_HEAD_DIM),
                                       k.reshape(bsz, seq, SB_HEADS, SB_HEAD_DIM),
                                       v_sb.reshape(bsz, seq, SB_HEADS, SB_HEAD_DIM))
        merged = jax.nn.sigmoid(g_a) * (y_a @ w_branch_a[i]) + jax.nn.sigmoid(g_b) * (y_b @ w_branch_b[i])
        h = layer_norm(DEEPNORM_ALPHA * h + merged @ w_out[i], ln1_g[i], ln1_b[i])
        r = DEEPNORM_ALPHA * h + moe_ffn(h, router_w[i], router_bias[i], moe_w_gate[i], moe_w_up[i],
                                         moe_w_down[i], sh_w_gate[i], sh_w_up[i], sh_w_down[i])
        r = r + jax.nn.sigmoid(r @ ple_w_gate[i]) * (p[i] @ ple_w_proj[i])
        h = layer_norm(r, ln2_g[i], ln2_b[i])
    return h


_drawn_inputs = setup_inputs


def setup_inputs(seed=0):
    import zlib

    import numpy as np

    out = dict(_drawn_inputs(seed))
    spreads = {}
    factors = {'sg_ln_g': 3.49, 'sg_ln_b': 3.434, 'ln2_g': 2.854, 'ln2_b': 2.807}
    for name, (base, spread) in spreads.items():
        noise = np.random.default_rng([zlib.crc32(name.encode()), seed]).standard_normal(out[name].shape)
        drawn = base * np.exp(spread * noise) if base else spread * noise
        out[name] = __import__('jax').numpy.asarray(drawn.astype(out[name].dtype))
    for name, factor in factors.items():
        out[name] = (out[name] * factor).astype(out[name].dtype)
    return out
```

```python
from contextlib import ExitStack

import concourse.bass as bass
from concourse import mybir

P = 128
D = 1024
SEQ = 512
NT = SEQ // P
KD = D // P
SG = 512
SGG = 4
HEADS = 8
HD = 64
NE = 64
NGRP = 8
FF = 256
PLE = 256
LN_EPS = 1e-5
ALPHA = 2.0 ** 0.25
ROUTED_SCALE = 2.5
SLOTS = 96
FAR = 4096.0
HC = 2048
NSPLIT = 4
NRAW = 2

F32 = mybir.dt.float32
F32R = mybir.dt.float32r
BF16 = mybir.dt.bfloat16
U32 = mybir.dt.uint32
I32 = mybir.dt.int32
ALU = mybir.AluOpType
ACT = mybir.ActivationFunctionType
AX = mybir.AxisListType.X
KB = 1024


class Memory:

    def __init__(self, nc, base, cap):
        def at(name, shape, dtype, kib):
            return nc.alloc_sbuf_tensor_at(name, shape, dtype, offset=base + int(kib * KB))

        self.raw = at("raw", [P, NRAW, HC], F32, 0)
        self.w_hi = at("w_hi", [P, NSPLIT, HC], F32R, 16)
        self.w_lo = at("w_lo", [P, NSPLIT, HC], F32R, 48)
        self.act_hi = at("act_hi", [P, KD, SEQ], F32R, 80)
        self.act_lo = at("act_lo", [P, KD, SEQ], F32R, 96)
        self.qT = at("qT", [P, 4, SEQ], F32, 112)
        self.kT = at("kT", [P, 4, SEQ], F32, 120)
        self.ybT_hi = at("ybT_hi", [P, 4, SEQ], F32R, 112)
        self.ybT_lo = at("ybT_lo", [P, 4, SEQ], F32R, 120)
        self.vsb = at("vsb", [P, NT, 512], F32, 128)
        self.merged = at("merged", [P, NT, D], F32, 136)
        self.yaT_hi = at("yaT_hi", [P, 4, SEQ], F32R, 152)
        self.yaT_lo = at("yaT_lo", [P, 4, SEQ], F32R, 160)
        self.x = at("x_rows", [P, NT, D], F32, 152)
        self.yb = at("yb", [P, NT, 512], F32, 168)
        self.ln_g = at("ln_g", [P, D], F32, 168)
        self.ln_b = at("ln_b", [P, D], F32, 172)
        self.sig_neg = at("sig_neg", [P, 2, 512], F32, 176)
        self.sig_pos = at("sig_pos", [P, 2, 512], F32, 180)
        self.stick = at("stick", [P, 2, 520], F32, 184)
        self.aT = at("aT", [P, 2, 512], F32, 189)
        self.gate = at("gate", [P, 2, 512], F32, 193)
        self.sg_wT = at("sg_wT", [P, SGG, P], F32, 197)
        self.sg_b = at("sg_b", [P, SGG], F32, 199)
        self.sg_w = at("sg_w", [P, SGG, P], F32, 189)
        self.sg_g = at("sg_g", [P, SG], F32, 176)
        self.sg_bb = at("sg_bb", [P, SG], F32, 178)
        self.ident = at("ident", [P, P], F32, 201)
        self.ident_bf = at("ident_bf", [P, P], BF16, 201.5)
        self.future_bf = at("future_bf", [P, P], BF16, 201.75)
        self.earlier_bf = at("earlier_bf", [P, P], BF16, 202)
        self.ones_bf = at("ones_bf", [P, P], BF16, 202.25)
        self.lower_grp = at("lower_grp", [P, NGRP, NGRP], F32, 202.5)
        self.slots = at("slots", [P, SEQ + P], F32, 202.75)
        self.stats = at("stats", [P, NT, 2, 6], F32, 205.25)
        self.mv = at("mv", [P, NT, 2], F32, 205.5)
        self.rstd = at("rstd", [P, NT, 1], F32, 205.625)
        self.nmr = at("nmr", [P, NT, 1], F32, 205.75)
        self.eps = at("eps", [P, 1], F32, 206.125)
        self.peak = at("peak", [P, 1], F32, 205.875)
        self.peak_i = at("peak_i", [P, 1], I32, 206)
        self.sh_down = at("sh_down", [P, HC], F32, 136)
        self.sh_h = at("sh_h", [P, NT, FF], F32, 168)
        self.sh_hT = at("sh_hT", [P, 2, SEQ], F32, 172)
        self.zero_rows = at("zero_rows", [P, D], F32, 128)
        self.acc = at("acc_rows", [P, 2, D], F32, 144)
        self.router = at("router", [P, KD, NE], F32, 184)
        self.r_hi = at("r_hi", [P, KD, NE], F32R, 186)
        self.r_lo = at("r_lo", [P, KD, NE], F32R, 188)
        self.r_bias = at("r_bias", [P, NE], F32, 190)
        self.score = at("score", [P, NT, NE], F32, 190.25)
        self.sel = at("sel", [P, NT, NE], F32, 191.25)
        self.top = at("top", [P, NT, NGRP, 8], F32, 192.25)
        self.grp = at("grp", [P, NT, NGRP], F32, 193.25)
        self.beats = at("beats", [P, NT, NGRP, NGRP], F32, 193.5)
        self.ties = at("ties", [P, NT, NGRP, NGRP], F32, 194.5)
        self.rank = at("rank", [P, NT, NGRP], F32, 195.5)
        self.top8 = at("top8", [P, NT, 8], F32, 195.75)
        self.rest = at("rest", [P, NT, NE], F32, 196)
        self.pick_bf = at("pick_bf", [P, NT, NE], BF16, 197)
        self.den = at("den", [P, NT], F32, 197.5)
        self.slot_of = at("slot_of", [P, NT, NE], F32, 176)
        self.tags = at("tags", [P, NT, NE, 6], BF16, 177)
        self.found = at("found", [P, NE, 2], F32, 180)
        self.get_idx = [at(f"get_idx{i}", [P, 1], U32, 180.5 + i * 0.0625) for i in range(4)]
        self.put_idx = [at(f"put_idx{i}", [P, 1], U32, 180.75 + i * 0.0625) for i in range(2)]
        self.gu_raw = at("gu_raw", [P, 4, HC], F32, 112)
        self.dn_raw = at("dn_raw", [P, 2, HC], F32, 184)
        self.dn_hi = at("dn_hi", [P, 2, HC], F32R, 0)
        self.dn_lo = at("dn_lo", [P, 2, HC], F32R, 160)
        self.xg = [at(f"xg{i}", [P, D], F32, 144 + 4 * i) for i in range(4)]
        self.xgT_hi = at("xgT_hi", [P, 2, KD * cap], F32R, 80)
        self.xgT_lo = at("xgT_lo", [P, 2, KD * cap], F32R, 88)
        self.silu = at("silu", [P, 2, FF], F32, 96)
        self.h = at("h_ff", [P, 2, FF], F32, 98)
        self.hT_hi = at("hT_hi", [P, 2, 2 * cap], F32R, 100)
        self.hT_lo = at("hT_lo", [P, 2, 2 * cap], F32R, 181)
        self.y = [at(f"y{i}", [P, D], F32, 102 + 4 * i) for i in range(2)]
        self.onehot = at("onehot", [P, 2, NT, cap], BF16, 110)
        self.p = at("p_rows", [P, NT, PLE], F32, 112)
        self.pT = at("pT", [P, 2, SEQ], F32, 116)
        self.p_w = at("p_w", [P, HC], F32, 120)
        self.x_odd = at("x_odd", [P, NT, D], F32, 176)
        self.pp = at("pp", [P, NT, D], F32, 128)


def make_constants(nc, m):
    with nc.semaphore("base_set") as base_set, nc.Block() as block:

        @block.gpsimd
        def _(pool):
            nc.gpsimd.memset(m.ident[:], 0.0).then_inc(base_set, 1)
            nc.gpsimd.memset(m.ident_bf[:], 0.0).then_inc(base_set, 1)
            nc.gpsimd.memset(m.future_bf[:], 0.0).then_inc(base_set, 1)
            nc.gpsimd.memset(m.earlier_bf[:], 1.0).then_inc(base_set, 1)
            nc.gpsimd.memset(m.ones_bf[:], 1.0).then_inc(base_set, 1)
            nc.gpsimd.memset(m.lower_grp[:], 1.0).then_inc(base_set, 1)
            nc.gpsimd.memset(m.eps[:], LN_EPS)
            pool.wait_ge(base_set, 6)
            for eye in (m.ident, m.ident_bf):
                nc.gpsimd.affine_select(out=eye[:], in_=eye[:], compare_op=ALU.not_equal, fill=1.0, base=0,
                                        pattern=[[-1, P]], channel_multiplier=1)
            nc.gpsimd.affine_select(out=m.future_bf[:], in_=m.future_bf[:], compare_op=ALU.is_gt, fill=-1e30,
                                    base=0, pattern=[[-1, P]], channel_multiplier=1)
            nc.gpsimd.affine_select(out=m.earlier_bf[:], in_=m.earlier_bf[:], compare_op=ALU.is_gt, fill=0.0,
                                    base=0, pattern=[[1, P]], channel_multiplier=-1)
            nc.gpsimd.affine_select(out=m.lower_grp[:], in_=m.lower_grp[:], compare_op=ALU.is_gt, fill=0.0,
                                    base=0, pattern=[[1, NGRP], [-1, NGRP]], channel_multiplier=0)
            nc.gpsimd.iota(m.slots[:], pattern=[[1, SEQ + P]], base=0, channel_multiplier=0,
                           allow_small_or_imprecise_dtypes=True)


def deviation(nc, m, t):
    return nc.scalar.activation(m.rstd[:, t], m.mv[:, t, 1:2], ACT.Sqrt, bias=m.eps[:])


def scale_and_shift(nc, m, chained, t):
    chained(nc.vector.reciprocal(m.rstd[:, t], m.rstd[:, t]))
    return nc.vector.scalar_tensor_tensor(out=m.nmr[:, t], in0=m.mv[:, t, 0:1], scalar=-1.0, in1=m.rstd[:, t],
                                          op0=ALU.mult, op1=ALU.mult)


class NormSemaphores:

    def __init__(self, nc, ctx):
        def sem(name):
            return ctx.enter_context(nc.semaphore(f"norm_{name}"))

        self.rows_in = [sem(f"rows_in{t}") for t in range(NT)]
        self.affine_in, self.rows_out = sem("affine_in"), sem("rows_out")
        self.moments, self.rooted, self.stats_done = sem("moments"), sem("rooted"), sem("stats_done")
        self.scaled, self.normed, self.turned = sem("scaled"), sem("normed"), sem("turned")
        self.hi_done, self.lo_done, self.chain = sem("hi_done"), sem("lo_done"), sem("chain")
        self.norms = 0
        self.links = 0


def norm_block(nc, m, ps, s, gain, bias, source=None, store=None, output=False):
    before = s.norms * NT
    s.norms += 1
    with ExitStack() as ctx:
        block = ctx.enter_context(nc.Block())

        @block.sync
        def _(sp):
            if source is not None:
                for t in range(NT):
                    sp.dma_start(m.x[:, t], source[t * P:(t + 1) * P, :]).then_inc(s.rows_in[t], 16)
            sp.dma_start(m.ln_g[:], gain.partition_broadcast(P)).then_inc(s.affine_in, 16)
            sp.dma_start(m.ln_b[:], bias.partition_broadcast(P)).then_inc(s.affine_in, 16)
            for t in range(NT):
                sp.wait_ge(s.normed, before + t + 1)
                sp.dma_start(store[t * P:(t + 1) * P, :], m.x[:, t]).then_inc(s.rows_out, 16)
            sp.wait_ge(s.rows_out, 16 * (before + NT))

        @block.vector
        def _(dve):
            def chained(ins):
                s.links += 1
                ins.then_inc(s.chain, 1)
                dve.wait_ge(s.chain, s.links)

            def statistics(t):
                if source is not None:
                    dve.wait_ge(s.rows_in[t], 16)
                for half in range(2):
                    last = nc.vector.bn_stats(m.stats[:, t, half], m.x[:, t, half * 512:(half + 1) * 512])
                    if half:
                        chained(last)
                    else:
                        s.links += 1
                        last.then_inc(s.chain, 1)
                nc.vector.bn_aggr(m.mv[:, t], m.stats[:, t]).then_inc(s.moments, 1)

            def affine(t):
                if t == 0:
                    dve.wait_ge(s.affine_in, 32 * (before // NT + 1))
                dve.wait_ge(s.scaled, before + t + 1)
                chained(nc.vector.tensor_tensor(m.x[:, t], m.x[:, t], m.ln_g[:], ALU.mult))
                nc.vector.tensor_tensor(m.x[:, t], m.x[:, t], m.ln_b[:], ALU.add).then_inc(s.normed, 1)

            def low_part(t):
                dve.wait_ge(s.hi_done, before + t + 1)
                b = 2 * (t % 2)
                nc.vector.tensor_tensor(m.act_lo[:, :, t * P:(t + 1) * P],
                                        ps[:, b:b + 2].rearrange("p b (k n) -> p (b k) n", n=P),
                                        m.act_hi[:, :, t * P:(t + 1) * P].bitcast(F32),
                                        ALU.subtract).then_inc(s.lo_done, 1)

            def finish(t):
                dve.wait_ge(s.rooted, before + t + 1)
                scale_and_shift(nc, m, chained, t).then_inc(s.stats_done, 1)

            for t in range(NT + 2):
                if t < NT:
                    statistics(t)
                    finish(t)
                if 1 <= t <= NT:
                    affine(t - 1)
                if t >= 2 and not output:
                    low_part(t - 2)

        @block.scalar
        def _(act):
            for t in range(NT + 1):
                if t < NT:
                    act.wait_ge(s.moments, before + t + 1)
                    deviation(nc, m, t).then_inc(s.rooted, 1)
                    act.wait_ge(s.stats_done, before + t + 1)
                    nc.scalar.activation(m.x[:, t], m.x[:, t], ACT.Identity, bias=m.nmr[:, t],
                                         scale=m.rstd[:, t]).then_inc(s.scaled, 1)
                if t >= 1 and not output:
                    act.wait_ge(s.turned, before + t)
                    b = 2 * ((t - 1) % 2)
                    nc.scalar.activation(m.act_hi[:, :, (t - 1) * P:t * P],
                                         ps[:, b:b + 2].rearrange("p b (k n) -> p (b k) n", n=P),
                                         ACT.Copy).then_inc(s.hi_done, 1)

        @block.tensor
        def _(pe):
            for t in range(0 if output else NT):
                pe.wait_ge(s.normed, before + t + 1)
                if t >= 2:
                    pe.wait_ge(s.lo_done, before + t - 1)
                for k in range(KD):
                    last = nc.tensor.transpose(ps[:, 2 * (t % 2) + k // 4, (k % 4) * P:(k % 4 + 1) * P],
                                               m.x[:, t, k::KD], m.ident[:])
                last.then_inc(s.turned, 1)


def dense_pieces(a):
    def columns(w, k, c, half):
        rows = k // 2
        return w.rearrange("(p k) n -> p k n", p=P)[:, half * rows:(half + 1) * rows, c * 512:(c + 1) * 512]

    w_in, w_a, w_b, w_out = a["w_in"][0], a["w_branch_a"][0], a["w_branch_b"][0], a["w_out"][0]
    pieces = []
    for c in range(5):
        pieces += [columns(w_in, KD, c, 0), columns(w_in, KD, c, 1)]
    for c, w in ((0, w_a), (1, w_a), (2, w_b), (3, w_b)):
        pieces += [columns(w_in, KD, 5 + c, 0), columns(w_in, KD, 5 + c, 1)]
        pieces.append(w.rearrange("(p k) n -> p k n", p=P)[:, :, (c % 2) * 512:(c % 2 + 1) * 512])
    for c in range(2):
        pieces += [columns(w_out, KD, c, 0), columns(w_out, KD, c, 1)]
    return pieces


class WeightRing:

    def __init__(self, nc, m, ctx, tag, pieces):
        self.nc, self.m, self.pieces = nc, m, pieces
        self.loaded = [ctx.enter_context(nc.semaphore(f"{tag}_loaded{i}")) for i in range(NRAW)]
        self.hi_split = ctx.enter_context(nc.semaphore(f"{tag}_hi_split"))
        self.lo_split = ctx.enter_context(nc.semaphore(f"{tag}_lo_split"))
        self.freed = {}

    def load(self, sp, i):
        if i >= NRAW:
            sp.wait_ge(self.lo_split, i - NRAW + 1)
        dst = self.m.raw[:, i % NRAW].rearrange("p (k n) -> p k n", n=512)
        src = self.pieces[i]
        if not isinstance(src, tuple):
            sp.dma_start(dst, src).then_inc(self.loaded[i % NRAW], 16)
        else:
            sp.dma_start(dst[:, :, 0:FF], src[0]).then_inc(self.loaded[i % NRAW], 16)
            sp.dma_start(dst[:, :, FF:512], src[1]).then_inc(self.loaded[i % NRAW], 16)

    def loads_of(self, i):
        return 16 * sum(1 + isinstance(self.pieces[j], tuple) for j in range(i % NRAW, i + 1, NRAW))

    def split_hi(self, act, i):
        act.wait_ge(self.loaded[i % NRAW], self.loads_of(i))
        if i >= NSPLIT:
            act.wait_ge(*self.freed[i - NSPLIT])
        self.nc.scalar.activation(self.m.w_hi[:, i % NSPLIT], self.m.raw[:, i % NRAW],
                                  ACT.Copy).then_inc(self.hi_split, 1)

    def split_lo(self, dve, i):
        dve.wait_ge(self.hi_split, i + 1)
        self.nc.vector.tensor_tensor(self.m.w_lo[:, i % NSPLIT], self.m.raw[:, i % NRAW],
                                     self.m.w_hi[:, i % NSPLIT].bitcast(F32),
                                     ALU.subtract).then_inc(self.lo_split, 1)

    def ready(self, pe, i):
        pe.wait_ge(self.lo_split, i + 1)

    def hi(self, i):
        return self.m.w_hi[:, i % NSPLIT].rearrange("p (k n) -> p k n", n=512)

    def lo(self, i):
        return self.m.w_lo[:, i % NSPLIT].rearrange("p (k n) -> p k n", n=512)


def product3(nc, out, x_hi, x_lo, w_hi, w_lo, first, last):
    nc.tensor.matmul(out, x_hi, w_hi, start=first, stop=False)
    nc.tensor.matmul(out, x_hi, w_lo, start=False, stop=False)
    return nc.tensor.matmul(out, x_lo, w_hi, start=False, stop=last)


def mix_block(nc, m, ps, a):
    MAIN, SIDE, Z, TURN, YB = (0, 1), 2, (3, 4), (5, 6), 7
    NA = NT * HEADS
    with ExitStack() as ctx:
        def sem(name):
            return ctx.enter_context(nc.semaphore(f"mix_{name}"))

        ring = WeightRing(nc, m, ctx, "mix", dense_pieces(a)[:22])
        half_used, projected, gelu_out, copied = sem("half_used"), sem("projected"), sem("gelu_out"), sem("copied")
        small_in = sem("small_in")
        sg_turned, sg_w_ready = sem("sg_turned"), sem("sg_w_ready")
        v_moments, v_rooted = sem("v_moments"), sem("v_rooted")
        v_stats, v_scaled, v_normed = sem("v_stats"), sem("v_scaled"), sem("v_normed")
        gated, ya_ready = sem("gated"), sem("ya_ready")
        ya_turned, ya_hi, ya_lo = sem("ya_turned"), sem("ya_hi"), sem("ya_lo")
        z_ready, sig_ready, a_ready = sem("z_ready"), sem("sig_ready"), sem("a_ready")
        a_turned, aT_ready, av_done = sem("a_turned"), sem("aT_ready"), sem("av_done")
        yb_sum, yb_ready = sem("yb_sum"), sem("yb_ready")
        yb_turned, yb_hi, yb_lo = sem("yb_turned"), sem("yb_hi"), sem("yb_lo")
        gate_sum, branch_sum, gate_ready, merged = sem("gate_sum"), sem("branch_sum"), sem("gate_ready"), sem("merged")
        chain = sem("chain")
        for c in range(5):
            ring.freed[2 * c], ring.freed[2 * c + 1] = (half_used, c + 1), (projected, 4 * c + 4)
        for j in range(4):
            ring.freed[10 + 3 * j] = (half_used, 5 + j + 1)
            ring.freed[11 + 3 * j], ring.freed[12 + 3 * j] = (gate_sum, 4 * j + 4), (branch_sum, 4 * j + 4)
        block = ctx.enter_context(nc.Block())

        SPLIT_AFTER_STEP = {13: (14,), 15: (15,), 16: (16,), 29: (17,), 31: (18, 19)}
        SPLIT_AFTER_GATE = {10: (20,), 11: (21,)}

        def width(s):
            return (s // HEADS + 1) * P

        @block.sync
        def _(sp):
            ring.load(sp, 0)
            ring.load(sp, 1)
            sp.dma_start(m.sg_w[:], a["sg_w_s"][0].rearrange("g i j -> i g j")).then_inc(small_in, 16)
            sp.dma_start(m.sg_g[:], a["sg_ln_g"][0].partition_broadcast(P)).then_inc(small_in, 16)
            sp.dma_start(m.sg_bb[:], a["sg_ln_b"][0].partition_broadcast(P)).then_inc(small_in, 16)
            sp.dma_start(m.sg_b[:], a["sg_b_s"][0].rearrange("g i -> i g"),
                         allow_slow_non_contiguous=True).then_inc(small_in, 16)
            for i in range(2, len(ring.pieces)):
                ring.load(sp, i)

        @block.tensor
        def _(pe):
            def unit_start(u):
                if u - 2 >= 8:
                    pe.wait_ge(copied, u - 2 - 8 + 1)
                elif u - 2 >= 0:
                    pe.wait_ge(gelu_out, u - 2 + 1)

            def rows_unit(u, c, t):
                unit_start(u)
                for half in range(2):
                    i = 2 * c + half
                    if t == 0:
                        ring.ready(pe, i)
                    for k in range(4):
                        kk = 4 * half + k
                        last = product3(nc, ps[:, MAIN[u % 2]], m.act_hi[:, kk, t * P:(t + 1) * P],
                                        m.act_lo[:, kk, t * P:(t + 1) * P], ring.hi(i)[:, k], ring.lo(i)[:, k],
                                        kk == 0, kk == KD - 1)
                    if half == 0 and t == NT - 1:
                        last.then_inc(half_used, 1)
                last.then_inc(projected, 1)

            def features_unit(u, c, f):
                unit_start(u)
                for half in range(2):
                    i = 2 * c + half
                    if f == 0:
                        ring.ready(pe, i)
                    cols = slice(f * P, (f + 1) * P)
                    for k in range(4):
                        kk = 4 * half + k
                        last = product3(nc, ps[:, MAIN[u % 2]], ring.hi(i)[:, k, cols], ring.lo(i)[:, k, cols],
                                        m.act_hi[:, kk], m.act_lo[:, kk], kk == 0, kk == KD - 1)
                    if half == 0 and f == 3:
                        last.then_inc(half_used, 1)
                last.then_inc(projected, 1)

            for t in range(NT):
                rows_unit(t, 0, t)
            pe.wait_ge(small_in, 64)
            for g in range(SGG):
                last = nc.tensor.transpose(ps[:, YB, g * P:(g + 1) * P], m.sg_w[:, g], m.ident[:])
            last.then_inc(sg_turned, 1)
            for t in range(NT):
                rows_unit(4 + t, 1, t)
            for f in range(4):
                features_unit(8 + f, 2, f)
            pe.wait_ge(sg_w_ready, 1)
            for t in range(NT):
                pe.wait_ge(v_normed, t + 1)
                if t >= 2:
                    pe.wait_ge(ya_ready, t - 1)
                for g in range(SGG):
                    last = nc.tensor.matmul(ps[:, Z[t % 2], g * P:(g + 1) * P], m.sg_wT[:, g],
                                            m.merged[:, t, SG + g * P:SG + (g + 1) * P], start=True, stop=True)
                last.then_inc(gated, 1)
            for f in range(4):
                features_unit(12 + f, 3, f)
            for t in range(NT):
                pe.wait_ge(ya_ready, t + 1)
                if t >= 2:
                    pe.wait_ge(ya_lo, t - 1)
                for k in range(4):
                    last = nc.tensor.transpose(ps[:, TURN[t % 2], k * P:(k + 1) * P],
                                               m.merged[:, t, k:SG:4], m.ident[:])
                last.then_inc(ya_turned, 1)
            for t in range(NT):
                rows_unit(16 + t, 4, t)

            def gate_part(g, part):
                j, t = divmod(g, NT)
                bank = MAIN[g % 2]
                i = 10 + 3 * j + part // 2
                if part == 0:
                    if g < 2:
                        pe.wait_ge(copied, 12 - 1 + g)
                    else:
                        pe.wait_ge(gate_ready, g - 1)
                if t == 0 and part % 2 == 0:
                    ring.ready(pe, i)
                for k in (2 * (part % 2), 2 * (part % 2) + 1):
                    kk = 4 * (part // 2) + k
                    last = product3(nc, ps[:, bank], m.act_hi[:, kk, t * P:(t + 1) * P],
                                    m.act_lo[:, kk, t * P:(t + 1) * P], ring.hi(i)[:, k], ring.lo(i)[:, k],
                                    kk == 0, kk == KD - 1)
                if part == 1 and t == NT - 1:
                    last.then_inc(half_used, 1)
                if part < 3:
                    return
                last.then_inc(gate_sum, 1)
                i += 1
                if t == 0:
                    ring.ready(pe, i)
                if g >= 1:
                    pe.wait_ge(merged, g)
                else:
                    pe.wait_ge(ya_lo, NT)
                y_hi, y_lo = (m.yaT_hi, m.yaT_lo) if j < 2 else (m.ybT_hi, m.ybT_lo)
                if g == 8:
                    pe.wait_ge(yb_lo, NT)
                for k in range(4):
                    last = product3(nc, ps[:, SIDE], y_hi[:, k, t * P:(t + 1) * P], y_lo[:, k, t * P:(t + 1) * P],
                                    ring.hi(i)[:, k], ring.lo(i)[:, k], k == 0, k == 3)
                last.then_inc(branch_sum, 1)

            def scores(s):
                qb, h = divmod(s, HEADS)
                n = width(s)
                if s >= 2:
                    pe.wait_ge(sig_ready, s - 1)
                elif s == 0:
                    pe.wait_ge(copied, 12)
                rows = slice(HD * (h % 2), HD * (h % 2) + HD)
                nc.tensor.matmul(ps[:, Z[s % 2], 0:n], m.qT[rows, h // 2, qb * P:(qb + 1) * P],
                                 m.kT[rows, h // 2, 0:n], start=True, stop=False)
                nc.tensor.matmul(ps[:, Z[s % 2], n - P:n], m.ident_bf[:], m.future_bf[:],
                                 start=False, stop=True).then_inc(z_ready, 1)

            def turn(s):
                pe.wait_ge(a_ready, s + 1)
                if s >= 2:
                    pe.wait_ge(aT_ready, s - 1)
                for c in range(width(s) // P):
                    last = nc.tensor.transpose(ps[:, TURN[s % 2], c * P:(c + 1) * P],
                                               m.sig_pos[:, s % 2, c * P:(c + 1) * P], m.ident[:])
                last.then_inc(a_turned, 1)

            def weighted_values(s):
                qb, h = divmod(s, HEADS)
                pe.wait_ge(aT_ready, s + 1)
                if h == 0 and qb:
                    pe.wait_ge(yb_ready, qb)
                for c in range(qb + 1):
                    last = nc.tensor.matmul(ps[:, YB, h * HD:(h + 1) * HD], m.aT[:, s % 2, c * P:(c + 1) * P],
                                            m.vsb[:, c, h * HD:(h + 1) * HD], start=(c == 0), stop=(c == qb))
                last.then_inc(av_done, 1)

            for s in range(NA + 3):
                if s < NA:
                    scores(s)
                    gate_part(s // 4, s % 4)
                if 2 <= s < NA + 2:
                    turn(s - 2)
                if s >= 3:
                    weighted_values(s - 3)
            for t in range(NT):
                pe.wait_ge(yb_ready, t + 1)
                if t >= 2:
                    pe.wait_ge(yb_lo, t - 1)
                for k in range(4):
                    last = nc.tensor.transpose(ps[:, TURN[t % 2], k * P:(k + 1) * P], m.yb[:, t, k:512:4],
                                               m.ident[:])
                last.then_inc(yb_turned, 1)
            for g in range(8, 16):
                for part in range(4):
                    gate_part(g, part)

        def turned_view(bank):
            return ps[:, bank].rearrange("p (k n) -> p k n", n=P)

        @block.scalar
        def _(act):
            for i in range(4):
                ring.split_hi(act, i)
            for u in range(8):
                t = u % 4
                act.wait_ge(projected, u + 1)
                half = SG * (u // 4)
                nc.scalar.activation(m.merged[:, t, half:half + SG], ps[:, MAIN[u % 2]],
                                     ACT.Gelu_apprx_tanh).then_inc(gelu_out, 1)
                if t >= 2:
                    ring.split_hi(act, 4 + 2 * (u // 4) + t - 2)
            act.wait_ge(v_moments, NT)
            for t in range(NT):
                deviation(nc, m, t).then_inc(v_rooted, 1)
            for t in range(NT):
                act.wait_ge(v_stats, t + 1)
                v = m.merged[:, t, SG:2 * SG]
                nc.scalar.activation(v, v, ACT.Identity, bias=m.nmr[:, t], scale=m.rstd[:, t]).then_inc(v_scaled, 1)
            for i in range(8, 12):
                ring.split_hi(act, i)
            for t in range(NT):
                act.wait_ge(ya_turned, t + 1)
                nc.scalar.activation(m.yaT_hi[:, :, t * P:(t + 1) * P], turned_view(TURN[t % 2]),
                                     ACT.Copy).then_inc(ya_hi, 1)
            ring.split_hi(act, 12)
            ring.split_hi(act, 13)

            def gate(g):
                act.wait_ge(gate_sum, g + 1)
                if g >= 2:
                    act.wait_ge(merged, g - 1)
                nc.scalar.activation(m.gate[:, g % 2], ps[:, MAIN[g % 2]], ACT.Sigmoid).then_inc(gate_ready, 1)

            for s in range(NA + 3):
                if s < NA:
                    n = width(s)
                    act.wait_ge(z_ready, s + 1)
                    if s >= 2:
                        act.wait_ge(a_turned, s - 1)
                    nc.scalar.activation(m.sig_neg[:, s % 2, 0:n], ps[:, Z[s % 2], 0:n], ACT.Sigmoid,
                                         scale=-HD ** -0.5)
                    nc.scalar.activation(m.sig_pos[:, s % 2, 0:n], ps[:, Z[s % 2], 0:n], ACT.Sigmoid,
                                         scale=HD ** -0.5).then_inc(sig_ready, 1)
                if s >= 2 and s - 2 < NA:
                    r = s - 2
                    act.wait_ge(a_turned, r + 1)
                    if r >= 2:
                        act.wait_ge(av_done, r - 1)
                    nc.scalar.activation(m.aT[:, r % 2, 0:width(r)], ps[:, TURN[r % 2], 0:width(r)],
                                         ACT.Copy).then_inc(aT_ready, 1)
                if s % 4 == 0 and 4 <= s:
                    gate(s // 4 - 1)
                for i in SPLIT_AFTER_STEP.get(s, ()):
                    ring.split_hi(act, i)
            for t in range(NT):
                act.wait_ge(yb_turned, t + 1)
                nc.scalar.activation(m.ybT_hi[:, :, t * P:(t + 1) * P], turned_view(TURN[t % 2]),
                                     ACT.Copy).then_inc(yb_hi, 1)
            for g in range(8, 16):
                gate(g)
                for i in SPLIT_AFTER_GATE.get(g, ()):
                    ring.split_hi(act, i)

        @block.vector
        def _(dve):
            done = [0]

            def chained(ins):
                done[0] += 1
                ins.then_inc(chain, 1)
                dve.wait_ge(chain, done[0])

            for i in range(6):
                ring.split_lo(dve, i)
            dve.wait_ge(sg_turned, 1)
            chained(nc.vector.tensor_copy(m.sg_wT[:], ps[:, YB].rearrange("p (g n) -> p g n", n=P)))
            nc.vector.memset(m.sg_wT[HD:P, :, 0:HD], 0.0).then_inc(sg_w_ready, 1)
            for t in range(NT):
                v = m.merged[:, t, SG:2 * SG]
                dve.wait_ge(gelu_out, 4 + t + 1)
                chained(nc.vector.bn_stats(m.stats[:, t, 0], v))
                nc.vector.bn_aggr(m.mv[:, t], m.stats[:, t, 0:1]).then_inc(v_moments, 1)
                if t >= 2:
                    ring.split_lo(dve, 4 + t)
            for t in range(NT):
                dve.wait_ge(v_rooted, t + 1)
                scale_and_shift(nc, m, chained, t).then_inc(v_stats, 1)
            for t in range(NT):
                v = m.merged[:, t, SG:2 * SG]
                dve.wait_ge(v_scaled, t + 1)
                chained(nc.vector.tensor_tensor(v, v, m.sg_g[:], ALU.mult))
                nc.vector.tensor_tensor(v, v, m.sg_bb[:], ALU.add).then_inc(v_normed, 1)

            def copy_out(u, dst):
                dve.wait_ge(projected, u + 1)
                nc.vector.tensor_copy(dst, ps[:, MAIN[u % 2]]).then_inc(copied, 1)

            for f in range(4):
                copy_out(8 + f, m.qT[:, f])
            ring.split_lo(dve, 8)
            ring.split_lo(dve, 9)
            for t in range(NT):
                dve.wait_ge(gated, t + 1)
                for g in range(SGG):
                    cols = slice(g * P, (g + 1) * P)
                    last = nc.vector.scalar_tensor_tensor(out=m.merged[:, t, cols], in0=ps[:, Z[t % 2], cols],
                                                          scalar=m.sg_b[:, g:g + 1], in1=m.merged[:, t, cols],
                                                          op0=ALU.add, op1=ALU.mult)
                last.then_inc(ya_ready, 1)
            for f in range(4):
                copy_out(12 + f, m.kT[:, f])
            ring.split_lo(dve, 10)
            ring.split_lo(dve, 11)
            for t in range(NT):
                dve.wait_ge(ya_hi, t + 1)
                nc.vector.tensor_tensor(m.yaT_lo[:, :, t * P:(t + 1) * P], turned_view(TURN[t % 2]),
                                        m.yaT_hi[:, :, t * P:(t + 1) * P].bitcast(F32),
                                        ALU.subtract).then_inc(ya_lo, 1)
            for t in range(NT):
                copy_out(16 + t, m.vsb[:, t])
            ring.split_lo(dve, 12)
            ring.split_lo(dve, 13)
            for b in range(2):
                last = nc.vector.memset(m.stick[:, b, P:SEQ + 1:P], 1.0)
            chained(last)

            def merge(g):
                j, t = divmod(g, NT)
                cols = slice((j % 2) * 512, (j % 2 + 1) * 512)
                dve.wait_ge(gate_ready, g + 1)
                dve.wait_ge(branch_sum, g + 1)
                gate = m.gate[:, g % 2]
                if j < 2:
                    nc.vector.tensor_tensor(m.merged[:, t, cols], gate, ps[:, SIDE], ALU.mult).then_inc(merged, 1)
                else:
                    chained(nc.vector.tensor_tensor(gate, gate, ps[:, SIDE], ALU.mult))
                    nc.vector.tensor_tensor(m.merged[:, t, cols], m.merged[:, t, cols], gate,
                                            ALU.add).then_inc(merged, 1)

            for s in range(NA + 3):
                if s < NA:
                    n = width(s)
                    b = s % 2
                    dve.wait_ge(sig_ready, s + 1)
                    chained(nc.vector.tensor_tensor_scan(m.stick[:, b, 0:n][:, ::-1], m.sig_neg[:, b, 0:n][:, ::-1],
                                                         m.sig_neg[:, b, 0:n][:, ::-1], 1.0, ALU.mult, ALU.bypass))
                    nc.vector.tensor_tensor(m.sig_pos[:, b, 0:n], m.sig_pos[:, b, 0:n], m.stick[:, b, 1:n + 1],
                                            ALU.mult).then_inc(a_ready, 1)
                if s >= 3 and (s - 3) % HEADS == HEADS - 1:
                    qb = (s - 3) // HEADS
                    dve.wait_ge(av_done, s - 3 + 1)
                    nc.vector.tensor_copy(m.yb[:, qb], ps[:, YB]).then_inc(yb_ready, 1)
                if s % 4 == 0 and 4 <= s:
                    merge(s // 4 - 1)
                for i in SPLIT_AFTER_STEP.get(s, ()):
                    ring.split_lo(dve, i)
            for t in range(NT):
                dve.wait_ge(yb_hi, t + 1)
                nc.vector.tensor_tensor(m.ybT_lo[:, :, t * P:(t + 1) * P], turned_view(TURN[t % 2]),
                                        m.ybT_hi[:, :, t * P:(t + 1) * P].bitcast(F32),
                                        ALU.subtract).then_inc(yb_lo, 1)
            for g in range(8, 16):
                merge(g)
                for i in SPLIT_AFTER_GATE.get(g, ()):
                    ring.split_lo(dve, i)


def out_block(nc, m, ps, a, h0):
    MAIN, TURN = (4, 5), (0, 2)
    with ExitStack() as ctx:
        def sem(name):
            return ctx.enter_context(nc.semaphore(f"out_{name}"))

        ring = WeightRing(nc, m, ctx, "out", dense_pieces(a)[22:])
        rows_in, turned, hi_done, lo_done = sem("rows_in"), sem("turned"), sem("hi_done"), sem("lo_done")
        summed, added = sem("summed"), sem("added")
        block = ctx.enter_context(nc.Block())

        @block.sync
        def _(sp):
            ring.load(sp, 0)
            ring.load(sp, 1)
            for t in range(NT):
                sp.dma_start(m.x[:, t], h0[t * P:(t + 1) * P, :]).then_inc(rows_in, 16)
            ring.load(sp, 2)
            ring.load(sp, 3)

        @block.tensor
        def _(pe):
            for t in range(NT):
                if t >= 2:
                    pe.wait_ge(lo_done, t - 1)
                for k in range(KD):
                    last = nc.tensor.transpose(ps[:, TURN[t % 2] + k // 4, (k % 4) * P:(k % 4 + 1) * P],
                                               m.merged[:, t, k::KD], m.ident[:])
                last.then_inc(turned, 1)
            for u in range(2 * NT):
                c, t = divmod(u, NT)
                if u < NT:
                    pe.wait_ge(lo_done, t + 1)
                if u >= 2:
                    pe.wait_ge(added, u - 1)
                for kk in range(KD):
                    i = 2 * c + kk // 4
                    if t == 0 and kk % 4 == 0:
                        ring.ready(pe, i)
                    last = product3(nc, ps[:, MAIN[u % 2]], m.act_hi[:, kk, t * P:(t + 1) * P],
                                    m.act_lo[:, kk, t * P:(t + 1) * P], ring.hi(i)[:, kk % 4],
                                    ring.lo(i)[:, kk % 4], kk == 0, kk == KD - 1)
                last.then_inc(summed, 1)

        @block.scalar
        def _(act):
            for t in range(NT):
                act.wait_ge(turned, t + 1)
                b = TURN[t % 2]
                nc.scalar.activation(m.act_hi[:, :, t * P:(t + 1) * P],
                                     ps[:, b:b + 2].rearrange("p b (k n) -> p (b k) n", n=P),
                                     ACT.Copy).then_inc(hi_done, 1)
                ring.split_hi(act, t)

        @block.vector
        def _(dve):
            for t in range(NT):
                dve.wait_ge(hi_done, t + 1)
                b = TURN[t % 2]
                nc.vector.tensor_tensor(m.act_lo[:, :, t * P:(t + 1) * P],
                                        ps[:, b:b + 2].rearrange("p b (k n) -> p (b k) n", n=P),
                                        m.act_hi[:, :, t * P:(t + 1) * P].bitcast(F32),
                                        ALU.subtract).then_inc(lo_done, 1)
                ring.split_lo(dve, t)
            dve.wait_ge(rows_in, 16 * NT)
            for u in range(2 * NT):
                c, t = divmod(u, NT)
                dve.wait_ge(summed, u + 1)
                row = m.x[:, t, c * 512:(c + 1) * 512]
                nc.vector.scalar_tensor_tensor(out=row, in0=row, scalar=ALPHA, in1=ps[:, MAIN[u % 2]],
                                               op0=ALU.mult, op1=ALU.add).then_inc(added, 1)


def routing_block(nc, m, ps, a, acc_dram, acc_odd_dram):
    LOGIT, MAIN, TURN, SUM, POS, ALL = 0, (1, 2), 3, (4, 5), 6, 7
    half_rows = KD // 2
    with ExitStack() as ctx:
        def sem(name):
            return ctx.enter_context(nc.semaphore(f"route_{name}"))

        def halves(w):
            v = w.rearrange("(p k) n -> p k n", p=P)
            return v[:, 0:half_rows], v[:, half_rows:KD]

        g, u = halves(a["sh_w_gate"][0]), halves(a["sh_w_up"][0])
        ring = WeightRing(nc, m, ctx, "shared", [(g[0], u[0]), (g[1], u[1])])
        router_in, down_in = sem("router_in"), sem("down_in")
        router_hi, router_split, logits, scored = sem("router_hi"), sem("router_split"), sem("logits"), sem("scored")
        picked, counted, tags_ready = sem("picked"), sem("counted"), sem("tags_ready")
        gu_sum, silu_out, h_ready = sem("gu_sum"), sem("silu_out"), sem("h_ready")
        turned, hT_ready, summed, acc_ready = sem("turned"), sem("hT_ready"), sem("summed"), sem("acc_ready")
        acc_out = [sem("acc_out0"), sem("acc_out1")]
        chain, index_base, zeros = sem("chain"), sem("index_base"), sem("zeros")
        block = ctx.enter_context(nc.Block())

        @block.sync
        def _(sp):
            sp.dma_start(m.router[:], a["router_w"][0].rearrange("(p k) n -> p k n", p=P)).then_inc(router_in, 16)
            sp.dma_start(m.r_bias[:], a["router_bias"][0].partition_broadcast(P)).then_inc(router_in, 16)
            ring.load(sp, 0)
            ring.load(sp, 1)
            sp.dma_start(m.sh_down[:], a["sh_w_down"][0].rearrange("(p j) n -> p (j n)", p=P)).then_inc(down_in, 16)
            sp.wait_ge(zeros, 1)
            for t in range(NT):
                sp.dma_start(acc_odd_dram[t * P:(t + 1) * P, :], m.zero_rows[:]).then_inc(acc_out[t % 2], 16)
            for t in range(NT):
                sp.wait_ge(acc_ready, t + 1)
                sp.dma_start(acc_dram[t * P:(t + 1) * P, :], m.acc[:, t % 2]).then_inc(acc_out[t % 2], 16)
            sp.wait_ge(acc_out[0], 64)
            sp.wait_ge(acc_out[1], 64)

        @block.gpsimd
        def _(pool):
            nc.gpsimd.memset(m.zero_rows[:], 0.0).then_inc(zeros, 1)
            for t in range(NT):
                nc.gpsimd.memset(m.tags[:, t, :, 0:1], float(t * P))
                nc.gpsimd.iota(m.tags[:, t, :, 1:2], pattern=[[0, NE], [0, 1]], base=0, channel_multiplier=1,
                               allow_small_or_imprecise_dtypes=True)
                last = nc.gpsimd.memset(m.tags[:, t, :, 2:3], -FAR)
            last.then_inc(index_base, 1)

        @block.tensor
        def _(pe):
            pe.wait_ge(router_split, 1)
            for t in range(NT):
                for k in range(KD):
                    last = product3(nc, ps[:, LOGIT, t * NE:(t + 1) * NE], m.act_hi[:, k, t * P:(t + 1) * P],
                                    m.act_lo[:, k, t * P:(t + 1) * P], m.r_hi[:, k], m.r_lo[:, k],
                                    k == 0, k == KD - 1)
            last.then_inc(logits, 1)
            for t in range(NT):
                if t >= 2:
                    pe.wait_ge(h_ready, t - 1)
                for kk in range(KD):
                    if t == 0 and kk % 4 == 0:
                        ring.ready(pe, kk // 4)
                    last = product3(nc, ps[:, MAIN[t % 2]], m.act_hi[:, kk, t * P:(t + 1) * P],
                                    m.act_lo[:, kk, t * P:(t + 1) * P], ring.hi(kk // 4)[:, kk % 4],
                                    ring.lo(kk // 4)[:, kk % 4], kk == 0, kk == KD - 1)
                last.then_inc(gu_sum, 1)
            pe.wait_ge(picked, 1)
            for t in range(NT):
                for o in range(t + 1):
                    last = nc.tensor.matmul(ps[:, POS, t * NE:(t + 1) * NE],
                                            m.ones_bf[:] if o < t else m.earlier_bf[:], m.pick_bf[:, o],
                                            start=(o == 0), stop=(o == t))
            for o in range(NT):
                last = nc.tensor.matmul(ps[:, ALL, 0:NE], m.ones_bf[:], m.pick_bf[:, o],
                                        start=(o == 0), stop=(o == NT - 1))
            last.then_inc(counted, 1)
            pe.wait_ge(down_in, 16)
            for t in range(NT):
                pe.wait_ge(h_ready, t + 1)
                if t >= 1:
                    pe.wait_ge(hT_ready, t)
                for j in range(2):
                    last = nc.tensor.transpose(ps[:, TURN, j * P:(j + 1) * P], m.sh_h[:, t, j::2], m.ident[:])
                last.then_inc(turned, 1)
                pe.wait_ge(hT_ready, t + 1)
                if t >= 1:
                    pe.wait_ge(acc_ready, t)
                for c in range(2):
                    for j in range(2):
                        last = nc.tensor.matmul(ps[:, SUM[c]], m.sh_hT[:, j, t * P:(t + 1) * P],
                                                m.sh_down[:, j * D + c * 512:j * D + (c + 1) * 512],
                                                start=(j == 0), stop=(j == 1))
                last.then_inc(summed, 1)

        @block.scalar
        def _(act):
            act.wait_ge(router_in, 32)
            nc.scalar.activation(m.r_hi[:], m.router[:], ACT.Copy).then_inc(router_hi, 1)
            ring.split_hi(act, 0)
            ring.split_hi(act, 1)
            act.wait_ge(logits, 1)
            nc.scalar.activation(m.score[:], ps[:, LOGIT, 0:NT * NE].rearrange("p (t e) -> p t e", e=NE),
                                 ACT.Sigmoid).then_inc(scored, 1)
            for t in range(NT):
                act.wait_ge(gu_sum, t + 1)
                nc.scalar.activation(m.sh_h[:, t], ps[:, MAIN[t % 2], 0:FF], ACT.Silu).then_inc(silu_out, 1)
            for t in range(NT):
                act.wait_ge(turned, t + 1)
                nc.scalar.activation(m.sh_hT[:, :, t * P:(t + 1) * P],
                                     ps[:, TURN, 0:2 * P].rearrange("p (j n) -> p j n", n=P),
                                     ACT.Copy).then_inc(hT_ready, 1)

        @block.vector
        def _(dve):
            done = [0]

            def chained(ins):
                done[0] += 1
                ins.then_inc(chain, 1)
                dve.wait_ge(chain, done[0])

            dve.wait_ge(router_hi, 1)
            nc.vector.tensor_tensor(m.r_lo[:], m.router[:], m.r_hi[:].bitcast(F32),
                                    ALU.subtract).then_inc(router_split, 1)
            ring.split_lo(dve, 0)
            ring.split_lo(dve, 1)
            dve.wait_ge(scored, 1)
            chained(nc.vector.tensor_tensor(m.sel[:], m.score[:], m.r_bias[:].unsqueeze(1).to_broadcast([P, NT, NE]),
                                            ALU.add))
            for t in range(NT):
                for q in range(NGRP):
                    last = nc.vector.max(out=m.top[:, t, q], in_=m.sel[:, t, q * 8:(q + 1) * 8])
            chained(last)
            chained(nc.vector.tensor_tensor(m.grp[:], m.top[:, :, :, 0], m.top[:, :, :, 1], ALU.add))
            for t in range(NT):
                mine = m.grp[:, t].unsqueeze(2).to_broadcast([P, NGRP, NGRP])
                other = m.grp[:, t].unsqueeze(1).to_broadcast([P, NGRP, NGRP])
                nc.vector.tensor_tensor(m.beats[:, t], other, mine, ALU.is_gt)
                last = nc.vector.tensor_tensor(m.ties[:, t], other, mine, ALU.is_equal)
            chained(last)
            for t in range(NT):
                last = nc.vector.tensor_tensor(m.ties[:, t], m.ties[:, t], m.lower_grp[:], ALU.mult)
            chained(last)
            chained(nc.vector.tensor_tensor(m.beats[:], m.beats[:], m.ties[:], ALU.add))
            chained(nc.vector.tensor_reduce(m.rank[:].rearrange("p t g -> p (t g)"),
                                            m.beats[:].rearrange("p t g o -> p (t g) o"), AX, ALU.add))
            chained(nc.vector.tensor_scalar(m.rank[:], m.rank[:], 3.5, -1e30, ALU.is_gt, ALU.mult))
            chained(nc.vector.tensor_tensor(m.sel[:].rearrange("p t (g e) -> p (t g) e", e=8),
                                            m.sel[:].rearrange("p t (g e) -> p (t g) e", e=8),
                                            m.rank[:].rearrange("p t g -> p (t g)").unsqueeze(2)
                                            .to_broadcast([P, NT * NGRP, 8]), ALU.add))
            for t in range(NT):
                last = nc.vector.max(out=m.top8[:, t], in_=m.sel[:, t])
            chained(last)
            for t in range(NT):
                last = nc.vector.match_replace(out=m.rest[:, t], in_to_replace=m.top8[:, t], in_values=m.sel[:, t],
                                               imm_value=-3e38)
            chained(last)
            chained(nc.vector.tensor_scalar(m.rest[:], m.rest[:], -2e38, None, ALU.is_lt))
            nc.vector.tensor_copy(m.pick_bf[:], m.rest[:]).then_inc(picked, 1)
            chained(nc.vector.tensor_tensor(m.score[:], m.score[:], m.rest[:], ALU.mult))
            chained(nc.vector.tensor_reduce(m.den[:], m.score[:], AX, ALU.add))
            chained(nc.vector.reciprocal(m.den[:], m.den[:]))
            for t in range(NT):
                last = nc.vector.tensor_scalar(m.score[:, t], m.score[:, t], m.den[:, t:t + 1], ROUTED_SCALE,
                                               ALU.mult, ALU.mult)
            chained(last)
            dve.wait_ge(index_base, 1)
            for part in range(3):
                tag = m.tags[:, :, :, 3 + part]
                chained(nc.vector.tensor_copy(tag, m.score[:]))
                if part < 2:
                    chained(nc.vector.tensor_tensor(m.score[:], m.score[:], tag, ALU.subtract))
            for t in range(NT):
                dve.wait_ge(silu_out, t + 1)
                nc.vector.tensor_tensor(m.sh_h[:, t], m.sh_h[:, t], ps[:, MAIN[t % 2], FF:2 * FF],
                                        ALU.mult).then_inc(h_ready, 1)
            for t in range(NT):
                dve.wait_ge(summed, t + 1)
                if t >= 2:
                    dve.wait_ge(acc_out[t % 2], 48)
                nc.vector.scalar_tensor_tensor(out=m.acc[:, t % 2].rearrange("p (c n) -> p c n", n=512),
                                               in0=m.x[:, t].rearrange("p (c n) -> p c n", n=512), scalar=ALPHA,
                                               in1=ps[:, SUM[0]:SUM[1] + 1], op0=ALU.mult,
                                               op1=ALU.add).then_inc(acc_ready, 1)
            chained(nc.vector.tensor_scalar(m.rest[:], m.rest[:], -FAR, FAR, ALU.mult, ALU.add))
            dve.wait_ge(counted, 1)
            nc.vector.tensor_tensor(m.slot_of[:], m.rest[:],
                                    ps[:, POS, 0:NT * NE].rearrange("p (t e) -> p t e", e=NE), ALU.add)
            chained(nc.vector.tensor_reduce(m.peak[:], ps[:, ALL, 0:NE], AX, ALU.max))
            nc.vector.tensor_copy(m.peak_i[:], m.peak[:])


class Expert:

    def __init__(self, r, quad, q):
        quad, q = quad + q // 4, q % 4
        self.r, self.quad, self.q = r, quad, q
        self.e = 4 * quad + q
        self.b = q % 2
        self.it = r * NE + self.e
        self.turn4 = r * (NE // 4) + quad + 1
        self.turn2 = r * (NE // 2) + 2 * quad + q // 2 + 1

    def next(self, n):
        return Expert(self.r, self.quad, self.q + n)


def experts_block(nc, m, ps, a, h1, acc_dram, acc_odd_dram, CAP):
    GU, HT, XT, Y, TAGS = (0, 1), 2, 3, 5, 7
    LEAD = 2
    LEAD4 = 4
    ROUNDS = -(-SEQ // CAP)
    QUADS = NE // 4
    w_gate, w_up, w_down = a["moe_w_gate"][0], a["moe_w_up"][0], a["moe_w_down"][0]
    with ExitStack() as ctx:
        def sem(name):
            return ctx.enter_context(nc.semaphore(f"moe_{name}"))

        gu_in = [[sem(f"gu_in{b}{half}") for half in range(2)] for b in range(2)]
        dn_in = [sem(f"dn_in{b}") for b in range(2)]
        gu_hi, gu_lo, half_used = sem("gu_hi"), sem("gu_lo"), sem("half_used")
        dn_hi, dn_lo = sem("dn_hi"), sem("dn_lo")
        hot_ready, located, found, get_ready, put_ready = (sem("hot_ready"), sem("located"), sem("found"),
                                                           sem("get_ready"), sem("put_ready"))
        got = [sem(f"got{q}") for q in range(4)]
        put = [sem("put_even"), sem("put_odd")]
        x_turned, x_hi, x_lo = sem("x_turned"), sem("x_hi"), sem("x_lo")
        gu_sum, silu_out, h_ready = sem("gu_sum"), sem("silu_out"), sem("h_ready")
        h_turned, hT_hi, hT_lo, y_sum, y_ready = (sem("h_turned"), sem("hT_hi"), sem("hT_lo"), sem("y_sum"),
                                                  sem("y_ready"))
        cleared, passed = sem("cleared"), sem("passed")
        block = ctx.enter_context(nc.Block())

        def rounds(eng, body):
            peak = eng.value_load(m.peak_i[0:1, 0:1], min_val=0, max_val=SEQ)
            with eng.Fori(0, ROUNDS) as r:
                with eng.If(peak > r * CAP):
                    body(r)

        def all_experts(eng, r, step):
            for q in range(4):
                step(Expert(r, 0, q), q)
            with eng.Fori(1, QUADS - 2) as quad:
                for q in range(4):
                    step(Expert(r, quad, q))
            for quad in (QUADS - 2, QUADS - 1):
                for q in range(4):
                    step(Expert(r, quad, q), 4 * (quad - QUADS) + q)

        def x_banks():
            return ps[:, XT:XT + 2, 0:4 * CAP]

        @block.sync
        def _(sp):
            def load_gate_up(x):
                for half in range(2):
                    sp.wait_ge(gu_lo, 2 * x.it + half - 4 + 1 + 2 * LEAD)
                    dst = m.gu_raw[:, 2 * x.b + half].rearrange("p (w n) -> p w n", w=2)
                    for w, src in enumerate((w_gate, w_up)):
                        rows = src[bass.ds(x.e, 1)].rearrange("o (p k) n -> p o (k n)", p=P)
                        sp.dma_start(dst[:, w:w + 1], rows[:, :, half * (HC // 2):(half + 1) * (HC // 2)]) \
                          .then_inc(gu_in[x.b][half], 16)

            def load_down(x):
                sp.wait_ge(dn_lo, x.it - 2 + 1 + LEAD)
                sp.dma_start(m.dn_raw[:, x.b:x.b + 1],
                             w_down[bass.ds(x.e, 1)].rearrange("o (p j) n -> p o (j n)", p=P)) \
                  .then_inc(dn_in[x.b], 16)

            def body(r):
                load_gate_up(Expert(r, 0, 0))
                load_gate_up(Expert(r, 0, 1))

                def step(x, at=0):
                    load_down(x)
                    if at not in (-1, -2):
                        load_gate_up(x.next(2))

                all_experts(sp, r, step)

            rounds(sp, body)

        @block.tensor
        def _(pe):
            pe.sem_inc(half_used, LEAD)
            pe.sem_inc(gu_sum, LEAD)
            pe.sem_inc(y_sum, LEAD)
            pe.sem_inc(x_turned, LEAD4)

            def locate(x):
                pe.wait_ge(hot_ready, x.it + 1)
                pe.wait_ge(found, x.it + LEAD)
                for t in range(NT):
                    last = nc.tensor.matmul(ps[0:CAP, TAGS, 0:6], m.onehot[:, x.b, t],
                                            m.tags[:, t, bass.ds(x.e, 1), :].rearrange("p o c -> p (o c)"),
                                            start=(t == 0), stop=(t == NT - 1))
                last.then_inc(located, 1)

            def turn_x(x):
                pe.wait_ge(got[x.q], 16 * x.turn4)
                pe.wait_ge(x_lo, x.it + LEAD)
                for k in range(KD):
                    last = nc.tensor.transpose(ps[:, XT + k // 4, (k % 4) * CAP:(k % 4 + 1) * CAP],
                                               m.xg[x.q][0:CAP, k::KD], m.ident[0:CAP, 0:CAP])
                last.then_inc(x_turned, 1)

            def gate_up(x, half):
                pe.wait_ge(gu_lo, 2 * x.it + half + 1 + 2 * LEAD)
                if half == 0:
                    pe.wait_ge(x_lo, x.it + 1 + LEAD)
                    pe.wait_ge(h_ready, x.it - 1 + LEAD)
                w_hi = m.w_hi[:, 2 * x.b + half].rearrange("p (w k n) -> p k w n", w=2, n=FF)
                w_lo = m.w_lo[:, 2 * x.b + half].rearrange("p (w k n) -> p k w n", w=2, n=FF)
                for k in range(4):
                    kk = 4 * half + k
                    cols = slice(kk * CAP, (kk + 1) * CAP)
                    last = product3(nc, ps[0:CAP, GU[x.b]].rearrange("p (w n) -> p w n", w=2),
                                    m.xgT_hi[:, x.b, cols], m.xgT_lo[:, x.b, cols], w_hi[:, k], w_lo[:, k],
                                    kk == 0, kk == KD - 1)
                last.then_inc(gu_sum if half else half_used, 1)

            def turn_h(x):
                pe.wait_ge(h_ready, x.it + 1 + LEAD)
                pe.wait_ge(hT_lo, x.it + LEAD)
                for j in range(2):
                    last = nc.tensor.transpose(ps[:, HT, j * CAP:(j + 1) * CAP], m.h[0:CAP, x.b, j::2],
                                               m.ident[0:CAP, 0:CAP])
                last.then_inc(h_turned, 1)

            def down(x):
                pe.wait_ge(hT_lo, x.it + 1 + LEAD)
                pe.wait_ge(dn_lo, x.it + 1 + LEAD)
                pe.wait_ge(y_ready, x.it + LEAD)
                for c in range(2):
                    for j in range(2):
                        rows, cols = slice(j * CAP, (j + 1) * CAP), slice(j * D + c * 512, j * D + (c + 1) * 512)
                        last = product3(nc, ps[0:CAP, Y + c], m.hT_hi[:, x.b, rows], m.hT_lo[:, x.b, rows],
                                        m.dn_hi[:, x.b, cols], m.dn_lo[:, x.b, cols], j == 0, j == 1)
                last.then_inc(y_sum, 1)

            def body(r):
                for q in range(4):
                    locate(Expert(r, 0, q))
                turn_x(Expert(r, 0, 0))

                def step(x, at=99):
                    if at != 0:
                        turn_h(x.next(-1))
                    gate_up(x, 0)
                    if not -4 <= at <= -1:
                        locate(x.next(4))
                    gate_up(x, 1)
                    if at != -1:
                        turn_x(x.next(1))
                    if at != 0:
                        down(x.next(-1))

                all_experts(pe, r, step)
                turn_h(Expert(r, QUADS - 1, 3))
                down(Expert(r, QUADS - 1, 3))

            rounds(pe, body)

        @block.scalar
        def _(act):
            def split(x, half):
                act.wait_ge(gu_in[x.b][half], 32 * x.turn2)
                act.wait_ge(gu_sum if half else half_used, x.it - 2 + 1 + LEAD)
                nc.scalar.activation(m.w_hi[:, 2 * x.b + half], m.gu_raw[:, 2 * x.b + half],
                                     ACT.Copy).then_inc(gu_hi, 1)

            def split_down(x):
                act.wait_ge(dn_in[x.b], 16 * x.turn2)
                act.wait_ge(y_sum, x.it - 2 + 1 + LEAD)
                nc.scalar.activation(m.dn_hi[:, x.b], m.dn_raw[:, x.b], ACT.Copy).then_inc(dn_hi, 1)

            def split_x(x):
                act.wait_ge(x_turned, x.it + 1 + LEAD4)
                nc.scalar.activation(m.xgT_hi[:, x.b].rearrange("p (c n) -> p c n", c=2), x_banks(),
                                     ACT.Copy).then_inc(x_hi, 1)

            def silu(x):
                act.wait_ge(gu_sum, x.it + 1 + LEAD)
                nc.scalar.activation(m.silu[0:CAP, x.b], ps[0:CAP, GU[x.b], 0:FF], ACT.Silu).then_inc(silu_out, 1)

            def split_hT(x):
                act.wait_ge(h_turned, x.it + 1)
                nc.scalar.activation(m.hT_hi[:, x.b], ps[:, HT, 0:2 * CAP], ACT.Copy).then_inc(hT_hi, 1)

            def scale_y(x):
                act.wait_ge(y_sum, x.it + 1 + LEAD)
                act.wait_ge(put[x.b], 16 * x.turn2)
                nc.scalar.activation(m.y[x.b][0:CAP].rearrange("p (c n) -> p c n", n=512), ps[0:CAP, Y:Y + 2],
                                     ACT.Copy,
                                     scale=m.found[0:CAP, bass.ds(x.e, 1), 1:2].rearrange("p o c -> p (o c)")) \
                  .then_inc(y_ready, 1)

            def body(r):
                split(Expert(r, 0, 0), 0)
                split(Expert(r, 0, 0), 1)
                split_x(Expert(r, 0, 0))

                def step(x, at=99):
                    if at != 0:
                        split_hT(x.next(-1))
                        split_down(x.next(-1))
                    if at != -1:
                        split(x.next(1), 0)
                        split(x.next(1), 1)
                    silu(x)
                    if at != -1:
                        split_x(x.next(1))
                    if at != 0:
                        scale_y(x.next(-1))

                all_experts(act, r, step)
                last = Expert(r, QUADS - 1, 3)
                split_hT(last)
                split_down(last)
                scale_y(last)

            act.sem_inc(y_ready, LEAD)
            rounds(act, body)

        @block.vector
        def _(dve):
            def one_hot(x):
                dve.wait_ge(located, x.it - 1 + LEAD)
                nc.vector.tensor_tensor(m.onehot[:, x.b],
                                        m.slots[:, bass.ds(x.r * CAP, CAP)].unsqueeze(1).to_broadcast([P, NT, CAP]),
                                        m.slot_of[:, :, bass.ds(x.e, 1)].to_broadcast([P, NT, CAP]),
                                        ALU.is_equal).then_inc(hot_ready, 1)

            def find(x):
                dve.wait_ge(located, x.it + 1 + LEAD)
                nc.vector.tensor_reduce(m.found[0:CAP, bass.ds(x.e, 1), :].rearrange("p o c -> p (o c)"),
                                        ps[0:CAP, TAGS, 0:6].rearrange("p (c x) -> p c x", x=3),
                                        AX, ALU.add).then_inc(found, 1)
                dve.wait_ge(found, x.it + 1 + LEAD)
                dve.wait_ge(x_turned, x.it - 4 + 1 + LEAD4)
                nc.vector.tensor_scalar(m.get_idx[x.q][0:CAP],
                                        m.found[0:CAP, bass.ds(x.e, 1), 0:1].rearrange("p o c -> p (o c)"),
                                        FAR, None, ALU.add).then_inc(get_ready, 1)

            def put_list(x):
                dve.wait_ge(put[x.b], 16 * x.turn2)
                nc.vector.tensor_scalar(m.put_idx[x.b][0:CAP],
                                        m.found[0:CAP, bass.ds(x.e, 1), 0:1].rearrange("p o c -> p (o c)"),
                                        FAR, None, ALU.add).then_inc(put_ready, 1)

            def split(x, half):
                dve.wait_ge(gu_hi, 2 * x.it + half + 1)
                nc.vector.tensor_tensor(m.w_lo[:, 2 * x.b + half], m.gu_raw[:, 2 * x.b + half],
                                        m.w_hi[:, 2 * x.b + half].bitcast(F32), ALU.subtract).then_inc(gu_lo, 1)

            def split_down(x):
                dve.wait_ge(dn_hi, x.it + 1)
                nc.vector.tensor_tensor(m.dn_lo[:, x.b], m.dn_raw[:, x.b], m.dn_hi[:, x.b].bitcast(F32),
                                        ALU.subtract).then_inc(dn_lo, 1)

            def split_x(x):
                dve.wait_ge(x_hi, x.it + 1)
                nc.vector.tensor_tensor(m.xgT_lo[:, x.b].rearrange("p (c n) -> p c n", c=2), x_banks(),
                                        m.xgT_hi[:, x.b].bitcast(F32).rearrange("p (c n) -> p c n", c=2),
                                        ALU.subtract).then_inc(x_lo, 1)

            def times_up(x):
                dve.wait_ge(silu_out, x.it + 1)
                nc.vector.tensor_tensor(m.h[0:CAP, x.b], m.silu[0:CAP, x.b], ps[0:CAP, GU[x.b], FF:2 * FF],
                                        ALU.mult).then_inc(h_ready, 1)

            def split_hT(x):
                dve.wait_ge(hT_hi, x.it + 1)
                nc.vector.tensor_tensor(m.hT_lo[:, x.b], ps[:, HT, 0:2 * CAP], m.hT_hi[:, x.b].bitcast(F32),
                                        ALU.subtract).then_inc(hT_lo, 1)

            def body(r):
                one_hot(Expert(r, 0, 0))
                for q in range(4):
                    one_hot(Expert(r, 0, q + 1))
                    find(Expert(r, 0, q))
                split(Expert(r, 0, 0), 0)
                split(Expert(r, 0, 0), 1)
                split_x(Expert(r, 0, 0))

                def step(x, at=99):
                    if at != 0:
                        split_hT(x.next(-1))
                        split_down(x.next(-1))
                    if at != -1:
                        split(x.next(1), 0)
                    if not -4 <= at <= -1:
                        find(x.next(4))
                    if at != -1:
                        split(x.next(1), 1)
                    times_up(x)
                    if at != -1:
                        split_x(x.next(1))
                    put_list(x)
                    if not -5 <= at <= -1:
                        one_hot(x.next(5))

                all_experts(dve, r, step)
                last = Expert(r, QUADS - 1, 3)
                split_hT(last)
                split_down(last)

            dve.sem_inc(found, LEAD)
            dve.sem_inc(x_lo, LEAD)
            dve.sem_inc(h_ready, LEAD)
            dve.sem_inc(gu_lo, 2 * LEAD)
            dve.sem_inc(dn_lo, LEAD)
            dve.sem_inc(hT_lo, LEAD)
            dve.sem_inc(located, LEAD)
            rounds(dve, body)

        @block.gpsimd
        def _(pool):
            last_token = pool.to_reg(SEQ - 1)
            for b in range(2):
                nc.gpsimd.dma_start(m.y[b][0:1], h1[b:b + 1]).then_inc(put[b], 16)
            for q in range(4):
                nc.gpsimd.memset(m.xg[q][:], 0.0).then_inc(cleared, 1)

            def gather(x):
                pool.wait_ge(get_ready, x.it + 1)
                pool.wait_ge(x_turned, x.it - 4 + 1 + LEAD4)
                pool.sem_inc(passed, 1)
                pool.wait_ge(cleared, 4)
                nc.gpsimd.indirect_dma_start(out=m.xg[x.q][0:CAP], out_offset=None, in_=h1,
                                             in_offset=bass.IndirectOffsetOnAxis(ap=m.get_idx[x.q][0:CAP], axis=0),
                                             bounds_check=last_token, oob_is_err=False).then_inc(got[x.q], 16)

            def scatter(x):
                pool.wait_ge(y_ready, x.it + 1 + LEAD)
                pool.wait_ge(put_ready, x.it + 1)
                pool.wait_ge(put[x.b], 16 * x.turn2)
                pool.sem_inc(passed, 1)
                pool.wait_ge(cleared, 4)
                nc.gpsimd.indirect_dma_start(out=(acc_dram, acc_odd_dram)[x.b],
                                             out_offset=bass.IndirectOffsetOnAxis(ap=m.put_idx[x.b][0:CAP], axis=0),
                                             in_=m.y[x.b][0:CAP], in_offset=None, bounds_check=last_token,
                                             oob_is_err=False, compute_op=ALU.add).then_inc(put[x.b], 16)

            def body(r):
                for q in range(4):
                    gather(Expert(r, 0, q))

                def step(x, at=99):
                    if not -4 <= at <= -1:
                        gather(x.next(4))
                    if at != 0:
                        scatter(x.next(-1))

                all_experts(pool, r, step)
                scatter(Expert(r, QUADS - 1, 3))
                for b in range(2):
                    pool.wait_ge(put[b], 16 * ((r + 1) * (NE // 2) + 1))

            rounds(pool, body)


def embedding_block(nc, m, ps, a, acc_dram, acc_odd_dram):
    MAIN, TURN, PT = (4, 5), (0, 2), 6
    with ExitStack() as ctx:
        def sem(name):
            return ctx.enter_context(nc.semaphore(f"ple_{name}"))

        w = a["ple_w_gate"][0].rearrange("(p k) n -> p k n", p=P)
        ring = WeightRing(nc, m, ctx, "ple", [w[:, 4 * half:4 * half + 4, c * 512:(c + 1) * 512]
                                              for c in range(2) for half in range(2)])
        rows_in = [sem(f"rows_in{t}") for t in range(NT)]
        p_in, pw_in, p_turned, pT_ready, p_sum, p_out = (sem("p_in"), sem("pw_in"), sem("p_turned"),
                                                         sem("pT_ready"), sem("p_sum"), sem("p_out"))
        turned, hi_done, lo_done, summed, gate_ready, added, chain = (
            sem("turned"), sem("hi_done"), sem("lo_done"), sem("summed"), sem("gate_ready"), sem("added"), sem("chain"))
        row_sum = sem("row_sum")
        block = ctx.enter_context(nc.Block())

        @block.sync
        def _(sp):
            for t in range(NT):
                sp.dma_start(m.x[:, t], acc_dram[t * P:(t + 1) * P, :]).then_inc(rows_in[t], 16)
                sp.dma_start(m.x_odd[:, t], acc_odd_dram[t * P:(t + 1) * P, :]).then_inc(rows_in[t], 16)
            sp.dma_start(m.p[:], a["p"][0, 0].rearrange("(t p) d -> p t d", p=P)).then_inc(p_in, 16)
            sp.dma_start(m.p_w[:], a["ple_w_proj"][0].rearrange("(p j) n -> p (j n)", p=P)).then_inc(pw_in, 16)
            for i in range(4):
                ring.load(sp, i)

        @block.tensor
        def _(pe):
            for t in range(NT):
                pe.wait_ge(row_sum, t + 1)
                if t >= 2:
                    pe.wait_ge(lo_done, t - 1)
                for k in range(KD):
                    last = nc.tensor.transpose(ps[:, TURN[t % 2] + k // 4, (k % 4) * P:(k % 4 + 1) * P],
                                               m.x[:, t, k::KD], m.ident[:])
                last.then_inc(turned, 1)
            pe.wait_ge(p_in, 16)
            for t in range(NT):
                if t:
                    pe.wait_ge(pT_ready, t)
                for j in range(2):
                    last = nc.tensor.transpose(ps[:, PT, j * P:(j + 1) * P], m.p[:, t, j::2], m.ident[:])
                last.then_inc(p_turned, 1)
            pe.wait_ge(pw_in, 16)
            pe.wait_ge(pT_ready, NT)
            for u in range(2 * NT):
                c, t = divmod(u, NT)
                if u >= 2:
                    pe.wait_ge(p_out, u - 1)
                for j in range(2):
                    last = nc.tensor.matmul(ps[:, MAIN[u % 2]], m.pT[:, j, t * P:(t + 1) * P],
                                            m.p_w[:, j * D + c * 512:j * D + (c + 1) * 512],
                                            start=(j == 0), stop=(j == 1))
                last.then_inc(p_sum, 1)
            for u in range(2 * NT):
                c, t = divmod(u, NT)
                if u < 2:
                    pe.wait_ge(p_out, 2 * NT - 1 + u)
                else:
                    pe.wait_ge(gate_ready, u - 1)
                if u < NT:
                    pe.wait_ge(lo_done, t + 1)
                for kk in range(KD):
                    i = 2 * c + kk // 4
                    if t == 0 and kk % 4 == 0:
                        ring.ready(pe, i)
                    last = product3(nc, ps[:, MAIN[u % 2]], m.act_hi[:, kk, t * P:(t + 1) * P],
                                    m.act_lo[:, kk, t * P:(t + 1) * P], ring.hi(i)[:, kk % 4],
                                    ring.lo(i)[:, kk % 4], kk == 0, kk == KD - 1)
                last.then_inc(summed, 1)

        @block.scalar
        def _(act):
            for t in range(NT):
                act.wait_ge(turned, t + 1)
                b = TURN[t % 2]
                nc.scalar.activation(m.act_hi[:, :, t * P:(t + 1) * P],
                                     ps[:, b:b + 2].rearrange("p b (k n) -> p (b k) n", n=P),
                                     ACT.Copy).then_inc(hi_done, 1)
            for t in range(NT):
                act.wait_ge(p_turned, t + 1)
                nc.scalar.activation(m.pT[:, :, t * P:(t + 1) * P],
                                     ps[:, PT, 0:2 * P].rearrange("p (j n) -> p j n", n=P),
                                     ACT.Copy).then_inc(pT_ready, 1)
            for i in range(4):
                ring.split_hi(act, i)
            for u in range(2 * NT):
                act.wait_ge(summed, u + 1)
                if u >= 2:
                    act.wait_ge(added, u - 1)
                nc.scalar.activation(m.gate[:, u % 2], ps[:, MAIN[u % 2]], ACT.Sigmoid).then_inc(gate_ready, 1)

        @block.vector
        def _(dve):
            for t in range(NT):
                dve.wait_ge(rows_in[t], 32)
                nc.vector.tensor_tensor(m.x[:, t], m.x[:, t], m.x_odd[:, t], ALU.add).then_inc(row_sum, 1)
            for t in range(NT):
                dve.wait_ge(hi_done, t + 1)
                b = TURN[t % 2]
                nc.vector.tensor_tensor(m.act_lo[:, :, t * P:(t + 1) * P],
                                        ps[:, b:b + 2].rearrange("p b (k n) -> p (b k) n", n=P),
                                        m.act_hi[:, :, t * P:(t + 1) * P].bitcast(F32),
                                        ALU.subtract).then_inc(lo_done, 1)
            for i in range(2):
                ring.split_lo(dve, i)
            for u in range(2 * NT):
                c, t = divmod(u, NT)
                dve.wait_ge(p_sum, u + 1)
                nc.vector.tensor_copy(m.pp[:, t, c * 512:(c + 1) * 512], ps[:, MAIN[u % 2]]).then_inc(p_out, 1)
            for i in range(2, 4):
                ring.split_lo(dve, i)
            for u in range(2 * NT):
                c, t = divmod(u, NT)
                cols = slice(c * 512, (c + 1) * 512)
                dve.wait_ge(gate_ready, u + 1)
                nc.vector.tensor_tensor(m.gate[:, u % 2], m.gate[:, u % 2], m.pp[:, t, cols],
                                        ALU.mult).then_inc(chain, 1)
                dve.wait_ge(chain, u + 1)
                nc.vector.tensor_tensor(m.x[:, t, cols], m.x[:, t, cols], m.gate[:, u % 2],
                                        ALU.add).then_inc(added, 1)


def encoder_block(nc, a, out, CAP=SLOTS):
    h0 = nc.dram_tensor("h0_rows", [SEQ, D], F32, kind="Internal").ap()
    h1 = nc.dram_tensor("h1_rows", [SEQ, D], F32, kind="Internal").ap()
    acc_dram = nc.dram_tensor("residual_rows", [SEQ, D], F32, kind="Internal").ap()
    acc_odd_dram = nc.dram_tensor("odd_rows", [SEQ, D], F32, kind="Internal").ap()
    m = Memory(nc, (nc.sbuf_base + 31) // 32 * 32, CAP)
    with ExitStack() as ctx:
        ps = ctx.enter_context(nc.psum_tensor("ps", [P, 8, 512], F32))
        norm = NormSemaphores(nc, ctx)
        make_constants(nc, m)
        norm_block(nc, m, ps, norm, a["ln_in_g"], a["ln_in_b"], source=a["x"][0], store=h0)
        mix_block(nc, m, ps, a)
        out_block(nc, m, ps, a, h0)
        norm_block(nc, m, ps, norm, a["ln1_g"][0], a["ln1_b"][0], store=h1)
        routing_block(nc, m, ps, a, acc_dram, acc_odd_dram)
        experts_block(nc, m, ps, a, h1, acc_dram, acc_odd_dram, CAP)
        embedding_block(nc, m, ps, a, acc_dram, acc_odd_dram)
        norm_block(nc, m, ps, norm, a["ln2_g"][0], a["ln2_b"][0], store=out[0], output=True)


_INS = ["x", "p", "ln_in_g", "ln_in_b", "w_in", "sg_ln_g", "sg_ln_b", "sg_w_s", "sg_b_s", "w_branch_a", "w_branch_b",
        "w_out", "ln1_g", "ln1_b", "router_w", "router_bias", "moe_w_gate", "moe_w_up", "moe_w_down", "sh_w_gate",
        "sh_w_up", "sh_w_down", "ple_w_proj", "ple_w_gate", "ln2_g", "ln2_b"]


def kernel(**inputs):
    import numpy as _np
    import concourse.bacc as _bacc
    from concourse import mybir as _mybir
    from concourse.bass_utils import run_bass_kernel_spmd as _run

    nc = _bacc.Bacc("TRN2", target_bir_lowering=False, num_devices=1)
    arrays, args = {}, {}
    for name in _INS:
        v = _np.ascontiguousarray(inputs[name])
        arrays[f"in_{name}"] = v
        args[name] = nc.dram_tensor(f"in_{name}", v.shape, _mybir.dt.from_np(v.dtype), kind="ExternalInput").ap()
    out = nc.dram_tensor("out_h", [1, SEQ, D], F32, kind="ExternalOutput").ap()
    encoder_block(nc, args, out)
    r = _run(nc, [arrays], core_ids=[0])
    return r.results[0]["out_h"]
```

```python
from contextlib import ExitStack

import concourse.bass as bass
from concourse import mybir

P = 128
D = 1024
SEQ = 512
NT = SEQ // P
KD = D // P
SG = 512
SGG = 4
HEADS = 8
HD = 64
NE = 64
NGRP = 8
FF = 256
PLE = 256
LN_EPS = 1e-5
ALPHA = 2.0 ** 0.25
ROUTED_SCALE = 2.5
SLOTS = 96
FAR = 4096.0
HC = 2048
NSPLIT = 4
NRAW = 2
DENSE_PIECES = 26

F32 = mybir.dt.float32
F32R = mybir.dt.float32r
BF16 = mybir.dt.bfloat16
U32 = mybir.dt.uint32
I32 = mybir.dt.int32
ALU = mybir.AluOpType
ACT = mybir.ActivationFunctionType
AX = mybir.AxisListType.X
KB = 1024


class Memory:

    def __init__(self, nc, base, cap):
        def at(name, shape, dtype, kib):
            return nc.alloc_sbuf_tensor_at(name, shape, dtype, offset=base + int(kib * KB))

        self.raw = at("raw", [P, NRAW, HC], F32, 0)
        self.w_hi = at("w_hi", [P, NSPLIT, HC], F32R, 16)
        self.w_lo = at("w_lo", [P, NSPLIT, HC], F32R, 48)
        self.act_hi = at("act_hi", [P, KD, SEQ], F32R, 80)
        self.act_lo = at("act_lo", [P, KD, SEQ], F32R, 96)
        self.qT = at("qT", [P, 4, SEQ], F32, 112)
        self.kT = at("kT", [P, 4, SEQ], F32, 120)
        self.ybT_hi = at("ybT_hi", [P, 4, SEQ], F32R, 112)
        self.ybT_lo = at("ybT_lo", [P, 4, SEQ], F32R, 120)
        self.vsb = at("vsb", [P, NT, 512], F32, 128)
        self.merged = at("merged", [P, NT, D], F32, 136)
        self.yaT_hi = at("yaT_hi", [P, 4, SEQ], F32R, 152)
        self.yaT_lo = at("yaT_lo", [P, 4, SEQ], F32R, 160)
        self.x = at("x_rows", [P, NT, D], F32, 152)
        self.yb = at("yb", [P, NT, 512], F32, 168)
        self.ln_g = at("ln_g", [P, D], F32, 168)
        self.ln_b = at("ln_b", [P, D], F32, 172)
        self.sig_neg = at("sig_neg", [P, 2, 512], F32, 176)
        self.sig_pos = at("sig_pos", [P, 2, 512], F32, 180)
        self.stick = at("stick", [P, 2, 520], F32, 184)
        self.aT = at("aT", [P, 2, 512], F32, 189)
        self.gate = at("gate", [P, 2, 512], F32, 193)
        self.sg_wT = at("sg_wT", [P, SGG, P], F32, 197)
        self.sg_b = at("sg_b", [P, SGG], F32, 199)
        self.sg_w = at("sg_w", [P, SGG, P], F32, 189)
        self.sg_g = at("sg_g", [P, SG], F32, 176)
        self.sg_bb = at("sg_bb", [P, SG], F32, 178)
        self.ident = at("ident", [P, P], F32, 201)
        self.ident_bf = at("ident_bf", [P, P], BF16, 201.5)
        self.future_bf = at("future_bf", [P, P], BF16, 201.75)
        self.earlier_bf = at("earlier_bf", [P, P], BF16, 202)
        self.ones_bf = at("ones_bf", [P, P], BF16, 202.25)
        self.lower_grp = at("lower_grp", [P, NGRP, NGRP], F32, 202.5)
        self.slots = at("slots", [P, SEQ + P], F32, 202.75)
        self.stats = at("stats", [P, NT, 2, 6], F32, 205.25)
        self.mv = at("mv", [P, NT, 2], F32, 205.5)
        self.rstd = at("rstd", [P, NT, 1], F32, 205.625)
        self.nmr = at("nmr", [P, NT, 1], F32, 205.75)
        self.eps = at("eps", [P, 1], F32, 206.125)
        self.peak = at("peak", [P, 1], F32, 205.875)
        self.peak_i = at("peak_i", [P, 1], I32, 206)
        self.sh_down = at("sh_down", [P, HC], F32, 136)
        self.sh_h = at("sh_h", [P, NT, FF], F32, 168)
        self.sh_hT = at("sh_hT", [P, 2, SEQ], F32, 172)
        self.zero_rows = at("zero_rows", [P, D], F32, 128)
        self.acc = at("acc_rows", [P, 2, D], F32, 144)
        self.router = at("router", [P, KD, NE], F32, 184)
        self.r_hi = at("r_hi", [P, KD, NE], F32R, 186)
        self.r_lo = at("r_lo", [P, KD, NE], F32R, 188)
        self.r_bias = at("r_bias", [P, NE], F32, 190)
        self.score = at("score", [P, NT, NE], F32, 190.25)
        self.sel = at("sel", [P, NT, NE], F32, 191.25)
        self.top = at("top", [P, NT, NGRP, 8], F32, 192.25)
        self.grp = at("grp", [P, NT, NGRP], F32, 193.25)
        self.beats = at("beats", [P, NT, NGRP, NGRP], F32, 193.5)
        self.ties = at("ties", [P, NT, NGRP, NGRP], F32, 194.5)
        self.rank = at("rank", [P, NT, NGRP], F32, 195.5)
        self.top8 = at("top8", [P, NT, 8], F32, 195.75)
        self.rest = at("rest", [P, NT, NE], F32, 196)
        self.pick_bf = at("pick_bf", [P, NT, NE], BF16, 197)
        self.den = at("den", [P, NT], F32, 197.5)
        self.slot_of = at("slot_of", [P, NT, NE], F32, 176)
        self.tags = at("tags", [P, NT, NE, 6], BF16, 177)
        self.found = at("found", [P, NE, 2], F32, 180)
        self.get_idx = [at(f"get_idx{i}", [P, 1], U32, 180.5 + i * 0.0625) for i in range(4)]
        self.put_idx = [at(f"put_idx{i}", [P, 1], U32, 180.75 + i * 0.0625) for i in range(2)]
        self.gu_raw = at("gu_raw", [P, 4, HC], F32, 112)
        self.dn_raw = at("dn_raw", [P, 2, HC], F32, 184)
        self.dn_hi = at("dn_hi", [P, 2, HC], F32R, 0)
        self.dn_lo = at("dn_lo", [P, 2, HC], F32R, 160)
        self.xg = [at(f"xg{i}", [P, D], F32, 144 + 4 * i) for i in range(4)]
        self.xgT_hi = at("xgT_hi", [P, 2, KD * cap], F32R, 80)
        self.xgT_lo = at("xgT_lo", [P, 2, KD * cap], F32R, 88)
        self.silu = at("silu", [P, 2, FF], F32, 96)
        self.h = at("h_ff", [P, 2, FF], F32, 98)
        self.hT_hi = at("hT_hi", [P, 2, 2 * cap], F32R, 100)
        self.hT_lo = at("hT_lo", [P, 2, 2 * cap], F32R, 181)
        self.y = [at(f"y{i}", [P, D], F32, 102 + 4 * i) for i in range(2)]
        self.onehot = at("onehot", [P, 2, NT, cap], BF16, 110)
        self.p = at("p_rows", [P, NT, PLE], F32, 112)
        self.pT = at("pT", [P, 2, SEQ], F32, 116)
        self.p_w = at("p_w", [P, HC], F32, 120)
        self.gate_out = at("gate_out", [P, 2, 512], F32, 112)
        self.pp = at("pp", [P, NT, D], F32, 0)
        self.x_odd = [at(f"x_odd{i}", [P, 2, D], F32, kib) for i, kib in enumerate((144, 176))]
        self.ple_raw = [at(f"ple_raw{i}", [P, HC], F32, kib)[:] for i, kib in enumerate((128, 136, 184, 192))]


def make_constants(nc, m):
    with nc.semaphore("base_set") as base_set, nc.Block() as block:

        @block.gpsimd
        def _(pool):
            nc.gpsimd.memset(m.ident[:], 0.0).then_inc(base_set, 1)
            nc.gpsimd.memset(m.ident_bf[:], 0.0).then_inc(base_set, 1)
            nc.gpsimd.memset(m.future_bf[:], 0.0).then_inc(base_set, 1)
            nc.gpsimd.memset(m.earlier_bf[:], 1.0).then_inc(base_set, 1)
            nc.gpsimd.memset(m.ones_bf[:], 1.0).then_inc(base_set, 1)
            nc.gpsimd.memset(m.lower_grp[:], 1.0).then_inc(base_set, 1)
            nc.gpsimd.memset(m.eps[:], LN_EPS)
            pool.wait_ge(base_set, 6)
            for eye in (m.ident, m.ident_bf):
                nc.gpsimd.affine_select(out=eye[:], in_=eye[:], compare_op=ALU.not_equal, fill=1.0, base=0,
                                        pattern=[[-1, P]], channel_multiplier=1)
            nc.gpsimd.affine_select(out=m.future_bf[:], in_=m.future_bf[:], compare_op=ALU.is_gt, fill=-1e30,
                                    base=0, pattern=[[-1, P]], channel_multiplier=1)
            nc.gpsimd.affine_select(out=m.earlier_bf[:], in_=m.earlier_bf[:], compare_op=ALU.is_gt, fill=0.0,
                                    base=0, pattern=[[1, P]], channel_multiplier=-1)
            nc.gpsimd.affine_select(out=m.lower_grp[:], in_=m.lower_grp[:], compare_op=ALU.is_gt, fill=0.0,
                                    base=0, pattern=[[1, NGRP], [-1, NGRP]], channel_multiplier=0)
            nc.gpsimd.iota(m.slots[:], pattern=[[1, SEQ + P]], base=0, channel_multiplier=0,
                           allow_small_or_imprecise_dtypes=True)


def deviation(nc, m, t):
    return nc.scalar.activation(m.rstd[:, t], m.mv[:, t, 1:2], ACT.Sqrt, bias=m.eps[:])


def scale_and_shift(nc, m, chained, t):
    chained(nc.vector.reciprocal(m.rstd[:, t], m.rstd[:, t]))
    return nc.vector.scalar_tensor_tensor(out=m.nmr[:, t], in0=m.mv[:, t, 0:1], scalar=-1.0, in1=m.rstd[:, t],
                                          op0=ALU.mult, op1=ALU.mult)


class NormSemaphores:

    def __init__(self, nc, ctx):
        def sem(name):
            return ctx.enter_context(nc.semaphore(f"norm_{name}"))

        self.rows_in = [sem(f"rows_in{t}") for t in range(NT)]
        self.affine_in, self.rows_out = sem("affine_in"), sem("rows_out")
        self.moments, self.rooted, self.stats_done = sem("moments"), sem("rooted"), sem("stats_done")
        self.scaled, self.gained, self.normed, self.turned = sem("scaled"), sem("gained"), sem("normed"), sem("turned")
        self.hi_done, self.lo_done, self.chain = sem("hi_done"), sem("lo_done"), sem("chain")
        self.norms = 0
        self.links = 0


class RowNorm:

    def __init__(self, nc, m, ps, s, banks=(0,)):
        self.nc, self.m, self.ps, self.s, self.banks = nc, m, ps, s, banks
        self.before = s.norms * NT
        self.affine_count = 32 * (s.norms + 1)
        s.norms += 1

    def load_affine(self, sp, gain, bias):
        sp.dma_start(self.m.ln_g[:], gain.partition_broadcast(P)).then_inc(self.s.affine_in, 16)
        sp.dma_start(self.m.ln_b[:], bias.partition_broadcast(P)).then_inc(self.s.affine_in, 16)

    def store(self, sp, t, rows):
        sp.wait_ge(self.s.normed, self.before + t + 1)
        sp.dma_start(rows[t * P:(t + 1) * P, :], self.m.x[:, t]).then_inc(self.s.rows_out, 16)

    def stored(self, sp):
        sp.wait_ge(self.s.rows_out, 16 * (self.before + NT))

    def chained(self, dve, ins):
        self.s.links += 1
        ins.then_inc(self.s.chain, 1)
        dve.wait_ge(self.s.chain, self.s.links)

    def statistics(self, dve, t):
        nc, m = self.nc, self.m
        nc.vector.bn_stats(m.stats[:, t, 0], m.x[:, t, 0:512])
        self.chained(dve, nc.vector.bn_stats(m.stats[:, t, 1], m.x[:, t, 512:D]))
        nc.vector.bn_aggr(m.mv[:, t], m.stats[:, t]).then_inc(self.s.moments, 1)

    def deviate(self, act, t):
        act.wait_ge(self.s.moments, self.before + t + 1)
        deviation(self.nc, self.m, t).then_inc(self.s.rooted, 1)

    def finish(self, dve, t):
        dve.wait_ge(self.s.rooted, self.before + t + 1)
        scale_and_shift(self.nc, self.m, lambda ins: self.chained(dve, ins), t).then_inc(self.s.stats_done, 1)

    def centre(self, act, t):
        m = self.m
        act.wait_ge(self.s.stats_done, self.before + t + 1)
        self.nc.scalar.activation(m.x[:, t], m.x[:, t], ACT.Identity, bias=m.nmr[:, t],
                                  scale=m.rstd[:, t]).then_inc(self.s.scaled, 1)

    def gain(self, dve, t):
        m = self.m
        if t == 0:
            dve.wait_ge(self.s.affine_in, self.affine_count)
        dve.wait_ge(self.s.scaled, self.before + t + 1)
        self.nc.vector.tensor_tensor(m.x[:, t], m.x[:, t], m.ln_g[:], ALU.mult).then_inc(self.s.gained, 1)

    def shift(self, eng, t, unit=None):
        m = self.m
        if t == 0:
            eng.wait_ge(self.s.affine_in, self.affine_count)
        eng.wait_ge(self.s.gained, self.before + t + 1)
        (unit or self.nc.gpsimd).tensor_tensor(m.x[:, t], m.x[:, t], m.ln_b[:], ALU.add).then_inc(self.s.normed, 1)

    def view(self, t):
        b = self.banks[t % len(self.banks)]
        return self.ps[:, b:b + 2].rearrange("p b (k n) -> p (b k) n", n=P)

    def turn(self, pe, t):
        b = self.banks[t % len(self.banks)]
        pe.wait_ge(self.s.normed, self.before + t + 1)
        if t >= len(self.banks):
            pe.wait_ge(self.s.lo_done, self.before + t + 1 - len(self.banks))
        for k in range(KD):
            last = self.nc.tensor.transpose(self.ps[:, b + k // 4, (k % 4) * P:(k % 4 + 1) * P],
                                            self.m.x[:, t, k::KD], self.m.ident[:])
        last.then_inc(self.s.turned, 1)

    def high_part(self, act, t):
        act.wait_ge(self.s.turned, self.before + t + 1)
        self.nc.scalar.activation(self.m.act_hi[:, :, t * P:(t + 1) * P], self.view(t),
                                  ACT.Copy).then_inc(self.s.hi_done, 1)

    def low_part(self, dve, t):
        m = self.m
        dve.wait_ge(self.s.hi_done, self.before + t + 1)
        self.nc.vector.tensor_tensor(m.act_lo[:, :, t * P:(t + 1) * P], self.view(t),
                                     m.act_hi[:, :, t * P:(t + 1) * P].bitcast(F32),
                                     ALU.subtract).then_inc(self.s.lo_done, 1)


def input_norm_block(nc, m, ps, s, a, h0, ring):
    norm = RowNorm(nc, m, ps, s, banks=(0, 2))
    with nc.Block() as block:

        @block.sync
        def _(sp):
            sp.dma_start(m.x[:, 0], a["x"][0][0:P, :]).then_inc(s.rows_in[0], 16)
            norm.load_affine(sp, a["ln_in_g"], a["ln_in_b"])
            for t in range(1, NT):
                sp.dma_start(m.x[:, t], a["x"][0][t * P:(t + 1) * P, :]).then_inc(s.rows_in[t], 16)
            ring.load(sp, 0)
            ring.load(sp, 1)
            for t in range(NT):
                norm.store(sp, t, h0)
                if t >= 2:
                    ring.load(sp, t)
            norm.stored(sp)

        @block.vector
        def _(dve):
            for t in range(NT + 2):
                if t < NT:
                    dve.wait_ge(s.rows_in[t], 16)
                    norm.statistics(dve, t)
                    norm.finish(dve, t)
                if 1 <= t <= NT:
                    norm.gain(dve, t - 1)
                if t >= 2:
                    norm.low_part(dve, t - 2)

        @block.scalar
        def _(act):
            for t in range(NT + 1):
                if t < NT:
                    norm.deviate(act, t)
                    norm.centre(act, t)
                if t >= 1:
                    norm.high_part(act, t - 1)
                if t in (1, 2):
                    ring.split_hi(act, t - 1)

        @block.gpsimd
        def _(pool):
            for t in range(NT):
                norm.shift(pool, t)
                if t in (1, 2):
                    ring.split_lo(pool, t - 1, nc.gpsimd)

        @block.tensor
        def _(pe):
            for t in range(NT):
                norm.turn(pe, t)


def dense_pieces(a):
    def columns(w, k, c, half):
        rows = k // 2
        return w.rearrange("(p k) n -> p k n", p=P)[:, half * rows:(half + 1) * rows, c * 512:(c + 1) * 512]

    w_in, w_a, w_b, w_out = a["w_in"][0], a["w_branch_a"][0], a["w_branch_b"][0], a["w_out"][0]
    pieces = []
    for c in range(5):
        pieces += [columns(w_in, KD, c, 0), columns(w_in, KD, c, 1)]
    for c, w in ((0, w_a), (1, w_a), (2, w_b), (3, w_b)):
        pieces += [columns(w_in, KD, 5 + c, 0), columns(w_in, KD, 5 + c, 1)]
        pieces.append(w.rearrange("(p k) n -> p k n", p=P)[:, :, (c % 2) * 512:(c % 2 + 1) * 512])
    for c in range(2):
        pieces += [columns(w_out, KD, c, 0), columns(w_out, KD, c, 1)]
    assert len(pieces) == DENSE_PIECES
    for half in range(2):
        pieces.append(tuple(a[name][0].rearrange("(p k) n -> p k n", p=P)[:, 4 * half:4 * half + 4]
                            for name in ("sh_w_gate", "sh_w_up")))
    return pieces


class WeightRing:

    def __init__(self, nc, m, ctx, tag, pieces, raw):
        self.nc, self.m, self.pieces, self.raw = nc, m, pieces, raw
        self.slots = len(raw)
        self.loaded = [ctx.enter_context(nc.semaphore(f"{tag}_loaded{i}")) for i in range(self.slots)]
        self.hi_split = ctx.enter_context(nc.semaphore(f"{tag}_hi_split"))
        self.lo_split = ctx.enter_context(nc.semaphore(f"{tag}_lo_split"))
        self.freed = {}

    def load(self, sp, i):
        if i >= self.slots:
            sp.wait_ge(self.lo_split, i - self.slots + 1)
        dst = self.raw[i % self.slots].rearrange("p (k n) -> p k n", n=512)
        src = self.pieces[i]
        if not isinstance(src, tuple):
            sp.dma_start(dst, src).then_inc(self.loaded[i % self.slots], 16)
        else:
            sp.dma_start(dst[:, :, 0:FF], src[0]).then_inc(self.loaded[i % self.slots], 16)
            sp.dma_start(dst[:, :, FF:512], src[1]).then_inc(self.loaded[i % self.slots], 16)

    def loads_of(self, i):
        return 16 * sum(1 + isinstance(self.pieces[j], tuple) for j in range(i % self.slots, i + 1, self.slots))

    def split_hi(self, act, i):
        act.wait_ge(self.loaded[i % self.slots], self.loads_of(i))
        if i >= NSPLIT:
            act.wait_ge(*self.freed[i - NSPLIT])
        self.nc.scalar.activation(self.m.w_hi[:, i % NSPLIT], self.raw[i % self.slots],
                                  ACT.Copy).then_inc(self.hi_split, 1)

    def split_lo(self, eng, i, unit=None):
        eng.wait_ge(self.hi_split, i + 1)
        (unit or self.nc.vector).tensor_tensor(self.m.w_lo[:, i % NSPLIT], self.raw[i % self.slots],
                                     self.m.w_hi[:, i % NSPLIT].bitcast(F32),
                                     ALU.subtract).then_inc(self.lo_split, 1)

    def ready(self, pe, i):
        pe.wait_ge(self.lo_split, i + 1)

    def hi(self, i):
        return self.m.w_hi[:, i % NSPLIT].rearrange("p (k n) -> p k n", n=512)

    def lo(self, i):
        return self.m.w_lo[:, i % NSPLIT].rearrange("p (k n) -> p k n", n=512)


def product3(nc, out, x_hi, x_lo, w_hi, w_lo, first, last):
    nc.tensor.matmul(out, x_hi, w_hi, start=first, stop=False)
    nc.tensor.matmul(out, x_hi, w_lo, start=False, stop=False)
    return nc.tensor.matmul(out, x_lo, w_hi, start=False, stop=last)


def mix_block(nc, m, ps, a, ring):
    MAIN, SIDE, Z, TURN, YB = (0, 1), 2, (3, 4), (5, 6), 7
    NA = NT * HEADS
    with ExitStack() as ctx:
        def sem(name):
            return ctx.enter_context(nc.semaphore(f"mix_{name}"))

        half_used, projected, gelu_out, copied = sem("half_used"), sem("projected"), sem("gelu_out"), sem("copied")
        small_in = sem("small_in")
        sg_turned, sg_w_ready = sem("sg_turned"), sem("sg_w_ready")
        v_moments, v_rooted = sem("v_moments"), sem("v_rooted")
        v_stats, v_scaled, v_normed = sem("v_stats"), sem("v_scaled"), sem("v_normed")
        gated, ya_ready = sem("gated"), sem("ya_ready")
        ya_turned, ya_hi, ya_lo = sem("ya_turned"), sem("ya_hi"), sem("ya_lo")
        z_ready, sig_ready, a_ready = sem("z_ready"), sem("sig_ready"), sem("a_ready")
        a_turned, aT_ready, av_done = sem("a_turned"), sem("aT_ready"), sem("av_done")
        yb_sum, yb_ready = sem("yb_sum"), sem("yb_ready")
        yb_turned, yb_hi, yb_lo = sem("yb_turned"), sem("yb_hi"), sem("yb_lo")
        gate_sum, branch_sum, gate_ready, merged = sem("gate_sum"), sem("branch_sum"), sem("gate_ready"), sem("merged")
        chain = sem("chain")
        for c in range(5):
            ring.freed[2 * c], ring.freed[2 * c + 1] = (half_used, c + 1), (projected, 4 * c + 4)
        for j in range(4):
            ring.freed[10 + 3 * j] = (half_used, 5 + j + 1)
            ring.freed[11 + 3 * j], ring.freed[12 + 3 * j] = (gate_sum, 4 * j + 4), (branch_sum, 4 * j + 4)
        block = ctx.enter_context(nc.Block())

        SPLIT_AFTER_STEP = {13: (14,), 15: (15,), 16: (16,), 29: (17,), 31: (18, 19)}
        SPLIT_AFTER_GATE = {10: (20,), 11: (21,), 12: (22,)}

        def width(s):
            return (s // HEADS + 1) * P

        @block.sync
        def _(sp):
            sp.dma_start(m.sg_w[:], a["sg_w_s"][0].rearrange("g i j -> i g j")).then_inc(small_in, 16)
            sp.dma_start(m.sg_g[:], a["sg_ln_g"][0].partition_broadcast(P)).then_inc(small_in, 16)
            sp.dma_start(m.sg_bb[:], a["sg_ln_b"][0].partition_broadcast(P)).then_inc(small_in, 16)
            sp.dma_start(m.sg_b[:], a["sg_b_s"][0].rearrange("g i -> i g"),
                         allow_slow_non_contiguous=True).then_inc(small_in, 16)
            for i in range(4, DENSE_PIECES - 2):
                ring.load(sp, i)

        @block.tensor
        def _(pe):
            def unit_start(u):
                if u - 2 >= 8:
                    pe.wait_ge(copied, u - 2 - 8 + 1)
                elif u - 2 >= 0:
                    pe.wait_ge(gelu_out, u - 2 + 1)

            def rows_unit(u, c, t):
                unit_start(u)
                for half in range(2):
                    i = 2 * c + half
                    if t == 0:
                        ring.ready(pe, i)
                    for k in range(4):
                        kk = 4 * half + k
                        last = product3(nc, ps[:, MAIN[u % 2]], m.act_hi[:, kk, t * P:(t + 1) * P],
                                        m.act_lo[:, kk, t * P:(t + 1) * P], ring.hi(i)[:, k], ring.lo(i)[:, k],
                                        kk == 0, kk == KD - 1)
                    if half == 0 and t == NT - 1:
                        last.then_inc(half_used, 1)
                last.then_inc(projected, 1)

            def features_unit(u, c, f):
                unit_start(u)
                for half in range(2):
                    i = 2 * c + half
                    if f == 0:
                        ring.ready(pe, i)
                    cols = slice(f * P, (f + 1) * P)
                    for k in range(4):
                        kk = 4 * half + k
                        last = product3(nc, ps[:, MAIN[u % 2]], ring.hi(i)[:, k, cols], ring.lo(i)[:, k, cols],
                                        m.act_hi[:, kk], m.act_lo[:, kk], kk == 0, kk == KD - 1)
                    if half == 0 and f == 3:
                        last.then_inc(half_used, 1)
                last.then_inc(projected, 1)

            for t in range(NT):
                rows_unit(t, 0, t)
            pe.wait_ge(small_in, 64)
            for g in range(SGG):
                last = nc.tensor.transpose(ps[:, YB, g * P:(g + 1) * P], m.sg_w[:, g], m.ident[:])
            last.then_inc(sg_turned, 1)
            for t in range(NT):
                rows_unit(4 + t, 1, t)
            for f in range(4):
                features_unit(8 + f, 2, f)
            pe.wait_ge(sg_w_ready, 1)
            for t in range(NT):
                pe.wait_ge(v_normed, t + 1)
                if t >= 2:
                    pe.wait_ge(ya_ready, t - 1)
                for g in range(SGG):
                    last = nc.tensor.matmul(ps[:, Z[t % 2], g * P:(g + 1) * P], m.sg_wT[:, g],
                                            m.merged[:, t, SG + g * P:SG + (g + 1) * P], start=True, stop=True)
                last.then_inc(gated, 1)
            for f in range(4):
                features_unit(12 + f, 3, f)
            for t in range(NT):
                pe.wait_ge(ya_ready, t + 1)
                if t >= 2:
                    pe.wait_ge(ya_lo, t - 1)
                for k in range(4):
                    last = nc.tensor.transpose(ps[:, TURN[t % 2], k * P:(k + 1) * P],
                                               m.merged[:, t, k:SG:4], m.ident[:])
                last.then_inc(ya_turned, 1)
            for t in range(NT):
                rows_unit(16 + t, 4, t)

            def gate_part(g, part):
                j, t = divmod(g, NT)
                bank = MAIN[g % 2]
                i = 10 + 3 * j + part // 2
                if part == 0:
                    if g < 2:
                        pe.wait_ge(copied, 12 - 1 + g)
                    else:
                        pe.wait_ge(gate_ready, g - 1)
                if t == 0 and part % 2 == 0:
                    ring.ready(pe, i)
                for k in (2 * (part % 2), 2 * (part % 2) + 1):
                    kk = 4 * (part // 2) + k
                    last = product3(nc, ps[:, bank], m.act_hi[:, kk, t * P:(t + 1) * P],
                                    m.act_lo[:, kk, t * P:(t + 1) * P], ring.hi(i)[:, k], ring.lo(i)[:, k],
                                    kk == 0, kk == KD - 1)
                if part == 1 and t == NT - 1:
                    last.then_inc(half_used, 1)
                if part < 3:
                    return
                last.then_inc(gate_sum, 1)
                i += 1
                if t == 0:
                    ring.ready(pe, i)
                if g >= 1:
                    pe.wait_ge(merged, g)
                else:
                    pe.wait_ge(ya_lo, NT)
                y_hi, y_lo = (m.yaT_hi, m.yaT_lo) if j < 2 else (m.ybT_hi, m.ybT_lo)
                if g == 8:
                    pe.wait_ge(yb_lo, NT)
                for k in range(4):
                    last = product3(nc, ps[:, SIDE], y_hi[:, k, t * P:(t + 1) * P], y_lo[:, k, t * P:(t + 1) * P],
                                    ring.hi(i)[:, k], ring.lo(i)[:, k], k == 0, k == 3)
                last.then_inc(branch_sum, 1)

            def scores(s):
                qb, h = divmod(s, HEADS)
                n = width(s)
                if s >= 2:
                    pe.wait_ge(sig_ready, s - 1)
                elif s == 0:
                    pe.wait_ge(copied, 12)
                rows = slice(HD * (h % 2), HD * (h % 2) + HD)
                nc.tensor.matmul(ps[:, Z[s % 2], 0:n], m.qT[rows, h // 2, qb * P:(qb + 1) * P],
                                 m.kT[rows, h // 2, 0:n], start=True, stop=False)
                nc.tensor.matmul(ps[:, Z[s % 2], n - P:n], m.ident_bf[:], m.future_bf[:],
                                 start=False, stop=True).then_inc(z_ready, 1)

            def turn(s):
                pe.wait_ge(a_ready, s + 1)
                if s >= 2:
                    pe.wait_ge(aT_ready, s - 1)
                for c in range(width(s) // P):
                    last = nc.tensor.transpose(ps[:, TURN[s % 2], c * P:(c + 1) * P],
                                               m.sig_pos[:, s % 2, c * P:(c + 1) * P], m.ident[:])
                last.then_inc(a_turned, 1)

            def weighted_values(s):
                qb, h = divmod(s, HEADS)
                pe.wait_ge(aT_ready, s + 1)
                if h == 0 and qb:
                    pe.wait_ge(yb_ready, qb)
                for c in range(qb + 1):
                    last = nc.tensor.matmul(ps[:, YB, h * HD:(h + 1) * HD], m.aT[:, s % 2, c * P:(c + 1) * P],
                                            m.vsb[:, c, h * HD:(h + 1) * HD], start=(c == 0), stop=(c == qb))
                last.then_inc(av_done, 1)

            for s in range(NA + 3):
                if s < NA:
                    scores(s)
                    gate_part(s // 4, s % 4)
                if 2 <= s < NA + 2:
                    turn(s - 2)
                if s >= 3:
                    weighted_values(s - 3)
            for t in range(NT):
                pe.wait_ge(yb_ready, t + 1)
                if t >= 2:
                    pe.wait_ge(yb_lo, t - 1)
                for k in range(4):
                    last = nc.tensor.transpose(ps[:, TURN[t % 2], k * P:(k + 1) * P], m.yb[:, t, k:512:4],
                                               m.ident[:])
                last.then_inc(yb_turned, 1)
            for g in range(8, 16):
                for part in range(4):
                    gate_part(g, part)

        def turned_view(bank):
            return ps[:, bank].rearrange("p (k n) -> p k n", n=P)

        @block.scalar
        def _(act):
            ring.split_hi(act, 2)
            ring.split_hi(act, 3)
            for u in range(8):
                t = u % 4
                act.wait_ge(projected, u + 1)
                half = SG * (u // 4)
                nc.scalar.activation(m.merged[:, t, half:half + SG], ps[:, MAIN[u % 2]],
                                     ACT.Gelu_apprx_tanh).then_inc(gelu_out, 1)
                if t >= 2:
                    ring.split_hi(act, 4 + 2 * (u // 4) + t - 2)
            act.wait_ge(v_moments, NT)
            for t in range(NT):
                deviation(nc, m, t).then_inc(v_rooted, 1)
            for t in range(NT):
                act.wait_ge(v_stats, t + 1)
                v = m.merged[:, t, SG:2 * SG]
                nc.scalar.activation(v, v, ACT.Identity, bias=m.nmr[:, t], scale=m.rstd[:, t]).then_inc(v_scaled, 1)
            for i in range(8, 12):
                ring.split_hi(act, i)
            for t in range(NT):
                act.wait_ge(ya_turned, t + 1)
                nc.scalar.activation(m.yaT_hi[:, :, t * P:(t + 1) * P], turned_view(TURN[t % 2]),
                                     ACT.Copy).then_inc(ya_hi, 1)
            ring.split_hi(act, 12)
            ring.split_hi(act, 13)

            def gate(g):
                act.wait_ge(gate_sum, g + 1)
                if g >= 2:
                    act.wait_ge(merged, g - 1)
                nc.scalar.activation(m.gate[:, g % 2], ps[:, MAIN[g % 2]], ACT.Sigmoid).then_inc(gate_ready, 1)

            for s in range(NA + 3):
                if s < NA:
                    n = width(s)
                    act.wait_ge(z_ready, s + 1)
                    if s >= 2:
                        act.wait_ge(a_turned, s - 1)
                    nc.scalar.activation(m.sig_neg[:, s % 2, 0:n], ps[:, Z[s % 2], 0:n], ACT.Sigmoid,
                                         scale=-HD ** -0.5)
                    nc.scalar.activation(m.sig_pos[:, s % 2, 0:n], ps[:, Z[s % 2], 0:n], ACT.Sigmoid,
                                         scale=HD ** -0.5).then_inc(sig_ready, 1)
                if s >= 2 and s - 2 < NA:
                    r = s - 2
                    act.wait_ge(a_turned, r + 1)
                    if r >= 2:
                        act.wait_ge(av_done, r - 1)
                    nc.scalar.activation(m.aT[:, r % 2, 0:width(r)], ps[:, TURN[r % 2], 0:width(r)],
                                         ACT.Copy).then_inc(aT_ready, 1)
                if s % 4 == 0 and 4 <= s:
                    gate(s // 4 - 1)
                for i in SPLIT_AFTER_STEP.get(s, ()):
                    ring.split_hi(act, i)
            for t in range(NT):
                act.wait_ge(yb_turned, t + 1)
                nc.scalar.activation(m.ybT_hi[:, :, t * P:(t + 1) * P], turned_view(TURN[t % 2]),
                                     ACT.Copy).then_inc(yb_hi, 1)
            for g in range(8, 16):
                gate(g)
                for i in SPLIT_AFTER_GATE.get(g, ()):
                    ring.split_hi(act, i)

        @block.vector
        def _(dve):
            done = [0]

            def chained(ins):
                done[0] += 1
                ins.then_inc(chain, 1)
                dve.wait_ge(chain, done[0])

            for i in range(2, 6):
                ring.split_lo(dve, i)
            dve.wait_ge(sg_turned, 1)
            chained(nc.vector.tensor_copy(m.sg_wT[:], ps[:, YB].rearrange("p (g n) -> p g n", n=P)))
            nc.vector.memset(m.sg_wT[HD:P, :, 0:HD], 0.0).then_inc(sg_w_ready, 1)
            for t in range(NT):
                v = m.merged[:, t, SG:2 * SG]
                dve.wait_ge(gelu_out, 4 + t + 1)
                chained(nc.vector.bn_stats(m.stats[:, t, 0], v))
                nc.vector.bn_aggr(m.mv[:, t], m.stats[:, t, 0:1]).then_inc(v_moments, 1)
                if t >= 2:
                    ring.split_lo(dve, 4 + t)
            for t in range(NT):
                dve.wait_ge(v_rooted, t + 1)
                scale_and_shift(nc, m, chained, t).then_inc(v_stats, 1)
            for t in range(NT):
                v = m.merged[:, t, SG:2 * SG]
                dve.wait_ge(v_scaled, t + 1)
                chained(nc.vector.tensor_tensor(v, v, m.sg_g[:], ALU.mult))
                nc.vector.tensor_tensor(v, v, m.sg_bb[:], ALU.add).then_inc(v_normed, 1)

            def copy_out(u, dst):
                dve.wait_ge(projected, u + 1)
                nc.vector.tensor_copy(dst, ps[:, MAIN[u % 2]]).then_inc(copied, 1)

            for f in range(4):
                copy_out(8 + f, m.qT[:, f])
            ring.split_lo(dve, 8)
            ring.split_lo(dve, 9)
            for t in range(NT):
                dve.wait_ge(gated, t + 1)
                for g in range(SGG):
                    cols = slice(g * P, (g + 1) * P)
                    last = nc.vector.scalar_tensor_tensor(out=m.merged[:, t, cols], in0=ps[:, Z[t % 2], cols],
                                                          scalar=m.sg_b[:, g:g + 1], in1=m.merged[:, t, cols],
                                                          op0=ALU.add, op1=ALU.mult)
                last.then_inc(ya_ready, 1)
            for f in range(4):
                copy_out(12 + f, m.kT[:, f])
            ring.split_lo(dve, 10)
            ring.split_lo(dve, 11)
            for t in range(NT):
                dve.wait_ge(ya_hi, t + 1)
                nc.vector.tensor_tensor(m.yaT_lo[:, :, t * P:(t + 1) * P], turned_view(TURN[t % 2]),
                                        m.yaT_hi[:, :, t * P:(t + 1) * P].bitcast(F32),
                                        ALU.subtract).then_inc(ya_lo, 1)
            for t in range(NT):
                copy_out(16 + t, m.vsb[:, t])
            ring.split_lo(dve, 12)
            ring.split_lo(dve, 13)
            for b in range(2):
                last = nc.vector.memset(m.stick[:, b, P:SEQ + 1:P], 1.0)
            chained(last)

            def merge(g):
                j, t = divmod(g, NT)
                cols = slice((j % 2) * 512, (j % 2 + 1) * 512)
                dve.wait_ge(gate_ready, g + 1)
                dve.wait_ge(branch_sum, g + 1)
                gate = m.gate[:, g % 2]
                if j < 2:
                    nc.vector.tensor_tensor(m.merged[:, t, cols], gate, ps[:, SIDE], ALU.mult).then_inc(merged, 1)
                else:
                    chained(nc.vector.tensor_tensor(gate, gate, ps[:, SIDE], ALU.mult))
                    nc.vector.tensor_tensor(m.merged[:, t, cols], m.merged[:, t, cols], gate,
                                            ALU.add).then_inc(merged, 1)

            for s in range(NA + 3):
                if s < NA:
                    n = width(s)
                    b = s % 2
                    dve.wait_ge(sig_ready, s + 1)
                    chained(nc.vector.tensor_tensor_scan(m.stick[:, b, 0:n][:, ::-1], m.sig_neg[:, b, 0:n][:, ::-1],
                                                         m.sig_neg[:, b, 0:n][:, ::-1], 1.0, ALU.mult, ALU.bypass))
                    nc.vector.tensor_tensor(m.sig_pos[:, b, 0:n], m.sig_pos[:, b, 0:n], m.stick[:, b, 1:n + 1],
                                            ALU.mult).then_inc(a_ready, 1)
                if s >= 3 and (s - 3) % HEADS == HEADS - 1:
                    qb = (s - 3) // HEADS
                    dve.wait_ge(av_done, s - 3 + 1)
                    nc.vector.tensor_copy(m.yb[:, qb], ps[:, YB]).then_inc(yb_ready, 1)
                if s % 4 == 0 and 4 <= s:
                    merge(s // 4 - 1)
                for i in SPLIT_AFTER_STEP.get(s, ()):
                    ring.split_lo(dve, i)
            for t in range(NT):
                dve.wait_ge(yb_hi, t + 1)
                nc.vector.tensor_tensor(m.ybT_lo[:, :, t * P:(t + 1) * P], turned_view(TURN[t % 2]),
                                        m.ybT_hi[:, :, t * P:(t + 1) * P].bitcast(F32),
                                        ALU.subtract).then_inc(yb_lo, 1)
            for g in range(8, 16):
                merge(g)
                for i in SPLIT_AFTER_GATE.get(g, ()):
                    ring.split_lo(dve, i)


def out_block(nc, m, ps, norm_semaphores, a, h0, h1, ring):
    MAIN, TURN = (4, 5), (0, 2)
    FIRST = DENSE_PIECES - 4
    with ExitStack() as ctx:
        def sem(name):
            return ctx.enter_context(nc.semaphore(f"out_{name}"))

        rows_in, turned, hi_done, lo_done = sem("rows_in"), sem("turned"), sem("hi_done"), sem("lo_done")
        summed, added = sem("summed"), sem("added")
        for half in range(2):
            ring.freed[FIRST + half], ring.freed[FIRST + 2 + half] = (summed, 2 * NT - 1), (summed, 2 * NT)
        norm = RowNorm(nc, m, ps, norm_semaphores, banks=(6,))
        block = ctx.enter_context(nc.Block())

        def turned_view(t):
            b = TURN[t % 2]
            return ps[:, b:b + 2].rearrange("p b (k n) -> p (b k) n", n=P)

        @block.sync
        def _(sp):
            ring.load(sp, FIRST + 2)
            for t in range(NT):
                sp.dma_start(m.x[:, t], h0[t * P:(t + 1) * P, :]).then_inc(rows_in, 16)
            ring.load(sp, FIRST + 3)
            norm.load_affine(sp, a["ln1_g"][0], a["ln1_b"][0])
            ring.load(sp, FIRST + 4)
            ring.load(sp, FIRST + 5)
            for t in range(NT):
                norm.store(sp, t, h1)
            norm.stored(sp)

        @block.tensor
        def _(pe):
            def turn(t):
                if t >= 2:
                    pe.wait_ge(lo_done, t - 1)
                for k in range(KD):
                    last = nc.tensor.transpose(ps[:, TURN[t % 2] + k // 4, (k % 4) * P:(k % 4 + 1) * P],
                                               m.merged[:, t, k::KD], m.ident[:])
                last.then_inc(turned, 1)

            turn(0)
            turn(1)
            for u in range(2 * NT):
                t, c = divmod(u, 2)
                if c == 0:
                    pe.wait_ge(lo_done, t + 1)
                if u >= 2:
                    pe.wait_ge(added, u - 1)
                for kk in range(KD):
                    i = FIRST + 2 * c + kk // 4
                    if t == 0 and kk % 4 == 0:
                        ring.ready(pe, i)
                    last = product3(nc, ps[:, MAIN[u % 2]], m.act_hi[:, kk, t * P:(t + 1) * P],
                                    m.act_lo[:, kk, t * P:(t + 1) * P], ring.hi(i)[:, kk % 4],
                                    ring.lo(i)[:, kk % 4], kk == 0, kk == KD - 1)
                last.then_inc(summed, 1)
                if c == 1:
                    if t + 2 < NT:
                        turn(t + 2)
                    if t >= 1:
                        norm.turn(pe, t - 1)
            norm.turn(pe, NT - 1)

        @block.scalar
        def _(act):
            def high_part(t):
                act.wait_ge(turned, t + 1)
                nc.scalar.activation(m.act_hi[:, :, t * P:(t + 1) * P], turned_view(t), ACT.Copy).then_inc(hi_done, 1)

            high_part(0)
            ring.split_hi(act, FIRST + 1)
            ring.split_hi(act, FIRST + 2)
            high_part(1)
            ring.split_hi(act, FIRST + 3)
            for t in range(NT):
                if t + 2 < NT:
                    high_part(t + 2)
                if t >= 1:
                    norm.high_part(act, t - 1)
                norm.deviate(act, t)
                norm.centre(act, t)
            ring.split_hi(act, FIRST + 4)
            ring.split_hi(act, FIRST + 5)
            norm.high_part(act, NT - 1)

        @block.vector
        def _(dve):
            def low_part(t):
                dve.wait_ge(hi_done, t + 1)
                nc.vector.tensor_tensor(m.act_lo[:, :, t * P:(t + 1) * P], turned_view(t),
                                        m.act_hi[:, :, t * P:(t + 1) * P].bitcast(F32),
                                        ALU.subtract).then_inc(lo_done, 1)

            low_part(0)
            ring.split_lo(dve, FIRST + 1)
            ring.split_lo(dve, FIRST + 2)
            low_part(1)
            ring.split_lo(dve, FIRST + 3)
            dve.wait_ge(rows_in, 16 * NT)
            for t in range(NT):
                for c in range(2):
                    u = 2 * t + c
                    dve.wait_ge(summed, u + 1)
                    row = m.x[:, t, c * 512:(c + 1) * 512]
                    last = nc.vector.scalar_tensor_tensor(out=row, in0=row, scalar=ALPHA, in1=ps[:, MAIN[u % 2]],
                                                          op0=ALU.mult, op1=ALU.add).then_inc(added, 1)
                dve.wait_ge(added, 2 * t + 2)
                norm.statistics(dve, t)
                if t + 2 < NT:
                    low_part(t + 2)
                norm.finish(dve, t)
                if t >= 1:
                    norm.low_part(dve, t - 1)
                norm.gain(dve, t)
            ring.split_lo(dve, FIRST + 4)
            ring.split_lo(dve, FIRST + 5)
            norm.low_part(dve, NT - 1)

        @block.gpsimd
        def _(pool):
            for t in range(NT):
                norm.shift(pool, t)


def routing_block(nc, m, ps, a, acc_dram, acc_odd_dram, ring):
    LOGIT, MAIN, TURN, SUM, POS, ALL = 0, (1, 2), 3, (4, 5), 6, 7
    with ExitStack() as ctx:
        def sem(name):
            return ctx.enter_context(nc.semaphore(f"route_{name}"))

        GU_PIECE = DENSE_PIECES
        router_in, down_in = sem("router_in"), sem("down_in")
        router_hi, router_split, logits, scored = sem("router_hi"), sem("router_split"), sem("logits"), sem("scored")
        picked, counted, tags_ready = sem("picked"), sem("counted"), sem("tags_ready")
        gu_sum, silu_out, h_ready = sem("gu_sum"), sem("silu_out"), sem("h_ready")
        turned, hT_ready, summed, acc_ready = sem("turned"), sem("hT_ready"), sem("summed"), sem("acc_ready")
        acc_out = [sem("acc_out0"), sem("acc_out1")]
        chain, index_base, zeros = sem("chain"), sem("index_base"), sem("zeros")
        block = ctx.enter_context(nc.Block())

        @block.sync
        def _(sp):
            sp.dma_start(m.router[:], a["router_w"][0].rearrange("(p k) n -> p k n", p=P)).then_inc(router_in, 16)
            sp.dma_start(m.r_bias[:], a["router_bias"][0].partition_broadcast(P)).then_inc(router_in, 16)
            sp.dma_start(m.sh_down[:], a["sh_w_down"][0].rearrange("(p j) n -> p (j n)", p=P)).then_inc(down_in, 16)
            sp.wait_ge(zeros, 1)
            for t in range(NT):
                sp.dma_start(acc_odd_dram[t * P:(t + 1) * P, :], m.zero_rows[:]).then_inc(acc_out[t % 2], 16)
            for t in range(NT):
                sp.wait_ge(acc_ready, t + 1)
                sp.dma_start(acc_dram[t * P:(t + 1) * P, :], m.acc[:, t % 2]).then_inc(acc_out[t % 2], 16)
            sp.wait_ge(acc_out[0], 64)
            sp.wait_ge(acc_out[1], 64)

        @block.gpsimd
        def _(pool):
            nc.gpsimd.memset(m.zero_rows[:], 0.0).then_inc(zeros, 1)
            for t in range(NT):
                nc.gpsimd.memset(m.tags[:, t, :, 0:1], float(t * P))
                nc.gpsimd.iota(m.tags[:, t, :, 1:2], pattern=[[0, NE], [0, 1]], base=0, channel_multiplier=1,
                               allow_small_or_imprecise_dtypes=True)
                last = nc.gpsimd.memset(m.tags[:, t, :, 2:3], -FAR)
            last.then_inc(index_base, 1)

        @block.tensor
        def _(pe):
            pe.wait_ge(router_split, 1)
            for t in range(NT):
                for k in range(KD):
                    last = product3(nc, ps[:, LOGIT, t * NE:(t + 1) * NE], m.act_hi[:, k, t * P:(t + 1) * P],
                                    m.act_lo[:, k, t * P:(t + 1) * P], m.r_hi[:, k], m.r_lo[:, k],
                                    k == 0, k == KD - 1)
            last.then_inc(logits, 1)
            for t in range(NT):
                if t >= 2:
                    pe.wait_ge(h_ready, t - 1)
                for kk in range(KD):
                    i = GU_PIECE + kk // 4
                    last = product3(nc, ps[:, MAIN[t % 2]], m.act_hi[:, kk, t * P:(t + 1) * P],
                                    m.act_lo[:, kk, t * P:(t + 1) * P], ring.hi(i)[:, kk % 4],
                                    ring.lo(i)[:, kk % 4], kk == 0, kk == KD - 1)
                last.then_inc(gu_sum, 1)
            pe.wait_ge(picked, 1)
            for t in range(NT):
                for o in range(t + 1):
                    last = nc.tensor.matmul(ps[:, POS, t * NE:(t + 1) * NE],
                                            m.ones_bf[:] if o < t else m.earlier_bf[:], m.pick_bf[:, o],
                                            start=(o == 0), stop=(o == t))
            for o in range(NT):
                last = nc.tensor.matmul(ps[:, ALL, 0:NE], m.ones_bf[:], m.pick_bf[:, o],
                                        start=(o == 0), stop=(o == NT - 1))
            last.then_inc(counted, 1)
            pe.wait_ge(down_in, 16)
            for t in range(NT):
                pe.wait_ge(h_ready, t + 1)
                if t >= 1:
                    pe.wait_ge(hT_ready, t)
                for j in range(2):
                    last = nc.tensor.transpose(ps[:, TURN, j * P:(j + 1) * P], m.sh_h[:, t, j::2], m.ident[:])
                last.then_inc(turned, 1)
                pe.wait_ge(hT_ready, t + 1)
                if t >= 1:
                    pe.wait_ge(acc_ready, t)
                for c in range(2):
                    for j in range(2):
                        last = nc.tensor.matmul(ps[:, SUM[c]], m.sh_hT[:, j, t * P:(t + 1) * P],
                                                m.sh_down[:, j * D + c * 512:j * D + (c + 1) * 512],
                                                start=(j == 0), stop=(j == 1))
                last.then_inc(summed, 1)

        @block.scalar
        def _(act):
            act.wait_ge(router_in, 32)
            nc.scalar.activation(m.r_hi[:], m.router[:], ACT.Copy).then_inc(router_hi, 1)
            act.wait_ge(logits, 1)
            nc.scalar.activation(m.score[:], ps[:, LOGIT, 0:NT * NE].rearrange("p (t e) -> p t e", e=NE),
                                 ACT.Sigmoid).then_inc(scored, 1)
            for t in range(NT):
                act.wait_ge(gu_sum, t + 1)
                nc.scalar.activation(m.sh_h[:, t], ps[:, MAIN[t % 2], 0:FF], ACT.Silu).then_inc(silu_out, 1)
            for t in range(NT):
                act.wait_ge(turned, t + 1)
                nc.scalar.activation(m.sh_hT[:, :, t * P:(t + 1) * P],
                                     ps[:, TURN, 0:2 * P].rearrange("p (j n) -> p j n", n=P),
                                     ACT.Copy).then_inc(hT_ready, 1)

        @block.vector
        def _(dve):
            done = [0]

            def chained(ins):
                done[0] += 1
                ins.then_inc(chain, 1)
                dve.wait_ge(chain, done[0])

            dve.wait_ge(router_hi, 1)
            nc.vector.tensor_tensor(m.r_lo[:], m.router[:], m.r_hi[:].bitcast(F32),
                                    ALU.subtract).then_inc(router_split, 1)
            dve.wait_ge(scored, 1)
            chained(nc.vector.tensor_tensor(m.sel[:], m.score[:], m.r_bias[:].unsqueeze(1).to_broadcast([P, NT, NE]),
                                            ALU.add))
            for t in range(NT):
                for q in range(NGRP):
                    last = nc.vector.max(out=m.top[:, t, q], in_=m.sel[:, t, q * 8:(q + 1) * 8])
            chained(last)
            chained(nc.vector.tensor_tensor(m.grp[:], m.top[:, :, :, 0], m.top[:, :, :, 1], ALU.add))
            for t in range(NT):
                mine = m.grp[:, t].unsqueeze(2).to_broadcast([P, NGRP, NGRP])
                other = m.grp[:, t].unsqueeze(1).to_broadcast([P, NGRP, NGRP])
                nc.vector.tensor_tensor(m.beats[:, t], other, mine, ALU.is_gt)
                last = nc.vector.tensor_tensor(m.ties[:, t], other, mine, ALU.is_equal)
            chained(last)
            for t in range(NT):
                last = nc.vector.tensor_tensor(m.ties[:, t], m.ties[:, t], m.lower_grp[:], ALU.mult)
            chained(last)
            chained(nc.vector.tensor_tensor(m.beats[:], m.beats[:], m.ties[:], ALU.add))
            chained(nc.vector.tensor_reduce(m.rank[:].rearrange("p t g -> p (t g)"),
                                            m.beats[:].rearrange("p t g o -> p (t g) o"), AX, ALU.add))
            chained(nc.vector.tensor_scalar(m.rank[:], m.rank[:], 3.5, -1e30, ALU.is_gt, ALU.mult))
            chained(nc.vector.tensor_tensor(m.sel[:].rearrange("p t (g e) -> p (t g) e", e=8),
                                            m.sel[:].rearrange("p t (g e) -> p (t g) e", e=8),
                                            m.rank[:].rearrange("p t g -> p (t g)").unsqueeze(2)
                                            .to_broadcast([P, NT * NGRP, 8]), ALU.add))
            for t in range(NT):
                last = nc.vector.max(out=m.top8[:, t], in_=m.sel[:, t])
            chained(last)
            for t in range(NT):
                last = nc.vector.match_replace(out=m.rest[:, t], in_to_replace=m.top8[:, t], in_values=m.sel[:, t],
                                               imm_value=-3e38)
            chained(last)
            chained(nc.vector.tensor_scalar(m.rest[:], m.rest[:], -2e38, None, ALU.is_lt))
            nc.vector.tensor_copy(m.pick_bf[:], m.rest[:]).then_inc(picked, 1)
            chained(nc.vector.tensor_tensor(m.score[:], m.score[:], m.rest[:], ALU.mult))
            chained(nc.vector.tensor_reduce(m.den[:], m.score[:], AX, ALU.add))
            chained(nc.vector.reciprocal(m.den[:], m.den[:]))
            for t in range(NT):
                last = nc.vector.tensor_scalar(m.score[:, t], m.score[:, t], m.den[:, t:t + 1], ROUTED_SCALE,
                                               ALU.mult, ALU.mult)
            chained(last)
            dve.wait_ge(index_base, 1)
            for part in range(3):
                tag = m.tags[:, :, :, 3 + part]
                chained(nc.vector.tensor_copy(tag, m.score[:]))
                if part < 2:
                    chained(nc.vector.tensor_tensor(m.score[:], m.score[:], tag, ALU.subtract))
            for t in range(NT):
                dve.wait_ge(silu_out, t + 1)
                nc.vector.tensor_tensor(m.sh_h[:, t], m.sh_h[:, t], ps[:, MAIN[t % 2], FF:2 * FF],
                                        ALU.mult).then_inc(h_ready, 1)
            for t in range(NT):
                dve.wait_ge(summed, t + 1)
                if t >= 2:
                    dve.wait_ge(acc_out[t % 2], 48)
                nc.vector.scalar_tensor_tensor(out=m.acc[:, t % 2].rearrange("p (c n) -> p c n", n=512),
                                               in0=m.x[:, t].rearrange("p (c n) -> p c n", n=512), scalar=ALPHA,
                                               in1=ps[:, SUM[0]:SUM[1] + 1], op0=ALU.mult,
                                               op1=ALU.add).then_inc(acc_ready, 1)
            chained(nc.vector.tensor_scalar(m.rest[:], m.rest[:], -FAR, FAR, ALU.mult, ALU.add))
            dve.wait_ge(counted, 1)
            nc.vector.tensor_tensor(m.slot_of[:], m.rest[:],
                                    ps[:, POS, 0:NT * NE].rearrange("p (t e) -> p t e", e=NE), ALU.add)
            chained(nc.vector.tensor_reduce(m.peak[:], ps[:, ALL, 0:NE], AX, ALU.max))
            nc.vector.tensor_copy(m.peak_i[:], m.peak[:])


class Expert:

    def __init__(self, r, quad, q):
        quad, q = quad + q // 4, q % 4
        self.r, self.quad, self.q = r, quad, q
        self.e = 4 * quad + q
        self.b = q % 2
        self.it = r * NE + self.e
        self.turn4 = r * (NE // 4) + quad + 1
        self.turn2 = r * (NE // 2) + 2 * quad + q // 2 + 1

    def next(self, n):
        return Expert(self.r, self.quad, self.q + n)


def experts_block(nc, m, ps, a, h1, acc_dram, acc_odd_dram, CAP, embedding):
    GU, HT, XT, Y, TAGS = (0, 1), 2, 3, 5, 7
    LEAD = 2
    LEAD4 = 4
    ROUNDS = -(-SEQ // CAP)
    QUADS = NE // 4
    w_gate, w_up, w_down = a["moe_w_gate"][0], a["moe_w_up"][0], a["moe_w_down"][0]
    with ExitStack() as ctx:
        def sem(name):
            return ctx.enter_context(nc.semaphore(f"moe_{name}"))

        gu_in = [[sem(f"gu_in{b}{half}") for half in range(2)] for b in range(2)]
        dn_in = [sem(f"dn_in{b}") for b in range(2)]
        gu_hi, gu_lo, half_used = sem("gu_hi"), sem("gu_lo"), sem("half_used")
        dn_hi, dn_lo = sem("dn_hi"), sem("dn_lo")
        hot_ready, located, found, get_ready, put_ready = (sem("hot_ready"), sem("located"), sem("found"),
                                                           sem("get_ready"), sem("put_ready"))
        got = [sem(f"got{q}") for q in range(4)]
        put = [sem("put_even"), sem("put_odd")]
        x_turned, x_hi, x_lo = sem("x_turned"), sem("x_hi"), sem("x_lo")
        gu_sum, silu_out, h_ready = sem("gu_sum"), sem("silu_out"), sem("h_ready")
        h_turned, hT_hi, hT_lo, y_sum, y_ready = (sem("h_turned"), sem("hT_hi"), sem("hT_lo"), sem("y_sum"),
                                                  sem("y_ready"))
        cleared, passed = sem("cleared"), sem("passed")
        block = ctx.enter_context(nc.Block())

        peak = [None]
        embedding.begin()

        def rounds(eng, body):
            peak[0] = eng.value_load(m.peak_i[0:1, 0:1], min_val=0, max_val=SEQ)
            with eng.Fori(0, ROUNDS) as r:
                with eng.If(peak[0] > r * CAP):
                    body(r)

        def all_experts(eng, r, step):
            for q in range(4):
                step(Expert(r, 0, q), q)
            with eng.Fori(1, QUADS - 2) as quad:
                for q in range(4):
                    step(Expert(r, quad, q))
            for quad in (QUADS - 2, QUADS - 1):
                for q in range(4):
                    step(Expert(r, quad, q), 4 * (quad - QUADS) + q)

        def x_banks():
            return ps[:, XT:XT + 2, 0:4 * CAP]

        @block.sync
        def _(sp):
            def load_gate_up(x):
                for half in range(2):
                    sp.wait_ge(gu_lo, 2 * x.it + half - 4 + 1 + 2 * LEAD)
                    dst = m.gu_raw[:, 2 * x.b + half].rearrange("p (w n) -> p w n", w=2)
                    for w, src in enumerate((w_gate, w_up)):
                        rows = src[bass.ds(x.e, 1)].rearrange("o (p k) n -> p o (k n)", p=P)
                        sp.dma_start(dst[:, w:w + 1], rows[:, :, half * (HC // 2):(half + 1) * (HC // 2)]) \
                          .then_inc(gu_in[x.b][half], 16)

            def load_down(x):
                sp.wait_ge(dn_lo, x.it - 2 + 1 + LEAD)
                sp.dma_start(m.dn_raw[:, x.b:x.b + 1],
                             w_down[bass.ds(x.e, 1)].rearrange("o (p j) n -> p o (j n)", p=P)) \
                  .then_inc(dn_in[x.b], 16)

            def body(r):
                load_gate_up(Expert(r, 0, 0))
                load_gate_up(Expert(r, 0, 1))

                def step(x, at=0):
                    load_down(x)
                    if at not in (-1, -2):
                        load_gate_up(x.next(2))

                all_experts(sp, r, step)
                with sp.If(peak[0] <= (r + 1) * CAP):
                    sp.wait_ge(gu_lo, 2 * ((r + 1) * NE) + 2 * LEAD)
                    embedding.load_p(sp)
                    sp.wait_ge(y_sum, (r + 1) * NE - 1 + LEAD)
                    embedding.load_weights(sp)

            rounds(sp, body)
            embedding.sync(sp)

        @block.tensor
        def _(pe):
            pe.sem_inc(half_used, LEAD)
            pe.sem_inc(gu_sum, LEAD)
            pe.sem_inc(y_sum, LEAD)
            pe.sem_inc(x_turned, LEAD4)

            def locate(x):
                pe.wait_ge(hot_ready, x.it + 1)
                pe.wait_ge(found, x.it + LEAD)
                for t in range(NT):
                    last = nc.tensor.matmul(ps[0:CAP, TAGS, 0:6], m.onehot[:, x.b, t],
                                            m.tags[:, t, bass.ds(x.e, 1), :].rearrange("p o c -> p (o c)"),
                                            start=(t == 0), stop=(t == NT - 1))
                last.then_inc(located, 1)

            def turn_x(x):
                pe.wait_ge(got[x.q], 16 * x.turn4)
                pe.wait_ge(x_lo, x.it + LEAD)
                for k in range(KD):
                    last = nc.tensor.transpose(ps[:, XT + k // 4, (k % 4) * CAP:(k % 4 + 1) * CAP],
                                               m.xg[x.q][0:CAP, k::KD], m.ident[0:CAP, 0:CAP])
                last.then_inc(x_turned, 1)

            def gate_up(x, half):
                pe.wait_ge(gu_lo, 2 * x.it + half + 1 + 2 * LEAD)
                if half == 0:
                    pe.wait_ge(x_lo, x.it + 1 + LEAD)
                    pe.wait_ge(h_ready, x.it - 1 + LEAD)
                w_hi = m.w_hi[:, 2 * x.b + half].rearrange("p (w k n) -> p k w n", w=2, n=FF)
                w_lo = m.w_lo[:, 2 * x.b + half].rearrange("p (w k n) -> p k w n", w=2, n=FF)
                for k in range(4):
                    kk = 4 * half + k
                    cols = slice(kk * CAP, (kk + 1) * CAP)
                    last = product3(nc, ps[0:CAP, GU[x.b]].rearrange("p (w n) -> p w n", w=2),
                                    m.xgT_hi[:, x.b, cols], m.xgT_lo[:, x.b, cols], w_hi[:, k], w_lo[:, k],
                                    kk == 0, kk == KD - 1)
                last.then_inc(gu_sum if half else half_used, 1)

            def turn_h(x):
                pe.wait_ge(h_ready, x.it + 1 + LEAD)
                pe.wait_ge(hT_lo, x.it + LEAD)
                for j in range(2):
                    last = nc.tensor.transpose(ps[:, HT, j * CAP:(j + 1) * CAP], m.h[0:CAP, x.b, j::2],
                                               m.ident[0:CAP, 0:CAP])
                last.then_inc(h_turned, 1)

            def down(x):
                pe.wait_ge(hT_lo, x.it + 1 + LEAD)
                pe.wait_ge(dn_lo, x.it + 1 + LEAD)
                pe.wait_ge(y_ready, x.it + LEAD)
                for c in range(2):
                    for j in range(2):
                        rows, cols = slice(j * CAP, (j + 1) * CAP), slice(j * D + c * 512, j * D + (c + 1) * 512)
                        last = product3(nc, ps[0:CAP, Y + c], m.hT_hi[:, x.b, rows], m.hT_lo[:, x.b, rows],
                                        m.dn_hi[:, x.b, cols], m.dn_lo[:, x.b, cols], j == 0, j == 1)
                last.then_inc(y_sum, 1)

            def body(r):
                for q in range(4):
                    locate(Expert(r, 0, q))
                turn_x(Expert(r, 0, 0))

                def step(x, at=99):
                    if at != 0:
                        turn_h(x.next(-1))
                    gate_up(x, 0)
                    if not -4 <= at <= -1:
                        locate(x.next(4))
                    gate_up(x, 1)
                    if at != -1:
                        turn_x(x.next(1))
                    if at != 0:
                        down(x.next(-1))

                all_experts(pe, r, step)
                turn_h(Expert(r, QUADS - 1, 3))
                down(Expert(r, QUADS - 1, 3))

            rounds(pe, body)
            embedding.tensor(pe)

        @block.scalar
        def _(act):
            def split(x, half):
                act.wait_ge(gu_in[x.b][half], 32 * x.turn2)
                act.wait_ge(gu_sum if half else half_used, x.it - 2 + 1 + LEAD)
                nc.scalar.activation(m.w_hi[:, 2 * x.b + half], m.gu_raw[:, 2 * x.b + half],
                                     ACT.Copy).then_inc(gu_hi, 1)

            def split_down(x):
                act.wait_ge(dn_in[x.b], 16 * x.turn2)
                act.wait_ge(y_sum, x.it - 2 + 1 + LEAD)
                nc.scalar.activation(m.dn_hi[:, x.b], m.dn_raw[:, x.b], ACT.Copy).then_inc(dn_hi, 1)

            def split_x(x):
                act.wait_ge(x_turned, x.it + 1 + LEAD4)
                nc.scalar.activation(m.xgT_hi[:, x.b].rearrange("p (c n) -> p c n", c=2), x_banks(),
                                     ACT.Copy).then_inc(x_hi, 1)

            def silu(x):
                act.wait_ge(gu_sum, x.it + 1 + LEAD)
                nc.scalar.activation(m.silu[0:CAP, x.b], ps[0:CAP, GU[x.b], 0:FF], ACT.Silu).then_inc(silu_out, 1)

            def split_hT(x):
                act.wait_ge(h_turned, x.it + 1)
                nc.scalar.activation(m.hT_hi[:, x.b], ps[:, HT, 0:2 * CAP], ACT.Copy).then_inc(hT_hi, 1)

            def scale_y(x):
                act.wait_ge(y_sum, x.it + 1 + LEAD)
                act.wait_ge(put[x.b], 16 * x.turn2)
                nc.scalar.activation(m.y[x.b][0:CAP].rearrange("p (c n) -> p c n", n=512), ps[0:CAP, Y:Y + 2],
                                     ACT.Copy,
                                     scale=m.found[0:CAP, bass.ds(x.e, 1), 1:2].rearrange("p o c -> p (o c)")) \
                  .then_inc(y_ready, 1)

            def body(r):
                split(Expert(r, 0, 0), 0)
                split(Expert(r, 0, 0), 1)
                split_x(Expert(r, 0, 0))

                def step(x, at=99):
                    if at != 0:
                        split_hT(x.next(-1))
                        split_down(x.next(-1))
                    if at != -1:
                        split(x.next(1), 0)
                        split(x.next(1), 1)
                    else:
                        split_down(x)
                    silu(x)
                    if at != -1:
                        split_x(x.next(1))
                    if at != 0:
                        scale_y(x.next(-1))

                all_experts(act, r, step)
                split_hT(Expert(r, QUADS - 1, 3))
                scale_y(Expert(r, QUADS - 1, 3))

            act.sem_inc(y_ready, LEAD)
            rounds(act, body)
            embedding.scalar(act)

        @block.vector
        def _(dve):
            def one_hot(x):
                dve.wait_ge(located, x.it - 1 + LEAD)
                nc.vector.tensor_tensor(m.onehot[:, x.b],
                                        m.slots[:, bass.ds(x.r * CAP, CAP)].unsqueeze(1).to_broadcast([P, NT, CAP]),
                                        m.slot_of[:, :, bass.ds(x.e, 1)].to_broadcast([P, NT, CAP]),
                                        ALU.is_equal).then_inc(hot_ready, 1)

            def find(x):
                dve.wait_ge(located, x.it + 1 + LEAD)
                nc.vector.tensor_reduce(m.found[0:CAP, bass.ds(x.e, 1), :].rearrange("p o c -> p (o c)"),
                                        ps[0:CAP, TAGS, 0:6].rearrange("p (c x) -> p c x", x=3),
                                        AX, ALU.add).then_inc(found, 1)
                dve.wait_ge(found, x.it + 1 + LEAD)
                dve.wait_ge(x_turned, x.it - 4 + 1 + LEAD4)
                nc.vector.tensor_scalar(m.get_idx[x.q][0:CAP],
                                        m.found[0:CAP, bass.ds(x.e, 1), 0:1].rearrange("p o c -> p (o c)"),
                                        FAR, None, ALU.add).then_inc(get_ready, 1)

            def put_list(x):
                dve.wait_ge(put[x.b], 16 * x.turn2)
                nc.vector.tensor_scalar(m.put_idx[x.b][0:CAP],
                                        m.found[0:CAP, bass.ds(x.e, 1), 0:1].rearrange("p o c -> p (o c)"),
                                        FAR, None, ALU.add).then_inc(put_ready, 1)

            def split(x, half):
                dve.wait_ge(gu_hi, 2 * x.it + half + 1)
                nc.vector.tensor_tensor(m.w_lo[:, 2 * x.b + half], m.gu_raw[:, 2 * x.b + half],
                                        m.w_hi[:, 2 * x.b + half].bitcast(F32), ALU.subtract).then_inc(gu_lo, 1)

            def split_down(x):
                dve.wait_ge(dn_hi, x.it + 1)
                nc.vector.tensor_tensor(m.dn_lo[:, x.b], m.dn_raw[:, x.b], m.dn_hi[:, x.b].bitcast(F32),
                                        ALU.subtract).then_inc(dn_lo, 1)

            def split_x(x):
                dve.wait_ge(x_hi, x.it + 1)
                nc.vector.tensor_tensor(m.xgT_lo[:, x.b].rearrange("p (c n) -> p c n", c=2), x_banks(),
                                        m.xgT_hi[:, x.b].bitcast(F32).rearrange("p (c n) -> p c n", c=2),
                                        ALU.subtract).then_inc(x_lo, 1)

            def times_up(x):
                dve.wait_ge(silu_out, x.it + 1)
                nc.vector.tensor_tensor(m.h[0:CAP, x.b], m.silu[0:CAP, x.b], ps[0:CAP, GU[x.b], FF:2 * FF],
                                        ALU.mult).then_inc(h_ready, 1)

            def split_hT(x):
                dve.wait_ge(hT_hi, x.it + 1)
                nc.vector.tensor_tensor(m.hT_lo[:, x.b], ps[:, HT, 0:2 * CAP], m.hT_hi[:, x.b].bitcast(F32),
                                        ALU.subtract).then_inc(hT_lo, 1)

            def body(r):
                one_hot(Expert(r, 0, 0))
                for q in range(4):
                    one_hot(Expert(r, 0, q + 1))
                    find(Expert(r, 0, q))
                split(Expert(r, 0, 0), 0)
                split(Expert(r, 0, 0), 1)
                split_x(Expert(r, 0, 0))

                def step(x, at=99):
                    if at != 0:
                        split_hT(x.next(-1))
                        split_down(x.next(-1))
                    if at != -1:
                        split(x.next(1), 0)
                    if not -4 <= at <= -1:
                        find(x.next(4))
                    if at != -1:
                        split(x.next(1), 1)
                    else:
                        split_down(x)
                    times_up(x)
                    if at != -1:
                        split_x(x.next(1))
                        put_list(x)
                    if not -5 <= at <= -1:
                        one_hot(x.next(5))

                all_experts(dve, r, step)
                split_hT(Expert(r, QUADS - 1, 3))
                put_list(Expert(r, QUADS - 1, 3))

            dve.sem_inc(found, LEAD)
            dve.sem_inc(x_lo, LEAD)
            dve.sem_inc(h_ready, LEAD)
            dve.sem_inc(gu_lo, 2 * LEAD)
            dve.sem_inc(dn_lo, LEAD)
            dve.sem_inc(hT_lo, LEAD)
            dve.sem_inc(located, LEAD)
            rounds(dve, body)
            embedding.vector(dve)

        @block.gpsimd
        def _(pool):
            last_token = pool.to_reg(SEQ - 1)
            for b in range(2):
                nc.gpsimd.dma_start(m.y[b][0:1], h1[b:b + 1]).then_inc(put[b], 16)
            for q in range(4):
                nc.gpsimd.memset(m.xg[q][:], 0.0).then_inc(cleared, 1)

            def gather(x):
                pool.wait_ge(get_ready, x.it + 1)
                pool.wait_ge(x_turned, x.it - 4 + 1 + LEAD4)
                pool.sem_inc(passed, 1)
                pool.wait_ge(cleared, 4)
                nc.gpsimd.indirect_dma_start(out=m.xg[x.q][0:CAP], out_offset=None, in_=h1,
                                             in_offset=bass.IndirectOffsetOnAxis(ap=m.get_idx[x.q][0:CAP], axis=0),
                                             bounds_check=last_token, oob_is_err=False).then_inc(got[x.q], 16)

            def scatter(x):
                pool.wait_ge(y_ready, x.it + 1 + LEAD)
                pool.wait_ge(put_ready, x.it + 1)
                pool.wait_ge(put[x.b], 16 * x.turn2)
                pool.sem_inc(passed, 1)
                pool.wait_ge(cleared, 4)
                nc.gpsimd.indirect_dma_start(out=(acc_dram, acc_odd_dram)[x.b],
                                             out_offset=bass.IndirectOffsetOnAxis(ap=m.put_idx[x.b][0:CAP], axis=0),
                                             in_=m.y[x.b][0:CAP], in_offset=None, bounds_check=last_token,
                                             oob_is_err=False, compute_op=ALU.add).then_inc(put[x.b], 16)

            def body(r):
                for q in range(4):
                    gather(Expert(r, 0, q))

                def step(x, at=99):
                    if not -4 <= at <= -1:
                        gather(x.next(4))
                    if at != 0:
                        scatter(x.next(-1))

                all_experts(pool, r, step)
                scatter(Expert(r, QUADS - 1, 3))
                for b in range(2):
                    pool.wait_ge(put[b], 16 * ((r + 1) * (NE // 2) + 1))

            rounds(pool, body)
            embedding.gpsimd(pool)


class Embedding:

    MAIN, TURN, PT = (0, 1), (3, 5), (2, 7)

    def __init__(self, nc, m, ps, ctx, norm_semaphores, a, acc_dram, acc_odd_dram, out):
        def sem(name):
            return ctx.enter_context(nc.semaphore(f"ple_{name}"))

        self.nc, self.m, self.ps, self.a, self.norm_semaphores = nc, m, ps, a, norm_semaphores
        self.acc, self.out = (acc_dram, acc_odd_dram), out
        w = a["ple_w_gate"][0].rearrange("(p k) n -> p k n", p=P)
        self.ring = WeightRing(nc, m, ctx, "ple", [w[:, 4 * half:4 * half + 4, c * 512:(c + 1) * 512]
                                                   for c in range(2) for half in range(2)], m.ple_raw)
        self.p_in, self.pw_in, self.scattered = sem("p_in"), sem("pw_in"), sem("scattered")
        self.rows_in = [sem(f"rows_in{t}") for t in range(NT)]
        self.p_turned, self.pT_ready, self.p_sum, self.p_out = sem("p_turned"), sem("pT_ready"), sem("p_sum"), sem("p_out")
        self.row_sum, self.turned, self.hi_done, self.lo_done = (sem("row_sum"), sem("turned"), sem("hi_done"),
                                                                 sem("lo_done"))
        self.summed, self.gate_ready, self.gate_used, self.added = (sem("summed"), sem("gate_ready"),
                                                                    sem("gate_used"), sem("added"))

    def begin(self):
        self.norm = RowNorm(self.nc, self.m, self.ps, self.norm_semaphores)

    def turned_view(self, t):
        b = self.TURN[t % 2]
        return self.ps[:, b:b + 2].rearrange("p b (k n) -> p (b k) n", n=P)

    def load_p(self, sp):
        m, a = self.m, self.a
        sp.dma_start(m.p[:], a["p"][0, 0].rearrange("(t p) d -> p t d", p=P)).then_inc(self.p_in, 16)
        sp.dma_start(m.p_w[:], a["ple_w_proj"][0].rearrange("(p j) n -> p (j n)", p=P)).then_inc(self.pw_in, 16)

    def load_weights(self, sp):
        self.ring.load(sp, 0)
        self.ring.load(sp, 1)

    def sync(self, sp):
        m = self.m
        sp.wait_ge(self.scattered, 1)
        for t in range(NT):
            sp.dma_start(m.x[:, t], self.acc[0][t * P:(t + 1) * P, :]).then_inc(self.rows_in[t], 16)
            sp.dma_start(m.x_odd[t // 2][:, t % 2], self.acc[1][t * P:(t + 1) * P, :]).then_inc(self.rows_in[t], 16)
            if t == 1:
                self.ring.load(sp, 2)
                self.ring.load(sp, 3)
        self.norm.load_affine(sp, self.a["ln2_g"][0], self.a["ln2_b"][0])
        for t in range(NT):
            self.norm.store(sp, t, self.out)
        self.norm.stored(sp)

    def gpsimd(self, pool):
        nc, m = self.nc, self.m
        pool.sem_inc(self.scattered, 1)
        self.ring.split_lo(pool, 0, nc.gpsimd)
        for t in range(NT):
            pool.wait_ge(self.rows_in[t], 32)
            nc.gpsimd.tensor_tensor(m.x[:, t], m.x[:, t], m.x_odd[t // 2][:, t % 2], ALU.add).then_inc(self.row_sum, 1)
        for t in range(NT - 1):
            self.norm.shift(pool, t)

    def tensor(self, pe):
        nc, m, ps, ring, MAIN = self.nc, self.m, self.ps, self.ring, self.MAIN

        def turn(t):
            pe.wait_ge(self.row_sum, t + 1)
            if t >= 2:
                pe.wait_ge(self.lo_done, t - 1)
            b = self.TURN[t % 2]
            for k in range(KD):
                last = nc.tensor.transpose(ps[:, b + k // 4, (k % 4) * P:(k % 4 + 1) * P], m.x[:, t, k::KD], m.ident[:])
            last.then_inc(self.turned, 1)

        pe.wait_ge(self.p_in, 16)
        for t in range(NT):
            if t >= 2:
                pe.wait_ge(self.pT_ready, t - 1)
            for j in range(2):
                last = nc.tensor.transpose(ps[:, self.PT[t % 2], j * P:(j + 1) * P], m.p[:, t, j::2], m.ident[:])
            last.then_inc(self.p_turned, 1)
        pe.wait_ge(self.pw_in, 16)
        for u in range(2 * NT):
            t, c = divmod(u, 2)
            if c == 0:
                pe.wait_ge(self.pT_ready, t + 1)
            if u >= 2:
                pe.wait_ge(self.p_out, u - 1)
            for j in range(2):
                last = nc.tensor.matmul(ps[:, MAIN[c]], m.pT[:, j, t * P:(t + 1) * P],
                                        m.p_w[:, j * D + c * 512:j * D + (c + 1) * 512],
                                        start=(j == 0), stop=(j == 1))
            last.then_inc(self.p_sum, 1)
            if u == 5:
                turn(0)
        turn(1)
        for u in range(2 * NT):
            t, c = divmod(u, 2)
            if u < 2:
                pe.wait_ge(self.p_out, 2 * NT - 1 + u)
            else:
                pe.wait_ge(self.gate_ready, u - 1)
            if c == 0:
                pe.wait_ge(self.lo_done, t + 1)
            for kk in range(KD):
                i = 2 * c + kk // 4
                if t == 0 and kk % 4 == 0:
                    ring.ready(pe, i)
                last = product3(nc, ps[:, MAIN[c]], m.act_hi[:, kk, t * P:(t + 1) * P],
                                m.act_lo[:, kk, t * P:(t + 1) * P], ring.hi(i)[:, kk % 4],
                                ring.lo(i)[:, kk % 4], kk == 0, kk == KD - 1)
            last.then_inc(self.summed, 1)
            if c == 1 and t + 2 < NT:
                turn(t + 2)

    def scalar(self, act):
        nc, m, ps, ring = self.nc, self.m, self.ps, self.ring

        def high_part(t):
            act.wait_ge(self.turned, t + 1)
            nc.scalar.activation(m.act_hi[:, :, t * P:(t + 1) * P], self.turned_view(t),
                                 ACT.Copy).then_inc(self.hi_done, 1)

        for t in range(NT):
            act.wait_ge(self.p_turned, t + 1)
            nc.scalar.activation(m.pT[:, :, t * P:(t + 1) * P],
                                 ps[:, self.PT[t % 2], 0:2 * P].rearrange("p (j n) -> p j n", n=P),
                                 ACT.Copy).then_inc(self.pT_ready, 1)
        ring.split_hi(act, 0)
        ring.split_hi(act, 1)
        high_part(0)
        high_part(1)
        ring.split_hi(act, 2)
        ring.split_hi(act, 3)
        for t in range(NT):
            for u in (2 * t, 2 * t + 1):
                act.wait_ge(self.summed, u + 1)
                if u >= 2:
                    act.wait_ge(self.added, u - 1)
                nc.scalar.activation(m.gate_out[:, u % 2], ps[:, self.MAIN[u % 2]],
                                     ACT.Sigmoid).then_inc(self.gate_ready, 1)
            if t + 2 < NT:
                high_part(t + 2)
            self.norm.deviate(act, t)
            self.norm.centre(act, t)

    def vector(self, dve):
        nc, m, ps, ring = self.nc, self.m, self.ps, self.ring

        def low_part(t):
            dve.wait_ge(self.hi_done, t + 1)
            nc.vector.tensor_tensor(m.act_lo[:, :, t * P:(t + 1) * P], self.turned_view(t),
                                    m.act_hi[:, :, t * P:(t + 1) * P].bitcast(F32),
                                    ALU.subtract).then_inc(self.lo_done, 1)

        for t in range(NT):
            for c in range(2):
                dve.wait_ge(self.p_sum, 2 * t + c + 1)
                nc.vector.tensor_copy(m.pp[:, t, c * 512:(c + 1) * 512], ps[:, self.MAIN[c]]).then_inc(self.p_out, 1)
            if t == 2:
                dve.wait_ge(ring.lo_split, 1)
                ring.split_lo(dve, 1)
        low_part(0)
        ring.split_lo(dve, 2)
        low_part(1)
        ring.split_lo(dve, 3)
        for t in range(NT):
            for c in range(2):
                u = 2 * t + c
                cols = slice(c * 512, (c + 1) * 512)
                dve.wait_ge(self.gate_ready, u + 1)
                nc.vector.tensor_tensor(m.gate_out[:, c], m.gate_out[:, c], m.pp[:, t, cols],
                                        ALU.mult).then_inc(self.gate_used, 1)
                dve.wait_ge(self.gate_used, u + 1)
                nc.vector.tensor_tensor(m.x[:, t, cols], m.x[:, t, cols], m.gate_out[:, c],
                                        ALU.add).then_inc(self.added, 1)
            dve.wait_ge(self.added, 2 * t + 2)
            self.norm.statistics(dve, t)
            if t + 2 < NT:
                low_part(t + 2)
            self.norm.finish(dve, t)
            self.norm.gain(dve, t)
        dve.wait_ge(self.norm_semaphores.normed, self.norm.before + NT - 1)
        self.norm.shift(dve, NT - 1, nc.vector)


def encoder_block(nc, a, out, CAP=SLOTS):
    h0 = nc.dram_tensor("h0_rows", [SEQ, D], F32, kind="Internal").ap()
    h1 = nc.dram_tensor("h1_rows", [SEQ, D], F32, kind="Internal").ap()
    acc_dram = nc.dram_tensor("residual_rows", [SEQ, D], F32, kind="Internal").ap()
    acc_odd_dram = nc.dram_tensor("odd_rows", [SEQ, D], F32, kind="Internal").ap()
    m = Memory(nc, (nc.sbuf_base + 31) // 32 * 32, CAP)
    with ExitStack() as ctx:
        ps = ctx.enter_context(nc.psum_tensor("ps", [P, 8, 512], F32))
        norm = NormSemaphores(nc, ctx)
        ring = WeightRing(nc, m, ctx, "dense", dense_pieces(a), [m.raw[:, i] for i in range(NRAW)])
        embedding = Embedding(nc, m, ps, ctx, norm, a, acc_dram, acc_odd_dram, out[0])
        make_constants(nc, m)
        input_norm_block(nc, m, ps, norm, a, h0, ring)
        mix_block(nc, m, ps, a, ring)
        out_block(nc, m, ps, norm, a, h0, h1, ring)
        routing_block(nc, m, ps, a, acc_dram, acc_odd_dram, ring)
        experts_block(nc, m, ps, a, h1, acc_dram, acc_odd_dram, CAP, embedding)


_INS = ["x", "p", "ln_in_g", "ln_in_b", "w_in", "sg_ln_g", "sg_ln_b", "sg_w_s", "sg_b_s", "w_branch_a", "w_branch_b",
        "w_out", "ln1_g", "ln1_b", "router_w", "router_bias", "moe_w_gate", "moe_w_up", "moe_w_down", "sh_w_gate",
        "sh_w_up", "sh_w_down", "ple_w_proj", "ple_w_gate", "ln2_g", "ln2_b"]


def kernel(**inputs):
    import numpy as _np
    import concourse.bacc as _bacc
    from concourse import mybir as _mybir
    from concourse.bass_utils import run_bass_kernel_spmd as _run

    nc = _bacc.Bacc("TRN2", target_bir_lowering=False, num_devices=1)
    arrays, args = {}, {}
    for name in _INS:
        v = _np.ascontiguousarray(inputs[name])
        arrays[f"in_{name}"] = v
        args[name] = nc.dram_tensor(f"in_{name}", v.shape, _mybir.dt.from_np(v.dtype), kind="ExternalInput").ap()
    out = nc.dram_tensor("out_h", [1, SEQ, D], F32, kind="ExternalOutput").ap()
    encoder_block(nc, args, out)
    r = _run(nc, [arrays], core_ids=[0])
    return r.results[0]["out_h"]
```

```python
from contextlib import ExitStack

import concourse.bass as bass
from concourse import mybir

P = 128
D = 1024
SEQ = 512
NT = SEQ // P
KD = D // P
SG = 512
SGG = 4
HEADS = 8
HD = 64
NE = 64
NGRP = 8
FF = 256
PLE = 256
LN_EPS = 1e-5
ALPHA = 2.0 ** 0.25
ROUTED_SCALE = 2.5
SLOTS = 96
FAR = 4096.0
HC = 2048
NSPLIT = 4
NRAW = 2
DENSE_PIECES = 26

F32 = mybir.dt.float32
F32R = mybir.dt.float32r
BF16 = mybir.dt.bfloat16
U32 = mybir.dt.uint32
I32 = mybir.dt.int32
ALU = mybir.AluOpType
ACT = mybir.ActivationFunctionType
AX = mybir.AxisListType.X
KB = 1024


class Memory:

    def __init__(self, nc, base, cap):
        def at(name, shape, dtype, kib):
            return nc.alloc_sbuf_tensor_at(name, shape, dtype, offset=base + int(kib * KB))

        self.raw = at("raw", [P, NRAW, HC], F32, 0)
        self.w_hi = at("w_hi", [P, NSPLIT, HC], F32R, 16)
        self.w_lo = at("w_lo", [P, NSPLIT, HC], F32R, 48)
        self.act_hi = at("act_hi", [P, KD, SEQ], F32R, 80)
        self.act_lo = at("act_lo", [P, KD, SEQ], F32R, 96)
        self.qT = at("qT", [P, 4, SEQ], F32, 112)
        self.kT = at("kT", [P, 4, SEQ], F32, 120)
        self.ybT_hi = at("ybT_hi", [P, 4, SEQ], F32R, 112)
        self.ybT_lo = at("ybT_lo", [P, 4, SEQ], F32R, 120)
        self.vsb = at("vsb", [P, NT, 512], F32, 128)
        self.merged = at("merged", [P, NT, D], F32, 136)
        self.yaT_hi = at("yaT_hi", [P, 4, SEQ], F32R, 152)
        self.yaT_lo = at("yaT_lo", [P, 4, SEQ], F32R, 160)
        self.x = at("x_rows", [P, NT, D], F32, 152)
        self.yb = at("yb", [P, NT, 512], F32, 168)
        self.ln_g = at("ln_g", [P, D], F32, 168)
        self.ln_b = at("ln_b", [P, D], F32, 172)
        self.sig_neg = at("sig_neg", [P, 2, 512], F32, 176)
        self.sig_pos = at("sig_pos", [P, 2, 512], F32, 180)
        self.stick = at("stick", [P, 2, 520], F32, 184)
        self.aT = at("aT", [P, 2, 512], F32, 189)
        self.gate = at("gate", [P, 2, 512], F32, 193)
        self.sg_wT = at("sg_wT", [P, SGG, P], F32, 197)
        self.sg_b = at("sg_b", [P, SGG], F32, 199)
        self.sg_w = at("sg_w", [P, SGG, P], F32, 189)
        self.sg_g = at("sg_g", [P, SG], F32, 176)
        self.sg_bb = at("sg_bb", [P, SG], F32, 178)
        self.ident = at("ident", [P, P], F32, 201)
        self.ident_bf = at("ident_bf", [P, P], BF16, 201.5)
        self.future_bf = at("future_bf", [P, P], BF16, 201.75)
        self.earlier_bf = at("earlier_bf", [P, P], BF16, 202)
        self.ones_bf = at("ones_bf", [P, P], BF16, 202.25)
        self.lower_grp = at("lower_grp", [P, NGRP, NGRP], F32, 202.5)
        self.slots = at("slots", [P, SEQ + P], F32, 202.75)
        self.stats = at("stats", [P, NT, 2, 6], F32, 205.25)
        self.mv = at("mv", [P, NT, 2], F32, 205.5)
        self.rstd = at("rstd", [P, NT, 1], F32, 205.625)
        self.nmr = at("nmr", [P, NT, 1], F32, 205.75)
        self.eps = at("eps", [P, 1], F32, 206.125)
        self.peak = at("peak", [P, 1], F32, 205.875)
        self.peak_i = at("peak_i", [P, 1], I32, 206)
        self.sh_down = at("sh_down", [P, HC], F32, 0)
        self.sh_h = at("sh_h", [P, NT, FF], F32, 8)
        self.sh_hT = at("sh_hT", [P, 2, SEQ], F32, 12)
        self.router = at("router", [P, KD, NE], F32, 184)
        self.r_hi = at("r_hi", [P, KD, NE], F32R, 186)
        self.r_lo = at("r_lo", [P, KD, NE], F32R, 188)
        self.r_bias = at("r_bias", [P, NE], F32, 190)
        self.score = at("score", [P, NT, NE], F32, 190.25)
        self.sel = at("sel", [P, NT, NE], F32, 191.25)
        self.top = at("top", [P, NT, NGRP, 8], F32, 192.25)
        self.grp = at("grp", [P, NT, NGRP], F32, 193.25)
        self.beats = at("beats", [P, NT, NGRP, NGRP], F32, 193.5)
        self.ties = at("ties", [P, NT, NGRP, NGRP], F32, 194.5)
        self.rank = at("rank", [P, NT, NGRP], F32, 195.5)
        self.top8 = at("top8", [P, NT, 8], F32, 195.75)
        self.rest = at("rest", [P, NT, NE], F32, 196)
        self.pick_bf = at("pick_bf", [P, NT, NE], BF16, 197)
        self.den = at("den", [P, NT], F32, 197.5)
        self.logit = at("logit", [P, SEQ], F32, 198)
        self.slot_of = at("slot_of", [P, NT, NE], F32, 176)
        self.tags = at("tags", [P, NT, NE, 6], BF16, 177)
        self.found = at("found", [P, NE, 2], F32, 180)
        self.get_idx = [at(f"get_idx{i}", [P, 1], U32, 180.5 + i * 0.0625) for i in range(4)]
        self.put_idx = [at(f"put_idx{i}", [P, 1], U32, 180.75 + i * 0.0625) for i in range(2)]
        self.gu_raw = at("gu_raw", [P, 4, HC], F32, 112)
        self.dn_raw = at("dn_raw", [P, 2, HC], F32, 184)
        self.dn_hi = at("dn_hi", [P, 2, HC], F32R, 0)
        self.dn_lo = at("dn_lo", [P, 2, HC], F32R, 160)
        self.xg = [at(f"xg{i}", [P, D], F32, 144 + 4 * i) for i in range(4)]
        self.xgT_hi = at("xgT_hi", [P, 2, KD * cap], F32R, 80)
        self.xgT_lo = at("xgT_lo", [P, 2, KD * cap], F32R, 88)
        self.silu = at("silu", [P, 2, FF], F32, 96)
        self.h = at("h_ff", [P, 2, FF], F32, 98)
        self.hT_hi = at("hT_hi", [P, 2, 2 * cap], F32R, 100)
        self.hT_lo = at("hT_lo", [P, 2, 2 * cap], F32R, 181)
        self.y = [at(f"y{i}", [P, D], F32, 102 + 4 * i) for i in range(2)]
        self.onehot = at("onehot", [P, 2, NT, cap], BF16, 182.5)
        self.p = at("p_rows", [P, NT, PLE], F32, 112)
        self.pT = at("pT", [P, 2, SEQ], F32, 116)
        self.p_w = at("p_w", [P, HC], F32, 120)
        self.gate_out = at("gate_out", [P, 2, 512], F32, 112)
        self.pp = at("pp", [P, NT, D], F32, 0)
        self.x_odd = [at(f"x_odd{i}", [P, 2, D], F32, kib) for i, kib in enumerate((144, 176))]
        self.ple_raw = [at(f"ple_raw{i}", [P, HC], F32, kib)[:] for i, kib in enumerate((128, 136, 184, 192))]


def set_constants(nc, m, pool, base_set, constants_set):
    nc.gpsimd.memset(m.ident[:], 0.0).then_inc(base_set, 1)
    nc.gpsimd.memset(m.ident_bf[:], 0.0).then_inc(base_set, 1)
    nc.gpsimd.memset(m.future_bf[:], 0.0).then_inc(base_set, 1)
    nc.gpsimd.memset(m.earlier_bf[:], 1.0).then_inc(base_set, 1)
    nc.gpsimd.memset(m.ones_bf[:], 1.0).then_inc(base_set, 1)
    nc.gpsimd.memset(m.lower_grp[:], 1.0).then_inc(base_set, 1)
    nc.gpsimd.memset(m.eps[:], LN_EPS).then_inc(base_set, 1)
    pool.wait_ge(base_set, 7)
    for eye in (m.ident, m.ident_bf):
        nc.gpsimd.affine_select(out=eye[:], in_=eye[:], compare_op=ALU.not_equal, fill=1.0, base=0,
                                pattern=[[-1, P]], channel_multiplier=1)
    nc.gpsimd.affine_select(out=m.future_bf[:], in_=m.future_bf[:], compare_op=ALU.is_gt, fill=-1e30,
                            base=0, pattern=[[-1, P]], channel_multiplier=1)
    nc.gpsimd.affine_select(out=m.earlier_bf[:], in_=m.earlier_bf[:], compare_op=ALU.is_gt, fill=0.0,
                            base=0, pattern=[[1, P]], channel_multiplier=-1)
    nc.gpsimd.affine_select(out=m.lower_grp[:], in_=m.lower_grp[:], compare_op=ALU.is_gt, fill=0.0,
                            base=0, pattern=[[1, NGRP], [-1, NGRP]], channel_multiplier=0).then_inc(constants_set, 1)
    nc.gpsimd.iota(m.slots[:], pattern=[[1, SEQ + P]], base=0, channel_multiplier=0,
                   allow_small_or_imprecise_dtypes=True)


def deviation(nc, m, t):
    return nc.scalar.activation(m.rstd[:, t], m.mv[:, t, 1:2], ACT.Sqrt, bias=m.eps[:])


def scale_and_shift(nc, m, chained, t):
    chained(nc.vector.reciprocal(m.rstd[:, t], m.rstd[:, t]))
    return nc.vector.scalar_tensor_tensor(out=m.nmr[:, t], in0=m.mv[:, t, 0:1], scalar=-1.0, in1=m.rstd[:, t],
                                          op0=ALU.mult, op1=ALU.mult)


class NormSemaphores:

    def __init__(self, nc, ctx):
        def sem(name):
            return ctx.enter_context(nc.semaphore(f"norm_{name}"))

        self.rows_in = [sem(f"rows_in{t}") for t in range(NT)]
        self.affine_in, self.rows_out = sem("affine_in"), sem("rows_out")
        self.moments, self.rooted, self.stats_done = sem("moments"), sem("rooted"), sem("stats_done")
        self.scaled, self.gained, self.normed, self.turned = sem("scaled"), sem("gained"), sem("normed"), sem("turned")
        self.hi_done, self.lo_done, self.chain = sem("hi_done"), sem("lo_done"), sem("chain")
        self.norms = 0
        self.links = 0


class RowNorm:

    def __init__(self, nc, m, ps, s, banks=(0,)):
        self.nc, self.m, self.ps, self.s, self.banks = nc, m, ps, s, banks
        self.before = s.norms * NT
        self.affine_count = 32 * (s.norms + 1)
        s.norms += 1

    def load_affine(self, sp, gain, bias):
        sp.dma_start(self.m.ln_g[:], gain.partition_broadcast(P)).then_inc(self.s.affine_in, 16)
        sp.dma_start(self.m.ln_b[:], bias.partition_broadcast(P)).then_inc(self.s.affine_in, 16)

    def store(self, sp, t, rows):
        sp.wait_ge(self.s.normed, self.before + t + 1)
        sp.dma_start(rows[t * P:(t + 1) * P, :], self.m.x[:, t]).then_inc(self.s.rows_out, 16)

    def stored(self, sp):
        sp.wait_ge(self.s.rows_out, 16 * (self.before + NT))

    def chained(self, dve, ins):
        self.s.links += 1
        ins.then_inc(self.s.chain, 1)
        dve.wait_ge(self.s.chain, self.s.links)

    def half_statistics(self, dve, t, c):
        nc, m = self.nc, self.m
        stats = nc.vector.bn_stats(m.stats[:, t, c], m.x[:, t, c * 512:(c + 1) * 512])
        if c == 1:
            self.chained(dve, stats)
            nc.vector.bn_aggr(m.mv[:, t], m.stats[:, t]).then_inc(self.s.moments, 1)

    def statistics(self, dve, t):
        self.half_statistics(dve, t, 0)
        self.half_statistics(dve, t, 1)

    def deviate(self, act, t):
        act.wait_ge(self.s.moments, self.before + t + 1)
        deviation(self.nc, self.m, t).then_inc(self.s.rooted, 1)

    def finish(self, dve, t):
        dve.wait_ge(self.s.rooted, self.before + t + 1)
        scale_and_shift(self.nc, self.m, lambda ins: self.chained(dve, ins), t).then_inc(self.s.stats_done, 1)

    def centre(self, act, t):
        m = self.m
        act.wait_ge(self.s.stats_done, self.before + t + 1)
        self.nc.scalar.activation(m.x[:, t], m.x[:, t], ACT.Identity, bias=m.nmr[:, t],
                                  scale=m.rstd[:, t]).then_inc(self.s.scaled, 1)

    def gain(self, dve, t):
        m = self.m
        if t == 0:
            dve.wait_ge(self.s.affine_in, self.affine_count)
        dve.wait_ge(self.s.scaled, self.before + t + 1)
        self.nc.vector.tensor_tensor(m.x[:, t], m.x[:, t], m.ln_g[:], ALU.mult).then_inc(self.s.gained, 1)

    def shift(self, pool, t):
        m = self.m
        if t == 0:
            pool.wait_ge(self.s.affine_in, self.affine_count)
        pool.wait_ge(self.s.gained, self.before + t + 1)
        self.nc.gpsimd.tensor_tensor(m.x[:, t], m.x[:, t], m.ln_b[:], ALU.add).then_inc(self.s.normed, 1)

    def finish_on_vector(self, dve, t):
        nc, m, s, count = self.nc, self.m, self.s, self.before + t + 1
        if t == 0:
            dve.wait_ge(s.affine_in, self.affine_count)
        dve.wait_ge(s.moments, count)
        nc.vector.scalar_tensor_tensor(out=m.x[:, t], in0=m.x[:, t], scalar=m.mv[:, t, 0:1], in1=m.ln_g[:],
                                       op0=ALU.subtract, op1=ALU.mult).then_inc(s.scaled, 1)
        dve.wait_ge(s.rooted, count)
        nc.vector.reciprocal(m.rstd[:, t], m.rstd[:, t]).then_inc(s.stats_done, 1)
        dve.wait_ge(s.scaled, count)
        dve.wait_ge(s.stats_done, count)
        if t:
            dve.wait_ge(s.normed, count - 1)
        dve.sem_inc(s.gained, 1)
        nc.vector.scalar_tensor_tensor(out=m.x[:, t], in0=m.x[:, t], scalar=m.rstd[:, t], in1=m.ln_b[:],
                                       op0=ALU.mult, op1=ALU.add).then_inc(s.normed, 1)

    def view(self, t):
        b = self.banks[t % len(self.banks)]
        return self.ps[:, b:b + 2].rearrange("p b (k n) -> p (b k) n", n=P)

    def turn(self, pe, t):
        b = self.banks[t % len(self.banks)]
        pe.wait_ge(self.s.normed, self.before + t + 1)
        if t >= len(self.banks):
            pe.wait_ge(self.s.lo_done, self.before + t + 1 - len(self.banks))
        for k in range(KD):
            last = self.nc.tensor.transpose(self.ps[:, b + k // 4, (k % 4) * P:(k % 4 + 1) * P],
                                            self.m.x[:, t, k::KD], self.m.ident[:])
        last.then_inc(self.s.turned, 1)

    def high_part(self, act, t):
        act.wait_ge(self.s.turned, self.before + t + 1)
        self.nc.scalar.activation(self.m.act_hi[:, :, t * P:(t + 1) * P], self.view(t),
                                  ACT.Copy).then_inc(self.s.hi_done, 1)

    def low_part(self, dve, t):
        m = self.m
        dve.wait_ge(self.s.hi_done, self.before + t + 1)
        self.nc.vector.tensor_tensor(m.act_lo[:, :, t * P:(t + 1) * P], self.view(t),
                                     m.act_hi[:, :, t * P:(t + 1) * P].bitcast(F32),
                                     ALU.subtract).then_inc(self.s.lo_done, 1)


def dense_pieces(a):
    def columns(w, k, c, half):
        rows = k // 2
        return w.rearrange("(p k) n -> p k n", p=P)[:, half * rows:(half + 1) * rows, c * 512:(c + 1) * 512]

    w_in, w_a, w_b, w_out = a["w_in"][0], a["w_branch_a"][0], a["w_branch_b"][0], a["w_out"][0]
    pieces = []
    for c in range(5):
        pieces += [columns(w_in, KD, c, 0), columns(w_in, KD, c, 1)]
    for c, w in ((0, w_a), (1, w_a), (2, w_b), (3, w_b)):
        pieces += [columns(w_in, KD, 5 + c, 0), columns(w_in, KD, 5 + c, 1)]
        pieces.append(w.rearrange("(p k) n -> p k n", p=P)[:, :, (c % 2) * 512:(c % 2 + 1) * 512])
    for c in range(2):
        pieces += [columns(w_out, KD, c, 0), columns(w_out, KD, c, 1)]
    assert len(pieces) == DENSE_PIECES
    for half in range(2):
        pieces.append(tuple(a[name][0].rearrange("(p k) n -> p k n", p=P)[:, 4 * half:4 * half + 4]
                            for name in ("sh_w_gate", "sh_w_up")))
    return pieces


class WeightRing:

    def __init__(self, nc, m, ctx, tag, pieces, raw):
        self.nc, self.m, self.pieces, self.raw = nc, m, pieces, raw
        self.slots = len(raw)
        self.loaded = [ctx.enter_context(nc.semaphore(f"{tag}_loaded{i}")) for i in range(self.slots)]
        self.hi_split = ctx.enter_context(nc.semaphore(f"{tag}_hi_split"))
        self.lo_split = ctx.enter_context(nc.semaphore(f"{tag}_lo_split"))
        self.freed = {}

    def load(self, sp, i):
        if i >= self.slots:
            sp.wait_ge(self.lo_split, i - self.slots + 1)
        dst = self.raw[i % self.slots].rearrange("p (k n) -> p k n", n=512)
        src = self.pieces[i]
        if not isinstance(src, tuple):
            sp.dma_start(dst, src).then_inc(self.loaded[i % self.slots], 16)
        else:
            sp.dma_start(dst[:, :, 0:FF], src[0]).then_inc(self.loaded[i % self.slots], 16)
            sp.dma_start(dst[:, :, FF:512], src[1]).then_inc(self.loaded[i % self.slots], 16)

    def loads_of(self, i):
        return 16 * sum(1 + isinstance(self.pieces[j], tuple) for j in range(i % self.slots, i + 1, self.slots))

    def split_hi(self, act, i):
        act.wait_ge(self.loaded[i % self.slots], self.loads_of(i))
        if i >= NSPLIT:
            act.wait_ge(*self.freed[i - NSPLIT])
        self.nc.scalar.activation(self.m.w_hi[:, i % NSPLIT], self.raw[i % self.slots],
                                  ACT.Copy).then_inc(self.hi_split, 1)

    def split_lo(self, eng, i, unit=None):
        eng.wait_ge(self.hi_split, i + 1)
        (unit or self.nc.vector).tensor_tensor(self.m.w_lo[:, i % NSPLIT], self.raw[i % self.slots],
                                     self.m.w_hi[:, i % NSPLIT].bitcast(F32),
                                     ALU.subtract).then_inc(self.lo_split, 1)

    def ready(self, pe, i):
        pe.wait_ge(self.lo_split, i + 1)

    def hi(self, i):
        return self.m.w_hi[:, i % NSPLIT].rearrange("p (k n) -> p k n", n=512)

    def lo(self, i):
        return self.m.w_lo[:, i % NSPLIT].rearrange("p (k n) -> p k n", n=512)


def product3(nc, out, x_hi, x_lo, w_hi, w_lo, first, last):
    nc.tensor.matmul(out, x_hi, w_hi, start=first, stop=False)
    nc.tensor.matmul(out, x_hi, w_lo, start=False, stop=False)
    return nc.tensor.matmul(out, x_lo, w_hi, start=False, stop=last)


class Expert:

    def __init__(self, r, quad, q):
        quad, q = quad + q // 4, q % 4
        self.r, self.quad, self.q = r, quad, q
        self.e = 4 * quad + q
        self.b = q % 2
        self.it = r * NE + self.e
        self.turn4 = r * (NE // 4) + quad + 1
        self.turn2 = r * (NE // 2) + 2 * quad + q // 2 + 1

    def next(self, n):
        return Expert(self.r, self.quad, self.q + n)


class FirstExperts:

    def __init__(self, nc, m, ctx, a, acc_odd_dram):
        def sem(name):
            return ctx.enter_context(nc.semaphore(f"moe_{name}"))

        self.nc, self.m, self.acc_odd = nc, m, acc_odd_dram
        self.weights = (a["moe_w_gate"][0], a["moe_w_up"][0])
        self.gu_in = [[sem(f"gu_in{b}{half}") for half in range(2)] for b in range(2)]
        self.put = [sem("put_even"), sem("put_odd")]
        self.cleared = sem("cleared")

    def load_half(self, sp, x, half):
        dst = self.m.gu_raw[:, 2 * x.b + half].rearrange("p (w n) -> p w n", w=2)
        for w, src in enumerate(self.weights):
            rows = src[bass.ds(x.e, 1)].rearrange("o (p k) n -> p o (k n)", p=P)
            sp.dma_start(dst[:, w:w + 1], rows[:, :, half * (HC // 2):(half + 1) * (HC // 2)]) \
              .then_inc(self.gu_in[x.b][half], 16)

    def load_gate_up(self, sp, x):
        self.load_half(sp, x, 0)
        self.load_half(sp, x, 1)

    def clear(self, pool, q):
        self.nc.gpsimd.memset(self.m.xg[q][:], 0.0).then_inc(self.cleared, 1)

    def store_zeros(self, pool):
        pool.wait_ge(self.cleared, 1)
        for t in range(NT):
            self.nc.gpsimd.dma_start(self.acc_odd[t * P:(t + 1) * P, :], self.m.xg[0][:]).then_inc(self.put[1], 16)


class MergedTurn:

    BANKS = (3, 5)

    def __init__(self, nc, m, ps, ctx):
        self.nc, self.m, self.ps = nc, m, ps
        self.turned, self.hi_done, self.lo_done, self.rows_in = (
            ctx.enter_context(nc.semaphore(f"merged_{n}")) for n in ("turned", "hi_done", "lo_done", "rows_in"))

    def view(self, t):
        b = self.BANKS[t % 2]
        return self.ps[:, b:b + 2].rearrange("p b (k n) -> p (b k) n", n=P)

    def turn(self, pe, t):
        if t >= 2:
            pe.wait_ge(self.lo_done, t - 1)
        b = self.BANKS[t % 2]
        for k in range(KD):
            last = self.nc.tensor.transpose(self.ps[:, b + k // 4, (k % 4) * P:(k % 4 + 1) * P],
                                            self.m.merged[:, t, k::KD], self.m.ident[:])
        last.then_inc(self.turned, 1)

    def high_part(self, act, t):
        act.wait_ge(self.turned, t + 1)
        self.nc.scalar.activation(self.m.act_hi[:, :, t * P:(t + 1) * P], self.view(t), ACT.Copy).then_inc(self.hi_done, 1)

    def low_part(self, dve, t):
        dve.wait_ge(self.hi_done, t + 1)
        self.nc.vector.tensor_tensor(self.m.act_lo[:, :, t * P:(t + 1) * P], self.view(t),
                                     self.m.act_hi[:, :, t * P:(t + 1) * P].bitcast(F32),
                                     ALU.subtract).then_inc(self.lo_done, 1)


def mix_block(nc, m, ps, norm_semaphores, a, h0, ring, merged_turn):
    MAIN, SIDE, Z, TURN, YB = (0, 1), 2, (3, 4), (5, 6), 7
    NA = NT * HEADS
    with ExitStack() as ctx:
        def sem(name):
            return ctx.enter_context(nc.semaphore(f"mix_{name}"))

        half_used, projected, gelu_out, copied = sem("half_used"), sem("projected"), sem("gelu_out"), sem("copied")
        small_in = sem("small_in")
        sg_turned, sg_w_ready = sem("sg_turned"), sem("sg_w_ready")
        v_moments, v_rooted = sem("v_moments"), sem("v_rooted")
        v_stats, v_scaled, v_normed = sem("v_stats"), sem("v_scaled"), sem("v_normed")
        gated, ya_ready = sem("gated"), sem("ya_ready")
        ya_turned, ya_hi, ya_lo = sem("ya_turned"), sem("ya_hi"), sem("ya_lo")
        z_ready, sig_ready, a_ready = sem("z_ready"), sem("sig_ready"), sem("a_ready")
        a_turned, aT_ready, av_done = sem("a_turned"), sem("aT_ready"), sem("av_done")
        yb_ready = sem("yb_ready")
        yb_turned, yb_hi, yb_lo = sem("yb_turned"), sem("yb_hi"), sem("yb_lo")
        gate_sum, branch_sum, gate_ready, merged = sem("gate_sum"), sem("branch_sum"), sem("gate_ready"), sem("merged")
        chain, base_set, constants_set = sem("chain"), sem("base_set"), sem("constants_set")
        norm = RowNorm(nc, m, ps, norm_semaphores, banks=(3, 5))
        for c in range(5):
            ring.freed[2 * c], ring.freed[2 * c + 1] = (half_used, c + 1), (projected, 4 * c + 4)
        for j in range(4):
            ring.freed[10 + 3 * j] = (half_used, 5 + j + 1)
            ring.freed[11 + 3 * j], ring.freed[12 + 3 * j] = (gate_sum, 4 * j + 4), (branch_sum, 4 * j + 4)
        block = ctx.enter_context(nc.Block())

        SPLIT_AFTER_STEP = {13: (14,), 15: (15,), 16: (16,), 29: (17,), 31: (18, 19)}
        SPLIT_AFTER_GATE = {10: (20,), 11: (21,), 12: (22,)}

        LAST_BEFORE_H0 = DENSE_PIECES - 6

        def width(s):
            return (s // HEADS + 1) * P

        @block.sync
        def _(sp):
            for t in range(NT):
                sp.dma_start(m.x[:, t], a["x"][0][t * P:(t + 1) * P, :]).then_inc(norm_semaphores.rows_in[t], 16)
                if t == 1:
                    norm.load_affine(sp, a["ln_in_g"], a["ln_in_b"])
            ring.load(sp, 0)
            ring.load(sp, 1)
            sp.dma_start(m.sg_w[:], a["sg_w_s"][0].rearrange("g i j -> i g j")).then_inc(small_in, 16)
            sp.dma_start(m.sg_g[:], a["sg_ln_g"][0].partition_broadcast(P)).then_inc(small_in, 16)
            sp.dma_start(m.sg_bb[:], a["sg_ln_b"][0].partition_broadcast(P)).then_inc(small_in, 16)
            sp.dma_start(m.sg_b[:], a["sg_b_s"][0].rearrange("g i -> i g"),
                         allow_slow_non_contiguous=True).then_inc(small_in, 16)
            for t in range(NT):
                norm.store(sp, t, h0)
            for i in range(2, DENSE_PIECES):
                ring.load(sp, i)
                if i == LAST_BEFORE_H0:
                    norm.stored(sp)
                    sp.wait_ge(branch_sum, 8)
                    for t in range(NT):
                        sp.dma_start(m.x[:, t], h0[t * P:(t + 1) * P, :]).then_inc(merged_turn.rows_in, 16)

        @block.gpsimd
        def _(pool):
            set_constants(nc, m, pool, base_set, constants_set)
            for t in range(NT):
                norm.shift(pool, t)

        @block.tensor
        def _(pe):
            def unit_start(u):
                if u - 2 >= 8:
                    pe.wait_ge(copied, u - 2 - 8 + 1)
                elif u - 2 >= 0:
                    pe.wait_ge(gelu_out, u - 2 + 1)

            def rows_unit(u, c, t):
                unit_start(u)
                for half in range(2):
                    i = 2 * c + half
                    if t == 0:
                        ring.ready(pe, i)
                    for k in range(4):
                        kk = 4 * half + k
                        last = product3(nc, ps[:, MAIN[u % 2]], m.act_hi[:, kk, t * P:(t + 1) * P],
                                        m.act_lo[:, kk, t * P:(t + 1) * P], ring.hi(i)[:, k], ring.lo(i)[:, k],
                                        kk == 0, kk == KD - 1)
                    if half == 0 and t == NT - 1:
                        last.then_inc(half_used, 1)
                last.then_inc(projected, 1)

            def features_unit(u, c, f):
                unit_start(u)
                for half in range(2):
                    i = 2 * c + half
                    if f == 0:
                        ring.ready(pe, i)
                    cols = slice(f * P, (f + 1) * P)
                    for k in range(4):
                        kk = 4 * half + k
                        last = product3(nc, ps[:, MAIN[u % 2]], ring.hi(i)[:, k, cols], ring.lo(i)[:, k, cols],
                                        m.act_hi[:, kk], m.act_lo[:, kk], kk == 0, kk == KD - 1)
                    if half == 0 and f == 3:
                        last.then_inc(half_used, 1)
                last.then_inc(projected, 1)

            pe.wait_ge(constants_set, 1)
            for t in range(NT):
                norm.turn(pe, t)
            for t in range(NT):
                pe.wait_ge(norm_semaphores.lo_done, t + 1)
                rows_unit(t, 0, t)
            pe.wait_ge(small_in, 64)
            for g in range(SGG):
                last = nc.tensor.transpose(ps[:, YB, g * P:(g + 1) * P], m.sg_w[:, g], m.ident[:])
            last.then_inc(sg_turned, 1)
            for t in range(NT):
                rows_unit(4 + t, 1, t)
            for f in range(4):
                features_unit(8 + f, 2, f)

            def spatial(t):
                pe.wait_ge(v_normed, t + 1)
                if t >= 2:
                    pe.wait_ge(ya_ready, t - 1)
                for g in range(SGG):
                    last = nc.tensor.matmul(ps[:, Z[t % 2], g * P:(g + 1) * P], m.sg_wT[:, g],
                                            m.merged[:, t, SG + g * P:SG + (g + 1) * P], start=True, stop=True)
                last.then_inc(gated, 1)

            def turn_ya(t):
                pe.wait_ge(ya_ready, t + 1)
                if t >= 2:
                    pe.wait_ge(ya_lo, t - 1)
                for k in range(4):
                    last = nc.tensor.transpose(ps[:, TURN[t % 2], k * P:(k + 1) * P],
                                               m.merged[:, t, k:SG:4], m.ident[:])
                last.then_inc(ya_turned, 1)

            pe.wait_ge(sg_w_ready, 1)
            spatial(0)
            spatial(1)
            features_unit(12, 3, 0)
            spatial(2)
            features_unit(13, 3, 1)
            spatial(3)
            features_unit(14, 3, 2)
            turn_ya(0)
            turn_ya(1)
            features_unit(15, 3, 3)
            turn_ya(2)
            turn_ya(3)
            for t in range(NT):
                rows_unit(16 + t, 4, t)

            def gate_part(g, part):
                j, t = divmod(g, NT)
                bank = MAIN[g % 2]
                i = 10 + 3 * j + part // 2
                if part == 0:
                    if g < 2:
                        pe.wait_ge(copied, 12 - 1 + g)
                    else:
                        pe.wait_ge(gate_ready, g - 1)
                if t == 0 and part % 2 == 0:
                    ring.ready(pe, i)
                for k in (2 * (part % 2), 2 * (part % 2) + 1):
                    kk = 4 * (part // 2) + k
                    last = product3(nc, ps[:, bank], m.act_hi[:, kk, t * P:(t + 1) * P],
                                    m.act_lo[:, kk, t * P:(t + 1) * P], ring.hi(i)[:, k], ring.lo(i)[:, k],
                                    kk == 0, kk == KD - 1)
                if part == 1 and t == NT - 1:
                    last.then_inc(half_used, 1)
                if part < 3:
                    return
                last.then_inc(gate_sum, 1)
                i += 1
                if t == 0:
                    ring.ready(pe, i)
                if g >= 1:
                    pe.wait_ge(merged, g)
                else:
                    pe.wait_ge(ya_lo, NT)
                y_hi, y_lo = (m.yaT_hi, m.yaT_lo) if j < 2 else (m.ybT_hi, m.ybT_lo)
                if g == 8:
                    pe.wait_ge(yb_lo, NT)
                for k in range(4):
                    last = product3(nc, ps[:, SIDE], y_hi[:, k, t * P:(t + 1) * P], y_lo[:, k, t * P:(t + 1) * P],
                                    ring.hi(i)[:, k], ring.lo(i)[:, k], k == 0, k == 3)
                last.then_inc(branch_sum, 1)

            def scores(s):
                qb, h = divmod(s, HEADS)
                n = width(s)
                if s >= 2:
                    pe.wait_ge(sig_ready, s - 1)
                elif s == 0:
                    pe.wait_ge(copied, 12)
                rows = slice(HD * (h % 2), HD * (h % 2) + HD)
                nc.tensor.matmul(ps[:, Z[s % 2], 0:n], m.qT[rows, h // 2, qb * P:(qb + 1) * P],
                                 m.kT[rows, h // 2, 0:n], start=True, stop=False)
                nc.tensor.matmul(ps[:, Z[s % 2], n - P:n], m.ident_bf[:], m.future_bf[:],
                                 start=False, stop=True).then_inc(z_ready, 1)

            def turn(s):
                pe.wait_ge(a_ready, s + 1)
                if s >= 2:
                    pe.wait_ge(aT_ready, s - 1)
                for c in range(width(s) // P):
                    last = nc.tensor.transpose(ps[:, TURN[s % 2], c * P:(c + 1) * P],
                                               m.sig_pos[:, s % 2, c * P:(c + 1) * P], m.ident[:])
                last.then_inc(a_turned, 1)

            def weighted_values(s):
                qb, h = divmod(s, HEADS)
                pe.wait_ge(aT_ready, s + 1)
                if h == 0 and qb:
                    pe.wait_ge(yb_ready, qb)
                for c in range(qb + 1):
                    last = nc.tensor.matmul(ps[:, YB, h * HD:(h + 1) * HD], m.aT[:, s % 2, c * P:(c + 1) * P],
                                            m.vsb[:, c, h * HD:(h + 1) * HD], start=(c == 0), stop=(c == qb))
                last.then_inc(av_done, 1)

            for s in range(NA + 3):
                if s < NA:
                    scores(s)
                    gate_part(s // 4, s % 4)
                if 2 <= s < NA + 2:
                    turn(s - 2)
                if s >= 3:
                    weighted_values(s - 3)
            for t in range(NT):
                pe.wait_ge(yb_ready, t + 1)
                if t >= 2:
                    pe.wait_ge(yb_lo, t - 1)
                for k in range(4):
                    last = nc.tensor.transpose(ps[:, TURN[t % 2], k * P:(k + 1) * P], m.yb[:, t, k:512:4],
                                               m.ident[:])
                last.then_inc(yb_turned, 1)
            for g in range(8, 16):
                for part in range(4):
                    gate_part(g, part)
                if g >= 14:
                    pe.wait_ge(merged, g - 1)
                    merged_turn.turn(pe, g - 14)

        def turned_view(bank):
            return ps[:, bank].rearrange("p (k n) -> p k n", n=P)

        @block.scalar
        def _(act):
            act.wait_ge(constants_set, 1)
            for t in range(NT):
                norm.deviate(act, t)
                norm.centre(act, t)
                if t == 2:
                    norm.high_part(act, 0)
            ring.split_hi(act, 0)
            norm.high_part(act, 1)
            ring.split_hi(act, 1)
            norm.high_part(act, 2)
            norm.high_part(act, 3)
            for u in range(8):
                t = u % 4
                act.wait_ge(projected, u + 1)
                half = SG * (u // 4)
                nc.scalar.activation(m.merged[:, t, half:half + SG], ps[:, MAIN[u % 2]],
                                     ACT.Gelu_apprx_tanh).then_inc(gelu_out, 1)
                if u < 2:
                    ring.split_hi(act, 2 + u)
                if t >= 2:
                    ring.split_hi(act, 4 + 2 * (u // 4) + t - 2)
            act.wait_ge(v_moments, NT)
            for t in range(NT):
                deviation(nc, m, t).then_inc(v_rooted, 1)
            for t in range(NT):
                act.wait_ge(v_stats, t + 1)
                v = m.merged[:, t, SG:2 * SG]
                nc.scalar.activation(v, v, ACT.Identity, bias=m.nmr[:, t], scale=m.rstd[:, t]).then_inc(v_scaled, 1)

            def high_ya(t):
                act.wait_ge(ya_turned, t + 1)
                nc.scalar.activation(m.yaT_hi[:, :, t * P:(t + 1) * P], turned_view(TURN[t % 2]),
                                     ACT.Copy).then_inc(ya_hi, 1)

            ring.split_hi(act, 8)
            ring.split_hi(act, 9)
            high_ya(0)
            high_ya(1)
            ring.split_hi(act, 10)
            high_ya(2)
            high_ya(3)
            ring.split_hi(act, 11)
            ring.split_hi(act, 12)
            ring.split_hi(act, 13)

            def gate(g):
                act.wait_ge(gate_sum, g + 1)
                if g >= 2:
                    act.wait_ge(merged, g - 1)
                nc.scalar.activation(m.gate[:, g % 2], ps[:, MAIN[g % 2]], ACT.Sigmoid).then_inc(gate_ready, 1)

            for s in range(NA + 3):
                if s < NA:
                    n = width(s)
                    act.wait_ge(z_ready, s + 1)
                    if s >= 2:
                        act.wait_ge(a_turned, s - 1)
                    nc.scalar.activation(m.sig_neg[:, s % 2, 0:n], ps[:, Z[s % 2], 0:n], ACT.Sigmoid,
                                         scale=-HD ** -0.5)
                    nc.scalar.activation(m.sig_pos[:, s % 2, 0:n], ps[:, Z[s % 2], 0:n], ACT.Sigmoid,
                                         scale=HD ** -0.5).then_inc(sig_ready, 1)
                if s >= 2 and s - 2 < NA:
                    r = s - 2
                    act.wait_ge(a_turned, r + 1)
                    if r >= 2:
                        act.wait_ge(av_done, r - 1)
                    nc.scalar.activation(m.aT[:, r % 2, 0:width(r)], ps[:, TURN[r % 2], 0:width(r)],
                                         ACT.Copy).then_inc(aT_ready, 1)
                if s % 4 == 0 and 4 <= s:
                    gate(s // 4 - 1)
                for i in SPLIT_AFTER_STEP.get(s, ()):
                    ring.split_hi(act, i)
            for t in range(NT):
                act.wait_ge(yb_turned, t + 1)
                nc.scalar.activation(m.ybT_hi[:, :, t * P:(t + 1) * P], turned_view(TURN[t % 2]),
                                     ACT.Copy).then_inc(yb_hi, 1)
            for g in range(8, 16):
                gate(g)
                for i in SPLIT_AFTER_GATE.get(g, ()):
                    ring.split_hi(act, i)
                if g == 14:
                    ring.split_hi(act, 23)
                    merged_turn.high_part(act, 0)
            merged_turn.high_part(act, 1)

        @block.vector
        def _(dve):
            done = [0]

            def chained(ins):
                done[0] += 1
                ins.then_inc(chain, 1)
                dve.wait_ge(chain, done[0])

            for t in range(NT):
                dve.wait_ge(norm_semaphores.rows_in[t], 16)
                norm.statistics(dve, t)
                norm.finish(dve, t)
                if t >= 1:
                    norm.gain(dve, t - 1)
            norm.gain(dve, NT - 1)
            norm.low_part(dve, 0)
            ring.split_lo(dve, 0)
            norm.low_part(dve, 1)
            ring.split_lo(dve, 1)
            norm.low_part(dve, 2)
            norm.low_part(dve, 3)
            for i in range(2, 6):
                ring.split_lo(dve, i)
            dve.wait_ge(sg_turned, 1)
            chained(nc.vector.tensor_copy(m.sg_wT[:], ps[:, YB].rearrange("p (g n) -> p g n", n=P)))
            nc.vector.memset(m.sg_wT[HD:P, :, 0:HD], 0.0).then_inc(sg_w_ready, 1)
            for t in range(NT):
                v = m.merged[:, t, SG:2 * SG]
                dve.wait_ge(gelu_out, 4 + t + 1)
                chained(nc.vector.bn_stats(m.stats[:, t, 0], v))
                nc.vector.bn_aggr(m.mv[:, t], m.stats[:, t, 0:1]).then_inc(v_moments, 1)
                if t >= 2:
                    ring.split_lo(dve, 4 + t)
            for t in range(NT):
                dve.wait_ge(v_rooted, t + 1)
                scale_and_shift(nc, m, chained, t).then_inc(v_stats, 1)
            for t in range(NT):
                v = m.merged[:, t, SG:2 * SG]
                dve.wait_ge(v_scaled, t + 1)
                chained(nc.vector.tensor_tensor(v, v, m.sg_g[:], ALU.mult))
                nc.vector.tensor_tensor(v, v, m.sg_bb[:], ALU.add).then_inc(v_normed, 1)

            def copy_out(u, dst):
                dve.wait_ge(projected, u + 1)
                nc.vector.tensor_copy(dst, ps[:, MAIN[u % 2]]).then_inc(copied, 1)

            def gate_u(t):
                dve.wait_ge(gated, t + 1)
                for g in range(SGG):
                    cols = slice(g * P, (g + 1) * P)
                    last = nc.vector.scalar_tensor_tensor(out=m.merged[:, t, cols], in0=ps[:, Z[t % 2], cols],
                                                          scalar=m.sg_b[:, g:g + 1], in1=m.merged[:, t, cols],
                                                          op0=ALU.add, op1=ALU.mult)
                last.then_inc(ya_ready, 1)

            def low_ya(t):
                dve.wait_ge(ya_hi, t + 1)
                nc.vector.tensor_tensor(m.yaT_lo[:, :, t * P:(t + 1) * P], turned_view(TURN[t % 2]),
                                        m.yaT_hi[:, :, t * P:(t + 1) * P].bitcast(F32),
                                        ALU.subtract).then_inc(ya_lo, 1)

            for f in range(4):
                copy_out(8 + f, m.qT[:, f])
            gate_u(0)
            gate_u(1)
            ring.split_lo(dve, 8)
            copy_out(12, m.kT[:, 0])
            gate_u(2)
            ring.split_lo(dve, 9)
            copy_out(13, m.kT[:, 1])
            gate_u(3)
            copy_out(14, m.kT[:, 2])
            low_ya(0)
            low_ya(1)
            ring.split_lo(dve, 10)
            copy_out(15, m.kT[:, 3])
            low_ya(2)
            low_ya(3)
            ring.split_lo(dve, 11)
            for t in range(NT):
                copy_out(16 + t, m.vsb[:, t])
            ring.split_lo(dve, 12)
            ring.split_lo(dve, 13)
            for b in range(2):
                last = nc.vector.memset(m.stick[:, b, P:SEQ + 1:P], 1.0)
            chained(last)

            def merge(g):
                j, t = divmod(g, NT)
                cols = slice((j % 2) * 512, (j % 2 + 1) * 512)
                dve.wait_ge(gate_ready, g + 1)
                dve.wait_ge(branch_sum, g + 1)
                gate = m.gate[:, g % 2]
                if j < 2:
                    nc.vector.tensor_tensor(m.merged[:, t, cols], gate, ps[:, SIDE], ALU.mult).then_inc(merged, 1)
                else:
                    chained(nc.vector.tensor_tensor(gate, gate, ps[:, SIDE], ALU.mult))
                    nc.vector.tensor_tensor(m.merged[:, t, cols], m.merged[:, t, cols], gate,
                                            ALU.add).then_inc(merged, 1)

            for s in range(NA + 3):
                if s < NA:
                    n = width(s)
                    b = s % 2
                    dve.wait_ge(sig_ready, s + 1)
                    chained(nc.vector.tensor_tensor_scan(m.stick[:, b, 0:n][:, ::-1], m.sig_neg[:, b, 0:n][:, ::-1],
                                                         m.sig_neg[:, b, 0:n][:, ::-1], 1.0, ALU.mult, ALU.bypass))
                    nc.vector.tensor_tensor(m.sig_pos[:, b, 0:n], m.sig_pos[:, b, 0:n], m.stick[:, b, 1:n + 1],
                                            ALU.mult).then_inc(a_ready, 1)
                if s >= 3 and (s - 3) % HEADS == HEADS - 1:
                    qb = (s - 3) // HEADS
                    dve.wait_ge(av_done, s - 3 + 1)
                    nc.vector.tensor_copy(m.yb[:, qb], ps[:, YB]).then_inc(yb_ready, 1)
                if s % 4 == 0 and 4 <= s:
                    merge(s // 4 - 1)
                for i in SPLIT_AFTER_STEP.get(s, ()):
                    ring.split_lo(dve, i)
            for t in range(NT):
                dve.wait_ge(yb_hi, t + 1)
                nc.vector.tensor_tensor(m.ybT_lo[:, :, t * P:(t + 1) * P], turned_view(TURN[t % 2]),
                                        m.ybT_hi[:, :, t * P:(t + 1) * P].bitcast(F32),
                                        ALU.subtract).then_inc(yb_lo, 1)
            for g in range(8, 16):
                merge(g)
                for i in SPLIT_AFTER_GATE.get(g, ()):
                    ring.split_lo(dve, i)
                if g == 14:
                    ring.split_lo(dve, 23)
                    merged_turn.low_part(dve, 0)
            merged_turn.low_part(dve, 1)


def out_block(nc, m, ps, norm_semaphores, a, h0, h1, ring, merged_turn, routing, early):
    MAIN = (2, 7)
    FIRST = DENSE_PIECES - 4
    with ExitStack() as ctx:
        def sem(name):
            return ctx.enter_context(nc.semaphore(f"out_{name}"))

        summed, added = sem("summed"), sem("added")
        for half in range(2):
            ring.freed[FIRST + half], ring.freed[FIRST + 2 + half] = (summed, 2 * NT - 1), (summed, 2 * NT)
        norm = RowNorm(nc, m, ps, norm_semaphores, banks=(0,))
        block = ctx.enter_context(nc.Block())

        @block.sync
        def _(sp):
            norm.load_affine(sp, a["ln1_g"][0], a["ln1_b"][0])
            routing.load_router(sp)
            early.load_gate_up(sp, Expert(0, 0, 0))
            ring.load(sp, FIRST + 4)
            sp.wait_ge(merged_turn.lo_done, NT)
            early.load_gate_up(sp, Expert(0, 0, 1))
            ring.load(sp, FIRST + 5)
            for t in range(NT):
                norm.store(sp, t, h1)
            norm.stored(sp)

        @block.tensor
        def _(pe):
            for u in range(2 * NT):
                t, c = divmod(u, 2)
                if c == 0:
                    pe.wait_ge(merged_turn.lo_done, t + 1)
                if u >= 2:
                    pe.wait_ge(added, u - 1)
                for kk in range(KD):
                    i = FIRST + 2 * c + kk // 4
                    if t == 0 and kk % 4 == 0:
                        ring.ready(pe, i)
                    last = product3(nc, ps[:, MAIN[u % 2]], m.act_hi[:, kk, t * P:(t + 1) * P],
                                    m.act_lo[:, kk, t * P:(t + 1) * P], ring.hi(i)[:, kk % 4],
                                    ring.lo(i)[:, kk % 4], kk == 0, kk == KD - 1)
                last.then_inc(summed, 1)
                if c == 1:
                    if t + 2 < NT:
                        merged_turn.turn(pe, t + 2)
                    if t >= 1:
                        norm.turn(pe, t - 1)
            pe.wait_ge(norm_semaphores.lo_done, norm.before + 1)
            routing.gate_up(pe, 0)
            norm.turn(pe, NT - 1)

        @block.scalar
        def _(act):
            ring.split_hi(act, FIRST + 2)
            ring.split_hi(act, FIRST + 3)
            for t in range(NT):
                if t + 2 < NT:
                    merged_turn.high_part(act, t + 2)
                if t == NT - 1:
                    routing.split_router_high(act)
                    ring.split_hi(act, FIRST + 4)
                    ring.split_hi(act, FIRST + 5)
                if t >= 1:
                    norm.high_part(act, t - 1)
                norm.deviate(act, t)
                if t < NT - 1:
                    norm.centre(act, t)
            norm.high_part(act, NT - 1)

        @block.vector
        def _(dve):
            ring.split_lo(dve, FIRST + 2)
            ring.split_lo(dve, FIRST + 3)
            dve.wait_ge(merged_turn.rows_in, 16 * NT)
            for t in range(NT):
                for c in range(2):
                    u = 2 * t + c
                    if u == 2 * NT - 1:
                        routing.split_router_low(dve)
                        ring.split_lo(dve, FIRST + 4)
                    dve.wait_ge(summed, u + 1)
                    row = m.x[:, t, c * 512:(c + 1) * 512]
                    last = nc.vector.scalar_tensor_tensor(out=row, in0=row, scalar=ALPHA, in1=ps[:, MAIN[u % 2]],
                                                          op0=ALU.mult, op1=ALU.add).then_inc(added, 1)
                    dve.wait_ge(added, u + 1)
                    norm.half_statistics(dve, t, c)
                if t + 2 < NT:
                    merged_turn.low_part(dve, t + 2)
                if t == NT - 1:
                    norm.finish_on_vector(dve, t)
                else:
                    norm.finish(dve, t)
                if t >= 1:
                    norm.low_part(dve, t - 1)
                if t < NT - 1:
                    norm.gain(dve, t)
            norm.low_part(dve, NT - 1)

        @block.gpsimd
        def _(pool):
            for t in range(NT - 1):
                norm.shift(pool, t)
                if t == 1:
                    early.clear(pool, 0)
                    early.store_zeros(pool)
            pool.wait_ge(ring.lo_split, FIRST + 5)
            ring.split_lo(pool, FIRST + 5, nc.gpsimd)


class Routing:

    LOGIT, SCORE, MAIN, POS, ALL = 0, 3, (5, 2, 1, 0), 6, 7
    TURN, SUM = (4, 3), (5, 1)
    GU_PIECE = DENSE_PIECES

    def __init__(self, nc, m, ps, ctx, a, ring, acc_dram, acc_odd_dram):
        def sem(name):
            return ctx.enter_context(nc.semaphore(f"route_{name}"))

        self.nc, self.m, self.ps, self.a, self.ring = nc, m, ps, a, ring
        self.acc, self.acc_odd = acc_dram, acc_odd_dram
        self.router_in, self.down_in = sem("router_in"), sem("down_in")
        self.router_hi, self.router_split, self.logits, self.logits_out, self.logits_turned, self.scored = (
            sem("router_hi"), sem("router_split"), sem("logits"), sem("logits_out"), sem("logits_turned"), sem("scored"))
        self.picked, self.counted, self.peak_ready = sem("picked"), sem("counted"), sem("peak_ready")
        self.gu_sum, self.silu_out, self.h_ready = sem("gu_sum"), sem("silu_out"), sem("h_ready")
        self.turned, self.hT_ready, self.summed, self.acc_ready = (sem("turned"), sem("hT_ready"), sem("summed"),
                                                                   sem("acc_ready"))
        self.chain, self.index_base, self.rows_out = sem("chain"), sem("index_base"), sem("rows_out")
        self.links = 0

    def load_router(self, sp):
        m, a = self.m, self.a
        sp.dma_start(m.router[:], a["router_w"][0].rearrange("(p k) n -> p k n", p=P)).then_inc(self.router_in, 16)
        sp.dma_start(m.r_bias[:], a["router_bias"][0].partition_broadcast(P)).then_inc(self.router_in, 16)

    def load_down(self, sp):
        sp.dma_start(self.m.sh_down[:], self.a["sh_w_down"][0].rearrange("(p j) n -> p (j n)", p=P)) \
          .then_inc(self.down_in, 16)


    def set_tags(self, pool):
        nc, m = self.nc, self.m
        for t in range(NT):
            nc.gpsimd.memset(m.tags[:, t, :, 0:1], float(t * P))
            nc.gpsimd.iota(m.tags[:, t, :, 1:2], pattern=[[0, NE], [0, 1]], base=0, channel_multiplier=1,
                           allow_small_or_imprecise_dtypes=True)
            last = nc.gpsimd.memset(m.tags[:, t, :, 2:3], -FAR)
        last.then_inc(self.index_base, 1)



    def score(self, pe):
        nc, m, ps = self.nc, self.m, self.ps
        pe.wait_ge(self.router_split, 1)
        for k in range(KD):
            last = product3(nc, ps[0:NE, self.LOGIT], m.r_hi[:, k], m.r_lo[:, k], m.act_hi[:, k], m.act_lo[:, k],
                            k == 0, k == KD - 1)
        last.then_inc(self.logits, 1)

    def turn_scores(self, pe):
        nc, m, ps = self.nc, self.m, self.ps
        pe.wait_ge(self.logits_out, 1)
        for t in range(NT):
            last = nc.tensor.transpose(ps[:, self.SCORE, t * NE:(t + 1) * NE], m.logit[0:NE, t * P:(t + 1) * P],
                                       m.ident[0:NE, 0:NE])
        last.then_inc(self.logits_turned, 1)

    def gate_up(self, pe, t):
        nc, m, ps, ring = self.nc, self.m, self.ps, self.ring
        if self.MAIN[t] == self.LOGIT:
            pe.wait_ge(self.logits_out, 1)
        for kk in range(KD):
            i = self.GU_PIECE + kk // 4
            if t == 0 and kk % 4 == 0:
                ring.ready(pe, i)
            last = product3(nc, ps[:, self.MAIN[t]], m.act_hi[:, kk, t * P:(t + 1) * P],
                            m.act_lo[:, kk, t * P:(t + 1) * P], ring.hi(i)[:, kk % 4],
                            ring.lo(i)[:, kk % 4], kk == 0, kk == KD - 1)
        last.then_inc(self.gu_sum, 1)

    def count(self, pe):
        nc, m, ps = self.nc, self.m, self.ps
        pe.wait_ge(self.picked, 1)
        for t in range(NT):
            for o in range(t + 1):
                nc.tensor.matmul(ps[:, self.POS, t * NE:(t + 1) * NE], m.ones_bf[:] if o < t else m.earlier_bf[:],
                                 m.pick_bf[:, o], start=(o == 0), stop=(o == t))
        for o in range(NT):
            last = nc.tensor.matmul(ps[:, self.ALL, 0:NE], m.ones_bf[:], m.pick_bf[:, o],
                                    start=(o == 0), stop=(o == NT - 1))
        last.then_inc(self.counted, 1)

    def turn_h(self, pe, t):
        nc, m, ps = self.nc, self.m, self.ps
        pe.wait_ge(self.h_ready, NT)
        if t >= 2:
            pe.wait_ge(self.hT_ready, t - 1)
        for j in range(2):
            last = nc.tensor.transpose(ps[:, self.TURN[t % 2], j * P:(j + 1) * P], m.sh_h[:, t, j::2], m.ident[:])
        last.then_inc(self.turned, 1)

    def down(self, pe, t):
        nc, m, ps = self.nc, self.m, self.ps
        if t == 0:
            pe.wait_ge(self.down_in, 16)
        pe.wait_ge(self.hT_ready, t + 1)
        if t >= 2:
            pe.wait_ge(self.acc_ready, t - 1)
        for c in range(2):
            for j in range(2):
                last = nc.tensor.matmul(ps[:, self.SUM[t % 2] + c], m.sh_hT[:, j, t * P:(t + 1) * P],
                                        m.sh_down[:, j * D + c * 512:j * D + (c + 1) * 512],
                                        start=(j == 0), stop=(j == 1))
        last.then_inc(self.summed, 1)


    def store_rows(self, act, t):
        act.wait_ge(self.acc_ready, t + 1)
        if t == 2:
            act.wait_ge(self.rows_out, 16 * 2)
        act.dma_start(self.acc[t * P:(t + 1) * P, :], self.m.x[:, t]).then_inc(self.rows_out, 16)

    def split_router_high(self, act):
        act.wait_ge(self.router_in, 32)
        self.nc.scalar.activation(self.m.r_hi[:], self.m.router[:], ACT.Copy).then_inc(self.router_hi, 1)

    def sigmoid(self, act):
        act.wait_ge(self.logits_turned, 1)
        self.nc.scalar.activation(self.m.score[:],
                                  self.ps[:, self.SCORE, 0:NT * NE].rearrange("p (t e) -> p t e", e=NE),
                                  ACT.Sigmoid).then_inc(self.scored, 1)

    def silu(self, act, t):
        act.wait_ge(self.gu_sum, t + 1)
        self.nc.scalar.activation(self.m.sh_h[:, t], self.ps[:, self.MAIN[t], 0:FF],
                                  ACT.Silu).then_inc(self.silu_out, 1)

    def copy_hT(self, act, t):
        act.wait_ge(self.turned, t + 1)
        self.nc.scalar.activation(self.m.sh_hT[:, :, t * P:(t + 1) * P],
                                  self.ps[:, self.TURN[t % 2], 0:2 * P].rearrange("p (j n) -> p j n", n=P),
                                  ACT.Copy).then_inc(self.hT_ready, 1)


    def chained(self, dve, ins):
        self.links += 1
        ins.then_inc(self.chain, 1)
        dve.wait_ge(self.chain, self.links)

    def split_router_low(self, dve):
        m = self.m
        dve.wait_ge(self.router_hi, 1)
        self.nc.vector.tensor_tensor(m.r_lo[:], m.router[:], m.r_hi[:].bitcast(F32),
                                     ALU.subtract).then_inc(self.router_split, 1)

    def copy_logits(self, dve):
        nc, m = self.nc, self.m
        dve.wait_ge(self.logits, 1)
        nc.vector.tensor_copy(m.logit[0:NE, :], self.ps[0:NE, self.LOGIT]).then_inc(self.logits_out, 1)

    def pick(self, dve):
        nc, m = self.nc, self.m

        def chained(ins):
            self.chained(dve, ins)

        dve.wait_ge(self.scored, 1)
        chained(nc.vector.tensor_tensor(m.sel[:], m.score[:], m.r_bias[:].unsqueeze(1).to_broadcast([P, NT, NE]),
                                        ALU.add))
        for t in range(NT):
            for q in range(NGRP):
                last = nc.vector.max(out=m.top[:, t, q], in_=m.sel[:, t, q * 8:(q + 1) * 8])
        chained(last)
        chained(nc.vector.tensor_tensor(m.grp[:], m.top[:, :, :, 0], m.top[:, :, :, 1], ALU.add))
        for t in range(NT):
            mine = m.grp[:, t].unsqueeze(2).to_broadcast([P, NGRP, NGRP])
            other = m.grp[:, t].unsqueeze(1).to_broadcast([P, NGRP, NGRP])
            nc.vector.tensor_tensor(m.beats[:, t], other, mine, ALU.is_gt)
            last = nc.vector.tensor_tensor(m.ties[:, t], other, mine, ALU.is_equal)
        chained(last)
        for t in range(NT):
            last = nc.vector.tensor_tensor(m.ties[:, t], m.ties[:, t], m.lower_grp[:], ALU.mult)
        chained(last)
        chained(nc.vector.tensor_tensor(m.beats[:], m.beats[:], m.ties[:], ALU.add))
        chained(nc.vector.tensor_reduce(m.rank[:].rearrange("p t g -> p (t g)"),
                                        m.beats[:].rearrange("p t g o -> p (t g) o"), AX, ALU.add))
        chained(nc.vector.tensor_scalar(m.rank[:], m.rank[:], 3.5, -1e30, ALU.is_gt, ALU.mult))
        chained(nc.vector.tensor_tensor(m.sel[:].rearrange("p t (g e) -> p (t g) e", e=8),
                                        m.sel[:].rearrange("p t (g e) -> p (t g) e", e=8),
                                        m.rank[:].rearrange("p t g -> p (t g)").unsqueeze(2)
                                        .to_broadcast([P, NT * NGRP, 8]), ALU.add))
        for t in range(NT):
            last = nc.vector.max(out=m.top8[:, t], in_=m.sel[:, t])
        chained(last)
        for t in range(NT):
            last = nc.vector.match_replace(out=m.rest[:, t], in_to_replace=m.top8[:, t], in_values=m.sel[:, t],
                                           imm_value=-3e38)
        chained(last)
        chained(nc.vector.tensor_scalar(m.rest[:], m.rest[:], -2e38, None, ALU.is_lt))
        nc.vector.tensor_copy(m.pick_bf[:], m.rest[:]).then_inc(self.picked, 1)

    def weigh(self, dve):
        nc, m = self.nc, self.m

        def chained(ins):
            self.chained(dve, ins)

        chained(nc.vector.tensor_tensor(m.score[:], m.score[:], m.rest[:], ALU.mult))
        chained(nc.vector.tensor_reduce(m.den[:], m.score[:], AX, ALU.add))
        chained(nc.vector.reciprocal(m.den[:], m.den[:]))
        for t in range(NT):
            last = nc.vector.tensor_scalar(m.score[:, t], m.score[:, t], m.den[:, t:t + 1], ROUTED_SCALE,
                                           ALU.mult, ALU.mult)
        chained(last)
        dve.wait_ge(self.index_base, 1)
        for part in range(3):
            tag = m.tags[:, :, :, 3 + part]
            chained(nc.vector.tensor_copy(tag, m.score[:]))
            if part < 2:
                chained(nc.vector.tensor_tensor(m.score[:], m.score[:], tag, ALU.subtract))

    def place(self, dve):
        nc, m, ps = self.nc, self.m, self.ps
        self.chained(dve, nc.vector.tensor_scalar(m.rest[:], m.rest[:], -FAR, FAR, ALU.mult, ALU.add))
        dve.wait_ge(self.counted, 1)
        nc.vector.tensor_tensor(m.slot_of[:], m.rest[:],
                                ps[:, self.POS, 0:NT * NE].rearrange("p (t e) -> p t e", e=NE), ALU.add)
        self.chained(dve, nc.vector.tensor_reduce(m.peak[:], ps[:, self.ALL, 0:NE], AX, ALU.max))
        nc.vector.tensor_copy(m.peak_i[:], m.peak[:]).then_inc(self.peak_ready, 1)
        dve.wait_ge(self.peak_ready, 1)

    def times_up(self, dve, t):
        dve.wait_ge(self.silu_out, t + 1)
        self.nc.vector.tensor_tensor(self.m.sh_h[:, t], self.m.sh_h[:, t], self.ps[:, self.MAIN[t], FF:2 * FF],
                                     ALU.mult).then_inc(self.h_ready, 1)

    def add_rows(self, dve, t):
        m, b = self.m, self.SUM[t % 2]
        dve.wait_ge(self.summed, t + 1)
        rows = m.x[:, t].rearrange("p (c n) -> p c n", n=512)
        self.nc.vector.scalar_tensor_tensor(out=rows, in0=rows, scalar=ALPHA, in1=self.ps[:, b:b + 2],
                                            op0=ALU.mult, op1=ALU.add).then_inc(self.acc_ready, 1)


def experts_block(nc, m, ps, a, h1, acc_dram, acc_odd_dram, CAP, early, routing, embedding):
    GU, HT, XT, Y, TAGS = (0, 1), 2, 3, 5, 7
    LEAD = 2
    LEAD4 = 4
    ROUNDS = -(-SEQ // CAP)
    QUADS = NE // 4
    ZEROS = (0, NT)
    w_down = a["moe_w_down"][0]
    with ExitStack() as ctx:
        def sem(name):
            return ctx.enter_context(nc.semaphore(f"moe_{name}"))

        gu_in, put, cleared = early.gu_in, early.put, early.cleared
        dn_in = [sem(f"dn_in{b}") for b in range(2)]
        gu_hi, gu_lo, half_used = sem("gu_hi"), sem("gu_lo"), sem("half_used")
        dn_hi, dn_lo = sem("dn_hi"), sem("dn_lo")
        hot_ready, located, found, get_ready, put_ready = (sem("hot_ready"), sem("located"), sem("found"),
                                                           sem("get_ready"), sem("put_ready"))
        got = [sem(f"got{q}") for q in range(4)]
        x_turned, x_hi, x_lo = sem("x_turned"), sem("x_hi"), sem("x_lo")
        gu_sum, silu_out, h_ready = sem("gu_sum"), sem("silu_out"), sem("h_ready")
        h_turned, hT_hi, hT_lo, y_sum, y_ready = (sem("h_turned"), sem("hT_hi"), sem("hT_lo"), sem("y_sum"),
                                                  sem("y_ready"))
        passed = sem("passed")
        block = ctx.enter_context(nc.Block())

        peak = [None]
        embedding.begin()

        def rounds(eng, body):
            eng.wait_ge(routing.peak_ready, 1)
            peak[0] = eng.value_load(m.peak_i[0:1, 0:1], min_val=0, max_val=SEQ)
            body(0, True)
            with eng.If(peak[0] > CAP):
                with eng.Fori(1, ROUNDS) as r:
                    with eng.If(peak[0] > r * CAP):
                        body(r, False)

        def all_experts(eng, r, step):
            for q in range(4):
                step(Expert(r, 0, q), q)
            with eng.Fori(1, QUADS - 2) as quad:
                for q in range(4):
                    step(Expert(r, quad, q))
            for quad in (QUADS - 2, QUADS - 1):
                for q in range(4):
                    step(Expert(r, quad, q), 4 * (quad - QUADS) + q)

        def x_banks():
            return ps[:, XT:XT + 2, 0:4 * CAP]

        @block.sync
        def _(sp):
            def load_gate_up(x):
                for half in range(2):
                    sp.wait_ge(gu_lo, 2 * x.it + half - 4 + 1 + 2 * LEAD)
                    early.load_half(sp, x, half)

            def load_down(x):
                sp.wait_ge(dn_lo, x.it - 2 + 1 + LEAD)
                sp.dma_start(m.dn_raw[:, x.b:x.b + 1],
                             w_down[bass.ds(x.e, 1)].rearrange("o (p j) n -> p o (j n)", p=P)) \
                  .then_inc(dn_in[x.b], 16)

            def body(r, first):
                if not first:
                    for q in range(3):
                        load_gate_up(Expert(r, 0, q))

                def step(x, at=99):
                    load_down(x)
                    if at not in (0, -1, -2):
                        load_gate_up(x.next(2))

                all_experts(sp, r, step)
                with sp.If(peak[0] <= (r + 1) * CAP):
                    sp.wait_ge(gu_lo, 2 * ((r + 1) * NE) + 2 * LEAD)
                    embedding.load_p(sp)
                    sp.wait_ge(y_sum, (r + 1) * NE - 1 + LEAD)
                    embedding.load_weights(sp)

            routing.load_down(sp)
            load_gate_up(Expert(0, 0, 2))
            rounds(sp, body)
            embedding.sync(sp)

        @block.tensor
        def _(pe):
            pe.sem_inc(half_used, LEAD)
            pe.sem_inc(gu_sum, LEAD)
            pe.sem_inc(y_sum, LEAD)
            pe.sem_inc(x_turned, LEAD4)

            def locate(x):
                pe.wait_ge(hot_ready, x.it + 1)
                pe.wait_ge(found, x.it + LEAD)
                for t in range(NT):
                    last = nc.tensor.matmul(ps[0:CAP, TAGS, 0:6], m.onehot[:, x.b, t],
                                            m.tags[:, t, bass.ds(x.e, 1), :].rearrange("p o c -> p (o c)"),
                                            start=(t == 0), stop=(t == NT - 1))
                last.then_inc(located, 1)

            def turn_x(x):
                pe.wait_ge(got[x.q], 16 * x.turn4)
                pe.wait_ge(x_lo, x.it + LEAD)
                for k in range(KD):
                    last = nc.tensor.transpose(ps[:, XT + k // 4, (k % 4) * CAP:(k % 4 + 1) * CAP],
                                               m.xg[x.q][0:CAP, k::KD], m.ident[0:CAP, 0:CAP])
                last.then_inc(x_turned, 1)

            def gate_up(x, half):
                pe.wait_ge(gu_lo, 2 * x.it + half + 1 + 2 * LEAD)
                if half == 0:
                    pe.wait_ge(x_lo, x.it + 1 + LEAD)
                    pe.wait_ge(h_ready, x.it - 1 + LEAD)
                w_hi = m.w_hi[:, 2 * x.b + half].rearrange("p (w k n) -> p k w n", w=2, n=FF)
                w_lo = m.w_lo[:, 2 * x.b + half].rearrange("p (w k n) -> p k w n", w=2, n=FF)
                for k in range(4):
                    kk = 4 * half + k
                    cols = slice(kk * CAP, (kk + 1) * CAP)
                    last = product3(nc, ps[0:CAP, GU[x.b]].rearrange("p (w n) -> p w n", w=2),
                                    m.xgT_hi[:, x.b, cols], m.xgT_lo[:, x.b, cols], w_hi[:, k], w_lo[:, k],
                                    kk == 0, kk == KD - 1)
                last.then_inc(gu_sum if half else half_used, 1)

            def turn_h(x):
                pe.wait_ge(h_ready, x.it + 1 + LEAD)
                pe.wait_ge(hT_lo, x.it + LEAD)
                for j in range(2):
                    last = nc.tensor.transpose(ps[:, HT, j * CAP:(j + 1) * CAP], m.h[0:CAP, x.b, j::2],
                                               m.ident[0:CAP, 0:CAP])
                last.then_inc(h_turned, 1)

            def down(x):
                pe.wait_ge(hT_lo, x.it + 1 + LEAD)
                pe.wait_ge(dn_lo, x.it + 1 + LEAD)
                pe.wait_ge(y_ready, x.it + LEAD)
                for c in range(2):
                    for j in range(2):
                        rows, cols = slice(j * CAP, (j + 1) * CAP), slice(j * D + c * 512, j * D + (c + 1) * 512)
                        last = product3(nc, ps[0:CAP, Y + c], m.hT_hi[:, x.b, rows], m.hT_lo[:, x.b, rows],
                                        m.dn_hi[:, x.b, cols], m.dn_lo[:, x.b, cols], j == 0, j == 1)
                last.then_inc(y_sum, 1)

            def body(r, first):
                if not first:
                    for q in range(4):
                        locate(Expert(r, 0, q))
                    turn_x(Expert(r, 0, 0))

                def step(x, at=99):
                    if at == 1:
                        pe.wait_ge(routing.acc_ready, NT)
                    if at != 0:
                        turn_h(x.next(-1))
                    gate_up(x, 0)
                    if not -4 <= at <= -1:
                        locate(x.next(4))
                    gate_up(x, 1)
                    if at != -1:
                        turn_x(x.next(1))
                    if at != 0:
                        down(x.next(-1))

                all_experts(pe, r, step)
                turn_h(Expert(r, QUADS - 1, 3))
                down(Expert(r, QUADS - 1, 3))

            routing.score(pe)
            routing.turn_scores(pe)
            routing.gate_up(pe, 1)
            routing.gate_up(pe, 2)
            routing.count(pe)
            routing.gate_up(pe, 3)
            locate(Expert(0, 0, 0))
            locate(Expert(0, 0, 1))
            routing.turn_h(pe, 0)
            routing.turn_h(pe, 1)
            locate(Expert(0, 0, 2))
            locate(Expert(0, 0, 3))
            for t in (0, 1):
                routing.down(pe, t)
                routing.turn_h(pe, t + 2)
            pe.wait_ge(routing.hT_ready, NT)
            turn_x(Expert(0, 0, 0))
            routing.down(pe, 2)
            routing.down(pe, 3)
            rounds(pe, body)
            embedding.tensor(pe)

        @block.scalar
        def _(act):
            def split(x, half):
                act.wait_ge(gu_in[x.b][half], 32 * x.turn2)
                act.wait_ge(gu_sum if half else half_used, x.it - 2 + 1 + LEAD)
                nc.scalar.activation(m.w_hi[:, 2 * x.b + half], m.gu_raw[:, 2 * x.b + half],
                                     ACT.Copy).then_inc(gu_hi, 1)

            def split_down(x):
                act.wait_ge(dn_in[x.b], 16 * x.turn2)
                act.wait_ge(y_sum, x.it - 2 + 1 + LEAD)
                nc.scalar.activation(m.dn_hi[:, x.b], m.dn_raw[:, x.b], ACT.Copy).then_inc(dn_hi, 1)

            def split_x(x):
                act.wait_ge(x_turned, x.it + 1 + LEAD4)
                nc.scalar.activation(m.xgT_hi[:, x.b].rearrange("p (c n) -> p c n", c=2), x_banks(),
                                     ACT.Copy).then_inc(x_hi, 1)

            def silu(x):
                act.wait_ge(gu_sum, x.it + 1 + LEAD)
                nc.scalar.activation(m.silu[0:CAP, x.b], ps[0:CAP, GU[x.b], 0:FF], ACT.Silu).then_inc(silu_out, 1)

            def split_hT(x):
                act.wait_ge(h_turned, x.it + 1)
                nc.scalar.activation(m.hT_hi[:, x.b], ps[:, HT, 0:2 * CAP], ACT.Copy).then_inc(hT_hi, 1)

            def scale_y(x):
                act.wait_ge(y_sum, x.it + 1 + LEAD)
                act.wait_ge(put[x.b], 16 * (x.turn2 - 1 + ZEROS[x.b]))
                nc.scalar.activation(m.y[x.b][0:CAP].rearrange("p (c n) -> p c n", n=512), ps[0:CAP, Y:Y + 2],
                                     ACT.Copy,
                                     scale=m.found[0:CAP, bass.ds(x.e, 1), 1:2].rearrange("p o c -> p (o c)")) \
                  .then_inc(y_ready, 1)

            def body(r, first):
                if not first:
                    for q in range(2):
                        split(Expert(r, 0, q), 0)
                        split(Expert(r, 0, q), 1)
                    split_x(Expert(r, 0, 0))

                def step(x, at=99):
                    if at != 0:
                        split_hT(x.next(-1))
                    if at not in (0, -1):
                        split(x.next(1), 0)
                        split(x.next(1), 1)
                    if at == 0:
                        split_down(x)
                    silu(x)
                    if at != -1:
                        split_x(x.next(1))
                    if at != 0:
                        split_down(x)
                    if at != 0:
                        scale_y(x.next(-1))

                all_experts(act, r, step)
                split_hT(Expert(r, QUADS - 1, 3))
                scale_y(Expert(r, QUADS - 1, 3))

            act.sem_inc(y_ready, LEAD)
            routing.silu(act, 0)
            split(Expert(0, 0, 0), 0)
            routing.sigmoid(act)
            split(Expert(0, 0, 0), 1)
            for t in range(1, NT):
                routing.silu(act, t)
            split(Expert(0, 0, 1), 0)
            routing.copy_hT(act, 0)
            routing.copy_hT(act, 1)
            split(Expert(0, 0, 1), 1)
            routing.copy_hT(act, 2)
            routing.store_rows(act, 0)
            routing.copy_hT(act, 3)
            routing.store_rows(act, 1)
            split_x(Expert(0, 0, 0))
            routing.store_rows(act, 2)
            routing.store_rows(act, 3)
            rounds(act, body)
            embedding.scalar(act)

        @block.vector
        def _(dve):
            def one_hot(x):
                dve.wait_ge(located, x.it - 1 + LEAD)
                nc.vector.tensor_tensor(m.onehot[:, x.b],
                                        m.slots[:, bass.ds(x.r * CAP, CAP)].unsqueeze(1).to_broadcast([P, NT, CAP]),
                                        m.slot_of[:, :, bass.ds(x.e, 1)].to_broadcast([P, NT, CAP]),
                                        ALU.is_equal).then_inc(hot_ready, 1)

            def find(x):
                dve.wait_ge(located, x.it + 1 + LEAD)
                nc.vector.tensor_reduce(m.found[0:CAP, bass.ds(x.e, 1), :].rearrange("p o c -> p (o c)"),
                                        ps[0:CAP, TAGS, 0:6].rearrange("p (c x) -> p c x", x=3),
                                        AX, ALU.add).then_inc(found, 1)
                dve.wait_ge(found, x.it + 1 + LEAD)
                dve.wait_ge(x_turned, x.it - 4 + 1 + LEAD4)
                nc.vector.tensor_scalar(m.get_idx[x.q][0:CAP],
                                        m.found[0:CAP, bass.ds(x.e, 1), 0:1].rearrange("p o c -> p (o c)"),
                                        FAR, None, ALU.add).then_inc(get_ready, 1)

            def put_list(x):
                dve.wait_ge(put[x.b], 16 * (x.turn2 - 1 + ZEROS[x.b]))
                nc.vector.tensor_scalar(m.put_idx[x.b][0:CAP],
                                        m.found[0:CAP, bass.ds(x.e, 1), 0:1].rearrange("p o c -> p (o c)"),
                                        FAR, None, ALU.add).then_inc(put_ready, 1)

            def split(x, half):
                dve.wait_ge(gu_hi, 2 * x.it + half + 1)
                nc.vector.tensor_tensor(m.w_lo[:, 2 * x.b + half], m.gu_raw[:, 2 * x.b + half],
                                        m.w_hi[:, 2 * x.b + half].bitcast(F32), ALU.subtract).then_inc(gu_lo, 1)

            def split_down(x):
                dve.wait_ge(dn_hi, x.it + 1)
                nc.vector.tensor_tensor(m.dn_lo[:, x.b], m.dn_raw[:, x.b], m.dn_hi[:, x.b].bitcast(F32),
                                        ALU.subtract).then_inc(dn_lo, 1)

            def split_x(x):
                dve.wait_ge(x_hi, x.it + 1)
                nc.vector.tensor_tensor(m.xgT_lo[:, x.b].rearrange("p (c n) -> p c n", c=2), x_banks(),
                                        m.xgT_hi[:, x.b].bitcast(F32).rearrange("p (c n) -> p c n", c=2),
                                        ALU.subtract).then_inc(x_lo, 1)

            def times_up(x):
                dve.wait_ge(silu_out, x.it + 1)
                nc.vector.tensor_tensor(m.h[0:CAP, x.b], m.silu[0:CAP, x.b], ps[0:CAP, GU[x.b], FF:2 * FF],
                                        ALU.mult).then_inc(h_ready, 1)

            def split_hT(x):
                dve.wait_ge(hT_hi, x.it + 1)
                nc.vector.tensor_tensor(m.hT_lo[:, x.b], ps[:, HT, 0:2 * CAP], m.hT_hi[:, x.b].bitcast(F32),
                                        ALU.subtract).then_inc(hT_lo, 1)

            def body(r, first):
                if not first:
                    one_hot(Expert(r, 0, 0))
                    for q in range(4):
                        one_hot(Expert(r, 0, q + 1))
                        find(Expert(r, 0, q))
                    for q in range(2):
                        split(Expert(r, 0, q), 0)
                        split(Expert(r, 0, q), 1)
                    split_x(Expert(r, 0, 0))

                def step(x, at=99):
                    if at != 0:
                        split_hT(x.next(-1))
                    if at not in (0, -1):
                        split(x.next(1), 0)
                    if not -4 <= at <= -1:
                        find(x.next(4))
                    if at not in (0, -1):
                        split(x.next(1), 1)
                    times_up(x)
                    if at != -1:
                        split_x(x.next(1))
                    if at == 0:
                        dve.wait_ge(routing.rows_out, 16 * NT)
                    split_down(x)
                    if at != -1:
                        put_list(x)
                    if not -5 <= at <= -1:
                        one_hot(x.next(5))

                all_experts(dve, r, step)
                split_hT(Expert(r, QUADS - 1, 3))
                put_list(Expert(r, QUADS - 1, 3))

            dve.sem_inc(found, LEAD)
            dve.sem_inc(x_lo, LEAD)
            dve.sem_inc(h_ready, LEAD)
            dve.sem_inc(gu_lo, 2 * LEAD)
            dve.sem_inc(dn_lo, LEAD)
            dve.sem_inc(hT_lo, LEAD)
            dve.sem_inc(located, LEAD)
            routing.times_up(dve, 0)
            routing.copy_logits(dve)
            routing.pick(dve)
            routing.weigh(dve)
            routing.place(dve)
            one_hot(Expert(0, 0, 0))
            one_hot(Expert(0, 0, 1))
            routing.times_up(dve, 1)
            routing.times_up(dve, 2)
            find(Expert(0, 0, 0))
            routing.times_up(dve, 3)
            find(Expert(0, 0, 1))
            one_hot(Expert(0, 0, 2))
            one_hot(Expert(0, 0, 3))
            find(Expert(0, 0, 2))
            find(Expert(0, 0, 3))
            one_hot(Expert(0, 0, 4))
            dve.wait_ge(gu_lo, 2 + 2 * LEAD)
            split(Expert(0, 0, 1), 0)
            routing.add_rows(dve, 0)
            split(Expert(0, 0, 1), 1)
            routing.add_rows(dve, 1)
            split_x(Expert(0, 0, 0))
            routing.add_rows(dve, 2)
            routing.add_rows(dve, 3)
            rounds(dve, body)
            embedding.vector(dve)

        @block.gpsimd
        def _(pool):
            last_token = pool.to_reg(SEQ - 1)
            def gather(x, clear=4):
                pool.wait_ge(get_ready, x.it + 1)
                pool.wait_ge(x_turned, x.it - 4 + 1 + LEAD4)
                pool.sem_inc(passed, 1)
                pool.wait_ge(cleared, clear)
                nc.gpsimd.indirect_dma_start(out=m.xg[x.q][0:CAP], out_offset=None, in_=h1,
                                             in_offset=bass.IndirectOffsetOnAxis(ap=m.get_idx[x.q][0:CAP], axis=0),
                                             bounds_check=last_token, oob_is_err=False).then_inc(got[x.q], 16)

            def scatter(x):
                pool.wait_ge(y_ready, x.it + 1 + LEAD)
                pool.wait_ge(put_ready, x.it + 1)
                pool.wait_ge(put[x.b], 16 * (x.turn2 - 1 + ZEROS[x.b]))
                pool.sem_inc(passed, 1)
                pool.wait_ge(cleared, 4)
                nc.gpsimd.indirect_dma_start(out=(acc_dram, acc_odd_dram)[x.b],
                                             out_offset=bass.IndirectOffsetOnAxis(ap=m.put_idx[x.b][0:CAP], axis=0),
                                             in_=m.y[x.b][0:CAP], in_offset=None, bounds_check=last_token,
                                             oob_is_err=False, compute_op=ALU.add).then_inc(put[x.b], 16)

            def split(x, half):
                pool.wait_ge(gu_hi, 2 * x.it + half + 1)
                nc.gpsimd.tensor_tensor(m.w_lo[:, 2 * x.b + half], m.gu_raw[:, 2 * x.b + half],
                                        m.w_hi[:, 2 * x.b + half].bitcast(F32), ALU.subtract).then_inc(gu_lo, 1)

            def body(r, first):
                if not first:
                    for q in range(4):
                        gather(Expert(r, 0, q))

                def step(x, at=99):
                    if not -4 <= at <= -1:
                        gather(x.next(4))
                    if at != 0:
                        scatter(x.next(-1))

                all_experts(pool, r, step)
                scatter(Expert(r, QUADS - 1, 3))
                for b in range(2):
                    pool.wait_ge(put[b], 16 * ((r + 1) * (NE // 2) + ZEROS[b]))

            early.clear(pool, 1)
            routing.set_tags(pool)
            pool.wait_ge(gu_lo, 2 * LEAD)
            split(Expert(0, 0, 0), 0)
            split(Expert(0, 0, 0), 1)
            pool.wait_ge(put[1], 16 * NT)
            gather(Expert(0, 0, 0), clear=2)
            gather(Expert(0, 0, 1), clear=2)
            pool.wait_ge(routing.rows_out, 16 * 2)
            early.clear(pool, 2)
            early.clear(pool, 3)
            gather(Expert(0, 0, 2))
            gather(Expert(0, 0, 3))
            rounds(pool, body)
            embedding.gpsimd(pool)


class Embedding:

    MAIN, TURN, PT = (0, 1), (3, 5), (2, 7)

    def __init__(self, nc, m, ps, ctx, norm_semaphores, a, acc_dram, acc_odd_dram, out):
        def sem(name):
            return ctx.enter_context(nc.semaphore(f"ple_{name}"))

        self.nc, self.m, self.ps, self.a, self.norm_semaphores = nc, m, ps, a, norm_semaphores
        self.acc, self.out = (acc_dram, acc_odd_dram), out
        w = a["ple_w_gate"][0].rearrange("(p k) n -> p k n", p=P)
        self.ring = WeightRing(nc, m, ctx, "ple", [w[:, 4 * half:4 * half + 4, c * 512:(c + 1) * 512]
                                                   for c in range(2) for half in range(2)], m.ple_raw)
        self.p_in, self.pw_in, self.scattered = sem("p_in"), sem("pw_in"), sem("scattered")
        self.rows_in = [sem(f"rows_in{t}") for t in range(NT)]
        self.p_turned, self.pT_ready, self.p_sum, self.p_out = sem("p_turned"), sem("pT_ready"), sem("p_sum"), sem("p_out")
        self.row_sum, self.turned, self.hi_done, self.lo_done = (sem("row_sum"), sem("turned"), sem("hi_done"),
                                                                 sem("lo_done"))
        self.summed, self.gate_ready, self.gate_used, self.added = (sem("summed"), sem("gate_ready"),
                                                                    sem("gate_used"), sem("added"))

    def begin(self):
        self.norm = RowNorm(self.nc, self.m, self.ps, self.norm_semaphores)

    def turned_view(self, t):
        b = self.TURN[t % 2]
        return self.ps[:, b:b + 2].rearrange("p b (k n) -> p (b k) n", n=P)

    def load_p(self, sp):
        m, a = self.m, self.a
        sp.dma_start(m.p[:], a["p"][0, 0].rearrange("(t p) d -> p t d", p=P)).then_inc(self.p_in, 16)
        sp.dma_start(m.p_w[:], a["ple_w_proj"][0].rearrange("(p j) n -> p (j n)", p=P)).then_inc(self.pw_in, 16)

    def load_weights(self, sp):
        self.ring.load(sp, 0)
        self.ring.load(sp, 1)

    def sync(self, sp):
        m = self.m
        sp.wait_ge(self.scattered, 1)
        for t in range(NT):
            sp.dma_start(m.x[:, t], self.acc[0][t * P:(t + 1) * P, :]).then_inc(self.rows_in[t], 16)
            sp.dma_start(m.x_odd[t // 2][:, t % 2], self.acc[1][t * P:(t + 1) * P, :]).then_inc(self.rows_in[t], 16)
            if t == 1:
                self.ring.load(sp, 2)
                self.ring.load(sp, 3)
        self.norm.load_affine(sp, self.a["ln2_g"][0], self.a["ln2_b"][0])
        for t in range(NT):
            self.norm.store(sp, t, self.out)
        self.norm.stored(sp)

    def gpsimd(self, pool):
        nc, m = self.nc, self.m
        pool.sem_inc(self.scattered, 1)
        self.ring.split_lo(pool, 0, nc.gpsimd)
        for t in range(NT):
            pool.wait_ge(self.rows_in[t], 32)
            nc.gpsimd.tensor_tensor(m.x[:, t], m.x[:, t], m.x_odd[t // 2][:, t % 2], ALU.add).then_inc(self.row_sum, 1)
        for t in range(NT - 1):
            self.norm.shift(pool, t)

    def tensor(self, pe):
        nc, m, ps, ring, MAIN = self.nc, self.m, self.ps, self.ring, self.MAIN

        def turn(t):
            pe.wait_ge(self.row_sum, t + 1)
            if t >= 2:
                pe.wait_ge(self.lo_done, t - 1)
            b = self.TURN[t % 2]
            for k in range(KD):
                last = nc.tensor.transpose(ps[:, b + k // 4, (k % 4) * P:(k % 4 + 1) * P], m.x[:, t, k::KD], m.ident[:])
            last.then_inc(self.turned, 1)

        pe.wait_ge(self.p_in, 16)
        for t in range(NT):
            if t >= 2:
                pe.wait_ge(self.pT_ready, t - 1)
            for j in range(2):
                last = nc.tensor.transpose(ps[:, self.PT[t % 2], j * P:(j + 1) * P], m.p[:, t, j::2], m.ident[:])
            last.then_inc(self.p_turned, 1)
        pe.wait_ge(self.pw_in, 16)
        for u in range(2 * NT):
            t, c = divmod(u, 2)
            if c == 0:
                pe.wait_ge(self.pT_ready, t + 1)
            if u >= 2:
                pe.wait_ge(self.p_out, u - 1)
            for j in range(2):
                last = nc.tensor.matmul(ps[:, MAIN[c]], m.pT[:, j, t * P:(t + 1) * P],
                                        m.p_w[:, j * D + c * 512:j * D + (c + 1) * 512],
                                        start=(j == 0), stop=(j == 1))
            last.then_inc(self.p_sum, 1)
            if u == 5:
                turn(0)
        turn(1)
        for u in range(2 * NT):
            t, c = divmod(u, 2)
            if u < 2:
                pe.wait_ge(self.p_out, 2 * NT - 1 + u)
            else:
                pe.wait_ge(self.gate_ready, u - 1)
            if c == 0:
                pe.wait_ge(self.lo_done, t + 1)
            for kk in range(KD):
                i = 2 * c + kk // 4
                if t == 0 and kk % 4 == 0:
                    ring.ready(pe, i)
                last = product3(nc, ps[:, MAIN[c]], m.act_hi[:, kk, t * P:(t + 1) * P],
                                m.act_lo[:, kk, t * P:(t + 1) * P], ring.hi(i)[:, kk % 4],
                                ring.lo(i)[:, kk % 4], kk == 0, kk == KD - 1)
            last.then_inc(self.summed, 1)
            if c == 1 and t + 2 < NT:
                turn(t + 2)

    def scalar(self, act):
        nc, m, ps, ring = self.nc, self.m, self.ps, self.ring

        def high_part(t):
            act.wait_ge(self.turned, t + 1)
            nc.scalar.activation(m.act_hi[:, :, t * P:(t + 1) * P], self.turned_view(t),
                                 ACT.Copy).then_inc(self.hi_done, 1)

        for t in range(NT):
            act.wait_ge(self.p_turned, t + 1)
            nc.scalar.activation(m.pT[:, :, t * P:(t + 1) * P],
                                 ps[:, self.PT[t % 2], 0:2 * P].rearrange("p (j n) -> p j n", n=P),
                                 ACT.Copy).then_inc(self.pT_ready, 1)
        ring.split_hi(act, 0)
        ring.split_hi(act, 1)
        high_part(0)
        high_part(1)
        ring.split_hi(act, 2)
        ring.split_hi(act, 3)
        for t in range(NT):
            for u in (2 * t, 2 * t + 1):
                act.wait_ge(self.summed, u + 1)
                if u >= 2:
                    act.wait_ge(self.added, u - 1)
                nc.scalar.activation(m.gate_out[:, u % 2], ps[:, self.MAIN[u % 2]],
                                     ACT.Sigmoid).then_inc(self.gate_ready, 1)
            if t + 2 < NT:
                high_part(t + 2)
            self.norm.deviate(act, t)
            if t < NT - 1:
                self.norm.centre(act, t)

    def vector(self, dve):
        nc, m, ps, ring = self.nc, self.m, self.ps, self.ring

        def low_part(t):
            dve.wait_ge(self.hi_done, t + 1)
            nc.vector.tensor_tensor(m.act_lo[:, :, t * P:(t + 1) * P], self.turned_view(t),
                                    m.act_hi[:, :, t * P:(t + 1) * P].bitcast(F32),
                                    ALU.subtract).then_inc(self.lo_done, 1)

        for t in range(NT):
            for c in range(2):
                dve.wait_ge(self.p_sum, 2 * t + c + 1)
                nc.vector.tensor_copy(m.pp[:, t, c * 512:(c + 1) * 512], ps[:, self.MAIN[c]]).then_inc(self.p_out, 1)
            if t == 2:
                dve.wait_ge(ring.lo_split, 1)
                ring.split_lo(dve, 1)
                low_part(0)
        ring.split_lo(dve, 2)
        low_part(1)
        ring.split_lo(dve, 3)
        for t in range(NT):
            for c in range(2):
                u = 2 * t + c
                cols = slice(c * 512, (c + 1) * 512)
                dve.wait_ge(self.gate_ready, u + 1)
                nc.vector.tensor_tensor(m.gate_out[:, c], m.gate_out[:, c], m.pp[:, t, cols],
                                        ALU.mult).then_inc(self.gate_used, 1)
                dve.wait_ge(self.gate_used, u + 1)
                nc.vector.tensor_tensor(m.x[:, t, cols], m.x[:, t, cols], m.gate_out[:, c],
                                        ALU.add).then_inc(self.added, 1)
                dve.wait_ge(self.added, u + 1)
                self.norm.half_statistics(dve, t, c)
            if t + 2 < NT:
                low_part(t + 2)
            if t == NT - 1:
                self.norm.finish_on_vector(dve, t)
            else:
                self.norm.finish(dve, t)
                self.norm.gain(dve, t)


def encoder_block(nc, a, out, CAP=SLOTS):
    h0 = nc.dram_tensor("h0_rows", [SEQ, D], F32, kind="Internal").ap()
    h1 = nc.dram_tensor("h1_rows", [SEQ, D], F32, kind="Internal").ap()
    acc_dram = nc.dram_tensor("residual_rows", [SEQ, D], F32, kind="Internal").ap()
    acc_odd_dram = nc.dram_tensor("odd_rows", [SEQ, D], F32, kind="Internal").ap()
    m = Memory(nc, (nc.sbuf_base + 31) // 32 * 32, CAP)
    with ExitStack() as ctx:
        ps = ctx.enter_context(nc.psum_tensor("ps", [P, 8, 512], F32))
        norm = NormSemaphores(nc, ctx)
        ring = WeightRing(nc, m, ctx, "dense", dense_pieces(a), [m.raw[:, i] for i in range(NRAW)])
        merged_turn = MergedTurn(nc, m, ps, ctx)
        early = FirstExperts(nc, m, ctx, a, acc_odd_dram)
        routing = Routing(nc, m, ps, ctx, a, ring, acc_dram, acc_odd_dram)
        embedding = Embedding(nc, m, ps, ctx, norm, a, acc_dram, acc_odd_dram, out[0])
        mix_block(nc, m, ps, norm, a, h0, ring, merged_turn)
        out_block(nc, m, ps, norm, a, h0, h1, ring, merged_turn, routing, early)
        experts_block(nc, m, ps, a, h1, acc_dram, acc_odd_dram, CAP, early, routing, embedding)


_INS = ["x", "p", "ln_in_g", "ln_in_b", "w_in", "sg_ln_g", "sg_ln_b", "sg_w_s", "sg_b_s", "w_branch_a", "w_branch_b",
        "w_out", "ln1_g", "ln1_b", "router_w", "router_bias", "moe_w_gate", "moe_w_up", "moe_w_down", "sh_w_gate",
        "sh_w_up", "sh_w_down", "ple_w_proj", "ple_w_gate", "ln2_g", "ln2_b"]


def kernel(**inputs):
    import numpy as _np
    import concourse.bacc as _bacc
    from concourse import mybir as _mybir
    from concourse.bass_utils import run_bass_kernel_spmd as _run

    nc = _bacc.Bacc("TRN2", target_bir_lowering=False, num_devices=1)
    arrays, args = {}, {}
    for name in _INS:
        v = _np.ascontiguousarray(inputs[name])
        arrays[f"in_{name}"] = v
        args[name] = nc.dram_tensor(f"in_{name}", v.shape, _mybir.dt.from_np(v.dtype), kind="ExternalInput").ap()
    out = nc.dram_tensor("out_h", [1, SEQ, D], F32, kind="ExternalOutput").ap()
    encoder_block(nc, args, out)
    r = _run(nc, [arrays], core_ids=[0])
    return r.results[0]["out_h"]
```
